# Optimizing a Trainium2 kernel written in Bass

```python
import math
import jax, jax.numpy as jnp
from jax import lax
import numpy as np

D_MODEL = 1024
BATCH = 1
SEQ = 256
DEPTH = 2

NORM_EPS = 1e-6
D_FF = 256 * ((8 * D_MODEL // 3 + 255) // 256)
CHUNK = 64
MIX_W = D_MODEL
M_DH = 64
M_W = MIX_W // 4
M_HEADS = M_W // M_DH
R_DH = 64
R_W = MIX_W // 4
R_HEADS = R_W // R_DH
ROPE_BASE = 10000.0
G_DH = 128
G_W = MIX_W - M_W - R_W
G_HEADS = G_W // G_DH
CONV_K = 4
IN_SIZES = (M_W, M_W, M_W, M_W, M_HEADS, M_HEADS,
            R_W, R_W, R_W, R_W,
            G_W, G_W, G_W, G_W, G_HEADS, G_HEADS)
IN_W = sum(IN_SIZES)


def _rmsnorm(x, gain):
    x32 = x.astype(jnp.float32)
    y = x32 * lax.rsqrt(jnp.mean(x32 * x32, axis=-1, keepdims=True) + NORM_EPS)
    return (y * gain).astype(x.dtype)

def _swiglu(x, w_gate, w_up, w_down):
    hid = jax.nn.silu(jnp.einsum('bsd,df->bsf', x, w_gate)) * jnp.einsum('bsd,df->bsf', x, w_up)
    return jnp.einsum('bsf,fd->bsd', hid, w_down)

def _heads(t, n_heads):
    b, s, w = t.shape
    return t.reshape(b, s, n_heads, w // n_heads).transpose(0, 2, 1, 3)

def _head_rmsnorm(h, gain):
    h = h * lax.rsqrt(jnp.mean(h * h, axis=-1, keepdims=True) + NORM_EPS)
    b, nh, s, d = h.shape
    return h.transpose(0, 2, 1, 3).reshape(b, s, nh * d) * gain

def _l2norm(t):
    return t * lax.rsqrt(jnp.sum(t * t, axis=-1, keepdims=True) + NORM_EPS)

def _rope(t):
    d = t.shape[-1]
    inv_freq = ROPE_BASE ** (-jnp.arange(0, d, 2, dtype=jnp.float32) / d)
    ang = jnp.arange(t.shape[2], dtype=jnp.float32)[:, None] * inv_freq[None, :]
    cos, sin = jnp.cos(ang), jnp.sin(ang)
    t1, t2 = t[..., : d // 2], t[..., d // 2:]
    return jnp.concatenate([t1 * cos - t2 * sin, t1 * sin + t2 * cos], axis=-1)

def _causal_dwconv(x, w):
    k, c = w.shape
    return lax.conv_general_dilated(x, w[:, None, :].astype(x.dtype), window_strides=(1,),
                                    padding=[(k - 1, 0)], dimension_numbers=('NWC', 'WIO', 'NWC'),
                                    feature_group_count=c)

def _to_chunks(t):
    b, h, s = t.shape[:3]
    return jnp.moveaxis(t.reshape(b, h, s // CHUNK, CHUNK, *t.shape[3:]), 2, 0)

def _from_chunks(t):
    n, b, h, l, d = t.shape
    return jnp.moveaxis(t, 0, 2).reshape(b, h, n * l, d)

def _mlstm(q, k, v, i_pre, f_pre):
    b, nh, s, d = q.shape
    k = k * d ** -0.5
    log_f = jax.nn.log_sigmoid(f_pre)
    causal = jnp.tril(jnp.ones((CHUNK, CHUNK), dtype=bool))

    def step(carry, xs):
        c_st, n_st, m_st = carry
        qc, kc, vc, ic, fc = xs
        bcum = jnp.cumsum(fc, axis=-1)
        log_w = jnp.where(causal, bcum[..., :, None] - bcum[..., None, :] + ic[..., None, :], -jnp.inf)
        log_inter = bcum + m_st[..., None]
        m_row = jnp.maximum(log_inter, jnp.max(log_w, axis=-1))
        w = jnp.exp(log_w - m_row[..., None])
        inter = jnp.exp(log_inter - m_row)
        sc = jnp.einsum('bhid,bhjd->bhij', qc, kc) * w
        num = jnp.einsum('bhij,bhje->bhie', sc, vc) + inter[..., None] * jnp.einsum('bhid,bhde->bhie', qc, c_st)
        den = jnp.sum(sc, axis=-1) + inter * jnp.einsum('bhid,bhd->bhi', qc, n_st)
        hc = num / jnp.maximum(jnp.abs(den), jnp.exp(-m_row))[..., None]
        b_last = bcum[..., -1]
        log_src = b_last[..., None] - bcum + ic
        m_new = jnp.maximum(b_last + m_st, jnp.max(log_src, axis=-1))
        carry_decay = jnp.exp(b_last + m_st - m_new)
        kw = kc * jnp.exp(log_src - m_new[..., None])[..., None]
        c_st = carry_decay[..., None, None] * c_st + jnp.einsum('bhjd,bhje->bhde', kw, vc)
        n_st = carry_decay[..., None] * n_st + jnp.sum(kw, axis=2)
        return (c_st, n_st, m_new), hc

    init = (jnp.zeros((b, nh, d, v.shape[-1]), q.dtype), jnp.zeros((b, nh, d), q.dtype),
            jnp.zeros((b, nh), q.dtype))
    _, hs = lax.scan(step, init, (_to_chunks(q), _to_chunks(k), _to_chunks(v),
                                  _to_chunks(i_pre), _to_chunks(log_f)))
    return _from_chunks(hs)

def _retention(q, k, v):
    b, nh, s, d = q.shape
    k = k * d ** -0.5
    log_gamma = jnp.log1p(-jnp.exp2(-5.0 - jnp.arange(nh, dtype=jnp.float32)))
    pos = jnp.arange(CHUNK, dtype=jnp.float32)
    rel = pos[:, None] - pos[None, :]
    causal = rel >= 0
    intra = jnp.where(causal, jnp.exp(jnp.where(causal, rel, 0.0) * log_gamma[:, None, None]), 0.0)
    q_decay = jnp.exp((pos + 1.0) * log_gamma[:, None])[..., None]
    k_decay = jnp.exp((CHUNK - 1.0 - pos) * log_gamma[:, None])[..., None]
    chunk_decay = jnp.exp(CHUNK * log_gamma)[:, None, None]

    def step(r_st, xs):
        qc, kc, vc = xs
        sc = jnp.einsum('bhid,bhjd->bhij', qc, kc) * intra
        o = jnp.einsum('bhij,bhje->bhie', sc, vc) + jnp.einsum('bhid,bhde->bhie', qc * q_decay, r_st)
        r_st = chunk_decay * r_st + jnp.einsum('bhjd,bhje->bhde', kc * k_decay, vc)
        return r_st, o

    init = jnp.zeros((b, nh, d, v.shape[-1]), q.dtype)
    _, outs = lax.scan(step, init, (_to_chunks(q), _to_chunks(k), _to_chunks(v)))
    return _from_chunks(outs)

def _gated_delta(q, k, v, log_alpha, beta):
    b, nh, s, dk = q.shape
    dv = v.shape[-1]
    q = q * dk ** -0.5
    idx = jnp.arange(CHUNK)
    causal = idx[:, None] >= idx[None, :]
    strict = idx[:, None] > idx[None, :]
    eye = jnp.eye(CHUNK, dtype=q.dtype)

    def step(s_st, xs):
        qc, kc, vc, ac, bc = xs
        g = jnp.cumsum(ac, axis=-1)
        diff = g[..., :, None] - g[..., None, :]
        decay = jnp.where(causal, jnp.exp(jnp.where(causal, diff, 0.0)), 0.0)
        kb = kc * bc[..., None]
        a_mat = eye + jnp.where(strict, jnp.einsum('bhid,bhjd->bhij', kb, kc) * decay, 0.0)
        rhs = jnp.concatenate([vc * bc[..., None], kb * jnp.exp(g)[..., None]], axis=-1)
        sol = lax.linalg.triangular_solve(a_mat, rhs, left_side=True, lower=True, unit_diagonal=True)
        u = sol[..., :dv] - jnp.einsum('bhik,bhkv->bhiv', sol[..., dv:], s_st)
        qk = jnp.einsum('bhik,bhjk->bhij', qc, kc) * decay
        o = jnp.einsum('bhik,bhkv->bhiv', qc * jnp.exp(g)[..., None], s_st) + jnp.einsum('bhij,bhjv->bhiv', qk, u)
        g_last = g[..., -1:]
        s_st = jnp.exp(g_last)[..., None] * s_st + jnp.einsum('bhjk,bhjv->bhkv', kc * jnp.exp(g_last - g)[..., None], u)
        return s_st, o

    init = jnp.zeros((b, nh, dk, dv), q.dtype)
    _, outs = lax.scan(step, init, (_to_chunks(q), _to_chunks(k), _to_chunks(v),
                                    _to_chunks(log_alpha), _to_chunks(beta)))
    return _from_chunks(outs)

def _hybrid_mixer(u, w_in, m_i_bias, m_f_bias, g_conv, g_a_log, g_dt_bias,
                  m_out_norm, r_out_norm, g_out_norm, w_out):
    f32 = jnp.float32
    offsets = [int(o) for o in np.cumsum(IN_SIZES)[:-1]]
    proj = jnp.einsum('bsd,dp->bsp', u, w_in).astype(f32)
    (mq, mk, mv, mo, mi, mf, rq, rk, rv, rg, gq, gk, gv, gz, ga, gb) = jnp.split(proj, offsets, axis=-1)
    i_pre = jnp.transpose(mi + m_i_bias, (0, 2, 1))
    f_pre = jnp.transpose(mf + m_f_bias, (0, 2, 1))
    h_m = _mlstm(_heads(mq, M_HEADS), _heads(mk, M_HEADS), _heads(mv, M_HEADS), i_pre, f_pre)
    y_m = _head_rmsnorm(h_m, m_out_norm) * jax.nn.sigmoid(mo)
    h_r = _retention(_rope(_heads(rq, R_HEADS)), _rope(_heads(rk, R_HEADS)), _heads(rv, R_HEADS))
    y_r = _head_rmsnorm(h_r, r_out_norm) * jax.nn.silu(rg)
    qkv = jax.nn.silu(_causal_dwconv(jnp.concatenate([gq, gk, gv], axis=-1), g_conv))
    cq, ck, cv = jnp.split(qkv, 3, axis=-1)
    log_alpha = -jnp.exp(g_a_log) * jax.nn.softplus(ga + g_dt_bias)
    beta = jax.nn.sigmoid(gb)
    h_g = _gated_delta(_l2norm(_heads(cq, G_HEADS)), _l2norm(_heads(ck, G_HEADS)), _heads(cv, G_HEADS),
                       jnp.transpose(log_alpha, (0, 2, 1)), jnp.transpose(beta, (0, 2, 1)))
    y_g = _head_rmsnorm(h_g, g_out_norm) * jax.nn.silu(gz)
    y = jnp.concatenate([y_m, y_r, y_g], axis=-1).astype(u.dtype)
    return jnp.einsum('bsm,md->bsd', y, w_out)

def first_inputs(seed: int = 0) -> dict:
    key = jax.random.key(seed)
    ks = jax.random.split(key, 24)
    f32 = jnp.float32

    def nrm(k, shape, fan_in):
        return jax.random.normal(k, shape, f32) * fan_in ** -0.5

    def gain(k, shape):
        return 1.0 + 0.02 * jax.random.normal(k, shape, f32)

    x = jax.random.normal(ks[0], (BATCH, SEQ, D_MODEL), f32)
    ffn1_norm = gain(ks[1], (DEPTH, D_MODEL))
    ffn1_w_gate = nrm(ks[2], (DEPTH, D_MODEL, D_FF), D_MODEL)
    ffn1_w_up = nrm(ks[3], (DEPTH, D_MODEL, D_FF), D_MODEL)
    ffn1_w_down = nrm(ks[4], (DEPTH, D_FF, D_MODEL), D_FF)
    mix_norm = gain(ks[5], (DEPTH, D_MODEL))
    w_in = nrm(ks[6], (DEPTH, D_MODEL, IN_W), D_MODEL)
    m_i_bias = 0.1 * jax.random.normal(ks[7], (DEPTH, M_HEADS), f32)
    m_f_bias = jnp.linspace(3.0, 6.0, M_HEADS, dtype=f32)[None, :] + 0.1 * jax.random.normal(ks[8], (DEPTH, M_HEADS), f32)
    g_conv = nrm(ks[9], (DEPTH, CONV_K, 3 * G_W), CONV_K)
    g_a_log = jnp.log(jax.random.uniform(ks[10], (DEPTH, G_HEADS), f32, 1.0, 16.0))
    dt = jnp.exp(jax.random.uniform(ks[11], (DEPTH, G_HEADS), f32, math.log(1e-3), math.log(1e-1)))
    g_dt_bias = dt + jnp.log(-jnp.expm1(-dt))
    m_out_norm = gain(ks[12], (DEPTH, M_W))
    r_out_norm = gain(ks[13], (DEPTH, R_W))
    g_out_norm = gain(ks[14], (DEPTH, G_W))
    w_out = nrm(ks[15], (DEPTH, MIX_W, D_MODEL), MIX_W)
    ffn2_norm = gain(ks[16], (DEPTH, D_MODEL))
    ffn2_w_gate = nrm(ks[17], (DEPTH, D_MODEL, D_FF), D_MODEL)
    ffn2_w_up = nrm(ks[18], (DEPTH, D_MODEL, D_FF), D_MODEL)
    ffn2_w_down = nrm(ks[19], (DEPTH, D_FF, D_MODEL), D_FF)
    final_norm = gain(ks[20], (D_MODEL,))
    return {'x': x, 'ffn1_norm': ffn1_norm, 'ffn1_w_gate': ffn1_w_gate, 'ffn1_w_up': ffn1_w_up,
            'ffn1_w_down': ffn1_w_down, 'mix_norm': mix_norm, 'w_in': w_in, 'm_i_bias': m_i_bias,
            'm_f_bias': m_f_bias, 'g_conv': g_conv, 'g_a_log': g_a_log, 'g_dt_bias': g_dt_bias,
            'm_out_norm': m_out_norm, 'r_out_norm': r_out_norm, 'g_out_norm': g_out_norm, 'w_out': w_out,
            'ffn2_norm': ffn2_norm, 'ffn2_w_gate': ffn2_w_gate, 'ffn2_w_up': ffn2_w_up,
            'ffn2_w_down': ffn2_w_down, 'final_norm': final_norm}

def first_block(x, ffn1_norm, ffn1_w_gate, ffn1_w_up, ffn1_w_down, mix_norm, w_in, m_i_bias, m_f_bias,
              g_conv, g_a_log, g_dt_bias, m_out_norm, r_out_norm, g_out_norm, w_out,
              ffn2_norm, ffn2_w_gate, ffn2_w_up, ffn2_w_down, final_norm):
    h = x
    for l in range(DEPTH):
        h = h + 0.5 * _swiglu(_rmsnorm(h, ffn1_norm[l]), ffn1_w_gate[l], ffn1_w_up[l], ffn1_w_down[l])
        h = h + _hybrid_mixer(_rmsnorm(h, mix_norm[l]), w_in[l], m_i_bias[l], m_f_bias[l], g_conv[l],
                              g_a_log[l], g_dt_bias[l], m_out_norm[l], r_out_norm[l], g_out_norm[l], w_out[l])
        h = h + 0.5 * _swiglu(_rmsnorm(h, ffn2_norm[l]), ffn2_w_gate[l], ffn2_w_up[l], ffn2_w_down[l])
    return _rmsnorm(h, final_norm)


D_MIX = D_MODEL
GLA_HEADS = 4
GLA_WIDTH = D_MIX // 2
GLA_DV = GLA_WIDTH // GLA_HEADS
GLA_DK = GLA_DV // 2
GLA_GATE_RANK = 16
GLA_GATE_NORMALIZER = 16.0
SGU_WIDTH = D_MIX - GLA_WIDTH
SGU_GROUPS = 4
SGU_GROUP_DIM = SGU_WIDTH // SGU_GROUPS
SGU_WINDOW = 128
COL_Q = GLA_HEADS * GLA_DK
COL_K = GLA_HEADS * GLA_DK
COL_V = GLA_WIDTH
COL_R = GLA_WIDTH
COL_A = GLA_GATE_RANK
COL_SU = SGU_WIDTH
COL_SV = SGU_WIDTH
IN_COLS = COL_Q + COL_K + COL_V + COL_R + COL_A + COL_SU + COL_SV
PEER_HEADS = 8
PEER_NKEYS = 128
PEER_EXPERTS = PEER_NKEYS * PEER_NKEYS
PEER_TOPK = 16
PEER_DQ = 256
PEER_DQ_HALF = PEER_DQ // 2
PEER_HK = PEER_HEADS * PEER_TOPK
PEER_TOKEN_BLOCK = 128
LN_EPS = 1e-5
ALPHA = (2.0 * DEPTH) ** 0.25
BETA = (8.0 * DEPTH) ** -0.25


def _layer_norm(x, g, b):
    xf = x.astype(jnp.float32)
    mu = jnp.mean(xf, axis=-1, keepdims=True)
    var = jnp.mean(jnp.square(xf - mu), axis=-1, keepdims=True)
    y = (xf - mu) * lax.rsqrt(var + LN_EPS)
    return (y * g.astype(jnp.float32) + b.astype(jnp.float32)).astype(x.dtype)

def _rms_norm(x, g):
    xf = x.astype(jnp.float32)
    y = xf * lax.rsqrt(jnp.mean(jnp.square(xf), axis=-1, keepdims=True) + LN_EPS)
    return (y * g.astype(jnp.float32)).astype(x.dtype)

def _gla_chunked(q, k, v, logg):
    B, S, H, DK = q.shape
    DV = v.shape[-1]
    N = S // CHUNK

    def to_chunks(t):
        return t.astype(jnp.float32).reshape(B, N, CHUNK, H, t.shape[-1]).transpose(1, 0, 3, 2, 4)

    qc, kc, vc, gc = to_chunks(q), to_chunks(k), to_chunks(v), to_chunks(logg)
    causal = jnp.tril(jnp.ones((CHUNK, CHUNK), dtype=bool))

    def step(state, inp):
        qb, kb, vb, gb = inp
        bcum = jnp.cumsum(gb, axis=2)
        diff = bcum[:, :, :, None, :] - bcum[:, :, None, :, :]
        decay = jnp.exp(jnp.where(causal[:, :, None], diff, -jnp.inf))
        attn = jnp.einsum('bhtk,bhsk,bhtsk->bhts', qb, kb, decay)
        o = jnp.einsum('bhts,bhsv->bhtv', attn, vb) + \
            jnp.einsum('bhtk,bhkv->bhtv', qb * jnp.exp(bcum), state)
        b_last = bcum[:, :, -1:, :]
        state = jnp.exp(b_last[:, :, 0, :])[..., None] * state + \
            jnp.einsum('bhsk,bhsv->bhkv', kb * jnp.exp(b_last - bcum), vb)
        return state, o

    s0 = jnp.zeros((B, H, DK, DV), jnp.float32)
    _, o = lax.scan(step, s0, (qc, kc, vc, gc))
    return o.transpose(1, 0, 3, 2, 4).reshape(B, S, H, DV).astype(v.dtype)

def _spatial_gating(u_pre, v_pre, ln_g, ln_b, w_s, b_s):
    B, S, _ = u_pre.shape
    u = jax.nn.gelu(u_pre, approximate=False)
    v = _layer_norm(jax.nn.gelu(v_pre, approximate=False), ln_g, ln_b)
    blk = jnp.arange(SGU_WINDOW) // CHUNK
    mask = blk[None, :] <= blk[:, None]
    w = jnp.where(mask[None], w_s, 0)
    vb = v.reshape(B, S // SGU_WINDOW, SGU_WINDOW, SGU_GROUPS, SGU_GROUP_DIM)
    sv = jnp.einsum('gts,bnsgc->bntgc', w, vb) + b_s.T[:, :, None]
    return u * sv.reshape(B, S, SGU_WIDTH)

def _peer(x, wq, k1, k2, u_tab, v_tab):
    B, S, D = x.shape
    T = B * S
    xt = x.reshape(T, D)
    q = (xt @ wq).reshape(T, PEER_HEADS, 2, PEER_DQ_HALF)
    s1 = jnp.einsum('thd,nd->thn', q[:, :, 0], k1)
    s2 = jnp.einsum('thd,nd->thn', q[:, :, 1], k2)
    v1, i1 = lax.top_k(s1, PEER_TOPK)
    v2, i2 = lax.top_k(s2, PEER_TOPK)
    cand = (v1[..., :, None] + v2[..., None, :]).reshape(T, PEER_HEADS, PEER_TOPK * PEER_TOPK)
    cidx = (i1[..., :, None] * PEER_NKEYS + i2[..., None, :]).reshape(T, PEER_HEADS, PEER_TOPK * PEER_TOPK)
    sc, pos = lax.top_k(cand, PEER_TOPK)
    eidx = jnp.take_along_axis(cidx, pos, axis=-1).reshape(T, PEER_HK)
    gate = jax.nn.softmax(sc.astype(jnp.float32), axis=-1).astype(x.dtype).reshape(T, PEER_HK)
    nb = T // PEER_TOKEN_BLOCK

    def expert_block(args):
        xb, ib, gb = args
        ub = jnp.take(u_tab, ib, axis=0)
        act = jax.nn.gelu(jnp.einsum('td,tkd->tk', xb, ub), approximate=False)
        vb = jnp.take(v_tab, ib, axis=0)
        return jnp.einsum('tk,tkd->td', gb * act, vb)

    out = lax.map(expert_block, (xt.reshape(nb, PEER_TOKEN_BLOCK, D),
                                 eidx.reshape(nb, PEER_TOKEN_BLOCK, PEER_HK),
                                 gate.reshape(nb, PEER_TOKEN_BLOCK, PEER_HK)))
    return out.reshape(B, S, D)

def _mixer(x, w_in, w_gate_up, b_gate, gla_norm_g, sgu_ln_g, sgu_ln_b, sgu_w, sgu_b, w_out):
    B, S, _ = x.shape
    h = x @ w_in
    splits = np.cumsum([COL_Q, COL_K, COL_V, COL_R, COL_A, COL_SU]).tolist()
    q, k, v, r, a, su, sv = jnp.split(h, splits, axis=-1)
    logg = jax.nn.log_sigmoid((a @ w_gate_up + b_gate).astype(jnp.float32)) / GLA_GATE_NORMALIZER
    q = q.reshape(B, S, GLA_HEADS, GLA_DK) * (GLA_DK ** -0.5)
    k = k.reshape(B, S, GLA_HEADS, GLA_DK)
    v = v.reshape(B, S, GLA_HEADS, GLA_DV)
    o = _gla_chunked(q, k, v, logg.reshape(B, S, GLA_HEADS, GLA_DK))
    o = _rms_norm(o, gla_norm_g).reshape(B, S, GLA_WIDTH) * jax.nn.silu(r)
    g = _spatial_gating(su, sv, sgu_ln_g, sgu_ln_b, sgu_w, sgu_b)
    return jnp.concatenate([o, g], axis=-1) @ w_out

def second_inputs(seed: int = 0) -> dict:
    key = jax.random.key(seed)
    ks = jax.random.split(key, 24)
    L, D = DEPTH, D_MODEL
    nrm = lambda k, shape, s: jax.random.normal(k, shape, jnp.float32) * s
    return {
        "x": nrm(ks[0], (BATCH, SEQ, D), 1.0),
        "ln_in_g": 1.0 + nrm(ks[1], (D,), 0.02),
        "ln_in_b": nrm(ks[2], (D,), 0.02),
        "w_in": nrm(ks[3], (L, D, IN_COLS), D ** -0.5),
        "w_gate_up": nrm(ks[4], (L, GLA_GATE_RANK, GLA_HEADS * GLA_DK), GLA_GATE_RANK ** -0.5),
        "b_gate": nrm(ks[5], (L, GLA_HEADS * GLA_DK), 0.1),
        "gla_norm_g": 1.0 + nrm(ks[6], (L, GLA_DV), 0.02),
        "sgu_ln_g": 1.0 + nrm(ks[7], (L, SGU_WIDTH), 0.02),
        "sgu_ln_b": nrm(ks[8], (L, SGU_WIDTH), 0.02),
        "sgu_w": nrm(ks[9], (L, SGU_GROUPS, SGU_WINDOW, SGU_WINDOW), SGU_WINDOW ** -0.5),
        "sgu_b": 1.0 + nrm(ks[10], (L, SGU_GROUPS, SGU_WINDOW), 0.02),
        "w_out": nrm(ks[11], (L, D_MIX, D), BETA * D_MIX ** -0.5),
        "ln1_g": 1.0 + nrm(ks[12], (L, D), 0.02),
        "ln1_b": nrm(ks[13], (L, D), 0.02),
        "peer_wq": nrm(ks[14], (L, D, PEER_HEADS * PEER_DQ), D ** -0.5),
        "peer_k1": nrm(ks[15], (L, PEER_NKEYS, PEER_DQ_HALF), PEER_DQ_HALF ** -0.5),
        "peer_k2": nrm(ks[16], (L, PEER_NKEYS, PEER_DQ_HALF), PEER_DQ_HALF ** -0.5),
        "peer_u": nrm(ks[17], (L, PEER_EXPERTS, D), D ** -0.5),
        "peer_v": nrm(ks[18], (L, PEER_EXPERTS, D), BETA * PEER_HEADS ** -0.5),
        "ln2_g": 1.0 + nrm(ks[19], (L, D), 0.02),
        "ln2_b": nrm(ks[20], (L, D), 0.02),
    }

def second_block(x, ln_in_g, ln_in_b, w_in, w_gate_up, b_gate, gla_norm_g, sgu_ln_g, sgu_ln_b,
              sgu_w, sgu_b, w_out, ln1_g, ln1_b, peer_wq, peer_k1, peer_k2, peer_u, peer_v,
              ln2_g, ln2_b):
    h = _layer_norm(x, ln_in_g, ln_in_b)
    for l in range(DEPTH):
        mix = _mixer(h, w_in[l], w_gate_up[l], b_gate[l], gla_norm_g[l], sgu_ln_g[l], sgu_ln_b[l],
                     sgu_w[l], sgu_b[l], w_out[l])
        h = _layer_norm(ALPHA * h + mix, ln1_g[l], ln1_b[l])
        ffn = _peer(h, peer_wq[l], peer_k1[l], peer_k2[l], peer_u[l], peer_v[l])
        h = _layer_norm(ALPHA * h + ffn, ln2_g[l], ln2_b[l])
    return h


def setup_inputs(seed=0):
    out = dict(first_inputs(seed))
    for name, value in second_inputs(seed + 1).items():
        if name != "x":
            out[name + "_2"] = value
    return out


def reference(
    x, ffn1_norm, ffn1_w_gate, ffn1_w_up, ffn1_w_down, mix_norm, w_in, m_i_bias, m_f_bias,
    g_conv, g_a_log, g_dt_bias, m_out_norm, r_out_norm, g_out_norm, w_out, ffn2_norm,
    ffn2_w_gate, ffn2_w_up, ffn2_w_down, final_norm, ln_in_g_2, ln_in_b_2, w_in_2, w_gate_up_2,
    b_gate_2, gla_norm_g_2, sgu_ln_g_2, sgu_ln_b_2, sgu_w_2, sgu_b_2, w_out_2, ln1_g_2, ln1_b_2,
    peer_wq_2, peer_k1_2, peer_k2_2, peer_u_2, peer_v_2, ln2_g_2, ln2_b_2,
):
    x = first_block(
        x, ffn1_norm, ffn1_w_gate, ffn1_w_up, ffn1_w_down, mix_norm, w_in, m_i_bias, m_f_bias,
        g_conv, g_a_log, g_dt_bias, m_out_norm, r_out_norm, g_out_norm, w_out, ffn2_norm,
        ffn2_w_gate, ffn2_w_up, ffn2_w_down, final_norm,
    )
    return second_block(
        x, ln_in_g_2, ln_in_b_2, w_in_2, w_gate_up_2, b_gate_2, gla_norm_g_2, sgu_ln_g_2,
        sgu_ln_b_2, sgu_w_2, sgu_b_2, w_out_2, ln1_g_2, ln1_b_2, peer_wq_2, peer_k1_2,
        peer_k2_2, peer_u_2, peer_v_2, ln2_g_2, ln2_b_2,
    )


_drawn_inputs = setup_inputs


def setup_inputs(seed=0):
    import zlib

    import numpy as np

    out = dict(_drawn_inputs(seed))
    spreads = {}
    factors = {'m_i_bias': 64.0,
     'm_out_norm': 4.452,
     'r_out_norm': 4.469,
     'g_out_norm': 3.413,
     'ffn2_norm': 3.595,
     'b_gate_2': 4.482,
     'gla_norm_g_2': 7.229,
     'sgu_ln_g_2': 7.656,
     'sgu_ln_b_2': 18.335,
     'sgu_b_2': 17.37}
    for name, (base, spread) in spreads.items():
        noise = np.random.default_rng([zlib.crc32(name.encode()), seed]).standard_normal(out[name].shape)
        drawn = base * np.exp(spread * noise) if base else spread * noise
        out[name] = __import__('jax').numpy.asarray(drawn.astype(out[name].dtype))
    for name, factor in factors.items():
        out[name] = (out[name] * factor).astype(out[name].dtype)
    return out
```

```python
from contextlib import ExitStack

import numpy as np

import concourse.bass as bass
from concourse import mybir

F32 = mybir.dt.float32
U32 = mybir.dt.uint32
ALU = mybir.AluOpType
ACT = mybir.ActivationFunctionType
AX_X = mybir.AxisListType.X

P = 128
D = 1024
T = 256
NB = T // P
DC = D // P
DEPTH = 2
D_FF = 2816
FT = D_FF // P
RING = 6
NKEYS = 128
TOPK = 16
PH = 8
HK = PH * TOPK
EPS1 = 1e-6
EPS2 = 1e-5
ALPHA = (2.0 * DEPTH) ** 0.25
LOWEST = -3.0e38
LEVELS = 7
UNITS_BODY = 12

C_ID, C_TRI, C_ONE, C_LVL = 0, 128, 256, 384
C_RET = C_LVL + LEVELS * 128
C_COS = C_RET + 4 * 256
C_SIN = C_COS + 64
C_IOTA = C_SIN + 64
C_N = C_IOTA + 128
P_FFN1, P_MIX, P_FFN2, P_Y, P_CONV = 0, 8, 16, 24, 32
P_BIAS = P_CONV + 48
P_ALOG = P_BIAS + 12
P_W16 = P_ALOG + 4
P_N = P_W16 + 128
Q_GAIN, Q_BG, Q_SB, Q_K1 = 0, 8, 10, 14
Q_N = Q_K1 + 256

FFN_STAGES = [("xT", 8, 0), ("ffn", 2 * FT, 3 * FT)]
MIX1_STAGES = [("xT", 8, 0), ("tt", 16, 16), ("tok", 8, 16), ("small", 1, 0), ("cums", 1, 0), ("rows", 1, 0),
               ("mcols", 1, 0), ("bM", 2, 0), ("msc", 4, 0), ("mout", 2, 0), ("rtr", 4, 0), ("rsc", 4, 0),
               ("rout", 2, 0), ("gss", 4, 0), ("gtr", 4, 0), ("bg", 2, 0), ("bb", 2, 0), ("gkk", 4, 0),
               ("inv", 6 * LEVELS, 0), ("gout", 7, 0), ("yT", 8, 0), ("wout", 0, 8)]
MIX2_STAGES = [("xT", 8, 0), ("tt", 4, 4), ("tok", 8, 16), ("small", 1, 0), ("logg", 1, 0), ("lvl", 2 * LEVELS + 4, 0),
               ("gla", 2, 0), ("sgu", 2, 0), ("yT", 8, 0), ("wout", 0, 8)]
PEER_STAGES = [("xT", 8, 0), ("tt", 16, 16), ("score", 4, 0), ("U", NKEYS, NKEYS), ("selT", 2, 0), ("G", 64, 0),
               ("V", 0, NKEYS)]


def plan():
    base, k, j, u = {}, 0, 0, 0
    parts = []
    for l in range(DEPTH):
        parts += [(f"ffn1{l}", FFN_STAGES), (f"mix1{l}", MIX1_STAGES), (f"ffn2{l}", FFN_STAGES)]
    for l in range(DEPTH):
        parts += [(f"mix2{l}", MIX2_STAGES), (f"peer{l}", PEER_STAGES)]
    for part, stages in parts:
        for name, jobs, units in stages:
            base[part, name] = (k, j, u)
            k, u = k + jobs, u + units
            if not units:
                j += jobs
    return base, u


BASE, UNITS = plan()


def build_program(nc, x, stream, consts, p1, p2, swt, wa, wgu, rows1, rows2, rows3, out, debug=None):
    ctx = ExitStack()
    with ctx:
        def sb(name, shape, dt=F32):
            return ctx.enter_context(nc.sbuf_tensor(name, shape, dt))[tuple(slice(0, n) for n in shape)]

        def sem(name):
            return ctx.enter_context(nc.semaphore(name))

        arena = sb("arena", [P, NKEYS * T])
        ring = sb("ring", [P, RING, 1024])
        h = sb("h", [P, NB, D])
        xT = sb("xT_sb", [P, DC, T])
        cst = sb("cst", [P, C_N])
        rows = sb("rows_sb", [P, 2048])
        side = sb("side", [P, 2048])
        hid = sb("hid", [P, 4, T])
        pr1 = sb("pr1", [P, DEPTH, P_N])
        pr2 = sb("pr2", [P, DEPTH, Q_N])
        topv = sb("topv", [P, 2 * PH, TOPK])
        topi = sb("topi", [P, 2 * PH, TOPK], U32)
        topf = sb("topf", [P, 2 * PH, TOPK])
        st = sb("st", [P, 32])
        mhalf = sb("mhalf", [P, 1])
        eps1 = sb("eps1", [P, 1])
        posi = sb("posi", [P, PH, TOPK], U32)
        posa = sb("posa", [P, PH, TOPK], U32)
        pfa = sb("pfa", [P, PH, TOPK])
        pfb = sb("pfb", [P, PH, TOPK])
        gmx = sb("gmx", [P, PH])
        W = [ctx.enter_context(nc.psum_tensor(f"work{i}", [P, 512], F32)) for i in range(4)]
        ACC = [ctx.enter_context(nc.psum_tensor(f"acc{i}", [P, 512], F32)) for i in range(4)]

        ident = cst[:, C_ID:C_ID + 128]
        tri = cst[:, C_TRI:C_TRI + 128]
        ones = cst[:, C_ONE:C_ONE + 128]
        iota = cst[:, C_IOTA:C_IOTA + 128]

        def lvl(n):
            return cst[:, C_LVL + 128 * n:C_LVL + 128 * (n + 1)]

        used = [0]

        def area(*shape):
            n = int(np.prod(shape))
            a = arena[:, used[0]:used[0] + n]
            used[0] += n
            assert used[0] <= NKEYS * T
            if len(shape) == 1:
                return a
            names = "abcd"[:len(shape)]
            return a.rearrange(f"p ({' '.join(names)}) -> p {' '.join(names)}",
                               **{m: s for m, s in zip(names, shape)})

        xs = area(NB, D)
        y = area(NB, D)
        mark = used[0]
        mqk = area(4, T)
        cin = area(12, T + 4)
        cT = area(12, T)
        tok = area(NB, 2048)
        vaug = area(NB, 4, 65)
        g16 = area(NB, 16)
        lsg = area(3, NB, 8)
        nea = area(4)
        cg = area(NB, 8)
        cs = area(NB, 8)
        gl = area(NB, 4)
        pk = area(NB, 12)
        rows12 = area(T)
        mrow = area(T)
        mcol = area(NB, 4)
        guard = area(NB, 4)
        ew = area(4, 384)
        pm = area(4, 384)
        rden = area(4)
        hh = area(512)
        sq = area(512)
        ssq = area(4)
        rope = area(NB, 512)
        ropt = area(4, 512)
        rT = area(4, T)
        rp = area(4, 384)
        rn = area(2, 512)
        eg = area(NB, 4)
        el = area(NB, 4)
        vt = area(4, NB, P)
        vb = area(4, NB, P)
        kd = area(4, P)
        egb = area(4, P)
        qe = area(4, P)
        wT = area(4, P)
        S1 = area(4, P)
        u1 = area(4, P)

        def over(old, pattern, **sizes):
            names = "abc"[:len(old.shape) - 1]
            n = int(np.prod(list(sizes.values())))
            flat = old.rearrange(f"p {' '.join(names)} -> p ({' '.join(names)})") if len(names) > 1 else old
            return flat[:, 0:n].rearrange(pattern, **sizes)

        gsq = over(cin, "p (a t) -> p a t", a=8, t=T)
        kt = over(mqk, "p (h b t) -> p h b t", h=4, b=NB, t=P)
        kbe = over(rT, "p (h b t) -> p h b t", h=4, b=NB, t=P)
        dec = over(ew, "p (h b t) -> p h b t", h=4, b=NB, t=P)
        NT = over(pm, "p (h b t) -> p h b t", h=4, b=NB, t=P)
        QK = over(rp, "p (h b t) -> p h b t", h=4, b=NB, t=P)
        TI = over(xs[:, 0:1, :], "p (a t) -> p a t", a=8, t=P)
        WI = over(xs[:, 1:2, :], "p (a t) -> p a t", a=8, t=P)
        EL = over(ropt[:, 0:2, :], "p (a t) -> p a t", a=8, t=P)
        XI = over(ropt[:, 2:4, :], "p (a t) -> p a t", a=8, t=P)
        u0 = over(rope[:, 0:1, :], "p (a t) -> p a t", a=4, t=P)
        uv1 = over(rope[:, 1:2, :], "p (a t) -> p a t", a=4, t=P)
        used[0] = mark
        qkT = area(4, T)
        tok2 = area(NB, 2048)
        aT = area(T)
        zg = area(2, T)
        lg = area(2, T)
        bc = area(2, T)
        dff = area(2, T)
        lv_e = area(2, T)
        lv_q = area(2, 2, T)
        lv_k = area(2, 2, T)
        at = area(2, 4, P)
        off = area(4, P)
        lvt = area(512)
        hh2 = area(512)
        sq2 = area(512)
        ssq2 = area(4)
        bst = area(6)
        bag = area(2)
        used[0] = mark
        qT = area(16, T)
        A = arena[:, :].rearrange("p (j t) -> p j t", j=NKEYS)
        selv = rows[:, 0:3 * 2 * HK].rearrange("p (b s k) -> p b s k", b=NB, s=3)
        selT = rows[:, 768:768 + 3 * T].rearrange("p (s t) -> p s t", s=3)
        cand = rows[:, 1536:1792]
        cand2 = rows[:, 1792:2048]
        oh = xT[:, :, :].rearrange("p c t -> p (c t)").rearrange("p (r w t i) -> p r w t i", r=2, w=2, t=4)
        sc1 = side[:, :]
        swt_sb = side[:, 0:512].rearrange("p (g t) -> p g t", g=4)
        wa_sb = side[:, 512:640].rearrange("p (c n) -> p c n", c=DC)
        wgu_sb = side[0:16, 640:896]
        topf2 = topf[:, :, :]

        slot_loaded = [sem(f"slot_loaded{i}") for i in range(RING)]
        unit_done = sem("unit_done")
        job_done = sem("job_done")
        bank_free = [sem(f"bank_free{i}") for i in range(4)]
        acc_free = sem("acc_free")
        const_in = sem("const_in")
        x_in = sem("x_in")
        rows_in = sem("rows_in")
        side_in = sem("side_in")
        dve_step = sem("dve_step")
        act_step = sem("act_step")
        pool_step = sem("pool_step")
        stored = sem("stored")
        oh2_done = sem("oh2_done")
        stage_done = sem("stage_done")
        g_freed = sem("g_freed")
        rows_free = sem("rows_free")
        side_free = sem("side_free")
        named = {}

        def ev(name):
            if name not in named:
                named[name] = sem(name)
            return named[name]

        class Group:

            def __init__(self, part, name):
                self.k, self.j, self.u = BASE[part, name]

            def bank(self, q):
                return W[(self.k + q) % 4]

            def claim(self, pe, q, it=0):
                n = (self.k + q) // 4
                if n > 0:
                    pe.wait_ge(bank_free[(self.k + q) % 4], n + it)

            def ready(self, eng, q):
                eng.wait_ge(job_done, self.j + q + 1)

            def ready_unit(self, eng, i, it=0):
                eng.wait_ge(unit_done, self.u + i + 1 + it)

            def free(self, ins, q):
                ins.then_inc(bank_free[(self.k + q) % 4], 1)

            def freed(self, eng, q, it=0):
                eng.wait_ge(bank_free[(self.k + q) % 4], (self.k + q) // 4 + 1 + it)

            def unit(self, pe, i, it=0):
                n = self.u + i
                pe.wait_ge(slot_loaded[n % RING], 16 * (n // RING + 1) + it)
                return ring[:, n % RING, :]

        class Chain:

            def __init__(self, eng, semaphore):
                self.eng, self.sem, self.n = eng, semaphore, 0

            def __call__(self, ins):
                ins.then_inc(self.sem, 1)
                self.n += 1
                self.eng.wait_ge(self.sem, self.n)

        acc_use = {}
        for l in range(DEPTH):
            for part in (f"ffn1{l}", f"mix1{l}", f"ffn2{l}"):
                acc_use[part] = len(acc_use)
        for l in range(DEPTH):
            for part in (f"mix2{l}", f"peer{l}s", f"peer{l}"):
                acc_use[part] = len(acc_use)

        def acc_claim(pe, part):
            if acc_use[part]:
                pe.wait_ge(acc_free, acc_use[part])

        def h_added(eng, part):
            eng.wait_ge(acc_free, acc_use[part] + 1)

        block = ctx.enter_context(nc.Block())

        @block.sync
        def _(sp):
            for n in range(RING):
                sp.dma_start(ring[:, n, :], stream[n]).then_inc(slot_loaded[n], 16)
            rounds = UNITS // RING - 1
            with sp.Fori(0, rounds) as it:
                for s in range(RING):
                    sp.wait_ge(unit_done, it * RING + s + 1)
                    sp.dma_start(ring[:, s, :], stream[bass.ds(it * RING + RING + s, 1)].rearrange("a p n -> p (a n)"))\
                      .then_inc(slot_loaded[s], 16)
            for n in range(RING * (rounds + 1), UNITS):
                sp.wait_ge(unit_done, n - RING + 1)
                sp.dma_start(ring[:, n % RING, :], stream[n]).then_inc(slot_loaded[n % RING], 16)

        served = [0]

        def serve(pool, a, times=1):
            for _ in range(times):
                served[0] += 1
                pool.wait_ge(ev("square_ready"), served[0])
                pool.tensor_tensor(a, a, mhalf.broadcast_to(a.shape), ALU.pow).then_inc(ev("rsqrt_ready"), 1)

        def pool_mix1(pool, step, part, l):
            serve(pool, st[:, 2:4])
            G = Group(part, "tok")
            G.freed(pool, 2)
            G.freed(pool, 3)
            qk = tok[:, :, 512:1024].rearrange("p b (h m j) -> p b h m j", h=8, m=2)
            ro = rope.rearrange("p b (h m j) -> p b h m j", h=8, m=2)
            cos = cst[:, C_COS:C_COS + 64].rearrange("p (b j) -> p b j", b=NB).unsqueeze(2).broadcast_to([P, NB, 8, 32])
            sin = cst[:, C_SIN:C_SIN + 64].rearrange("p (b j) -> p b j", b=NB).unsqueeze(2).broadcast_to([P, NB, 8, 32])
            r4 = [ropt[:, m, :].rearrange("p (b h j) -> p b h j", b=NB, h=8) for m in range(4)]
            for m, (half, table) in enumerate(((0, cos), (1, sin), (0, sin), (1, cos))):
                ins = pool.tensor_tensor(r4[m], qk[:, :, :, half, :], table, ALU.mult)
            step(ins)
            pool.tensor_tensor(ro[:, :, :, 0, :], r4[0], r4[1], ALU.subtract)
            pool.tensor_tensor(ro[:, :, :, 1, :], r4[2], r4[3], ALU.add).then_inc(ev("rope_ready"), 1)
            serve(pool, ssq, 4)
            G = Group(part, "gtr")
            for i in range(4):
                G.freed(pool, i)
            pool.wait_ge(ev("beta_ready"), l + 1)
            pool.wait_ge(ev("pk_ready"), l + 1)
            pool.wait_ge(ev("egel_ready"), 2 * l + 2)
            beta = pk[:, :, 8:12].rearrange("p b h -> p h b").unsqueeze(3).broadcast_to([P, 4, NB, P])
            pool.tensor_tensor(vb, vt, beta, ALU.mult)
            step(pool.tensor_tensor(kbe, kt, beta, ALU.mult))
            pool.tensor_tensor(kbe, kbe, eg.rearrange("p b h -> p h b").unsqueeze(3).broadcast_to([P, 4, NB, P]),
                               ALU.mult).then_inc(ev("vb_ready"), 1)
            pool.tensor_tensor(kd, kt[:, :, 0, :], el[:, 0, :].unsqueeze(2).broadcast_to([P, 4, P]), ALU.mult)
            pool.wait_ge(ev("qkn_ready"), 4 * l + 4)
            pool.wait_ge(ev("egb_ready"), 4 * l + 4)
            pool.tensor_tensor(qe, cT[:, 0:4, 128:256], egb, ALU.mult).then_inc(ev("kd_ready"), 1)
            pool.wait_ge(ev("dec_exp"), 2 * l + 2)
            d8 = dec.rearrange("p h b t -> p (h b) t")
            pool.tensor_tensor(d8, d8, tri.unsqueeze(1).broadcast_to([P, 8, P]), ALU.mult)\
                .then_inc(ev("dec_ready"), 1)
            i8 = ident.unsqueeze(1).broadcast_to([P, 8, P])
            if l:
                pool.wait_ge(ev("y_ready"), l)
            pool.tensor_copy(TI, i8)
            pool.tensor_copy(WI, i8)
            G = Group(part, "gkk")
            for i in range(4):
                G.freed(pool, i)
            n8 = NT.rearrange("p h b t -> p (h b) t")
            G = Group(part, "inv")
            for n in range(LEVELS):
                if n:
                    G.ready(pool, 6 * (n - 1) + 1)
                pool.tensor_tensor(EL, n8, lvl(n).unsqueeze(1).broadcast_to([P, 8, P]), ALU.mult)\
                    .then_inc(ev("EL_ready"), 1)
            serve(pool, ssq, 2)

        @block.gpsimd
        def _(pool):
            pool.dma_start(h[:, :, :], x.rearrange("(b p) d -> p b d", p=P)).then_inc(x_in, 16)
            pool.dma_start(cst[:, :], consts).then_inc(const_in, 16)
            pool.dma_start(pr1[:, :, :], p1.rearrange("l p n -> p l n")).then_inc(const_in, 16)
            pool.dma_start(pr2[:, :, :], p2.rearrange("l p n -> p l n")).then_inc(const_in, 16)

            def load_rows(a, b):
                pool.dma_start(rows[:, 0:a.shape[0]], a.partition_broadcast(P)).then_inc(rows_in, 16)
                pool.dma_start(rows[:, 1024:1024 + b.shape[0]], b.partition_broadcast(P)).then_inc(rows_in, 16)

            step = Chain(pool, pool_step)
            pool.memset(eps1, EPS1)
            step(pool.memset(mhalf, -0.5))
            pool.wait_ge(const_in, 48)
            pool.dma_start(side[:, 0:1024], rows1.partition_broadcast(P)).then_inc(side_in, 16)
            load_rows(rows2[0, 0], rows2[0, 1])
            for l in range(DEPTH):
                serve(pool, st[:, 2:4])
                pool_mix1(pool, step, f"mix1{l}", l)
                serve(pool, st[:, 2:4])
            serve(pool, st[:, 2:4])
            serve(pool, st[:, 14:15], 2)
            for l in range(DEPTH):
                pool.wait_ge(side_free, l + 1)
                pool.dma_start(swt_sb, swt[l]).then_inc(side_in, 16)
                pool.dma_start(wa_sb, wa[l]).then_inc(side_in, 16)
                pool.dma_start(wgu_sb, wgu[l]).then_inc(side_in, 16)
                pool.wait_ge(rows_free, 3 * l + 1)
                load_rows(rows3[l, 0], rows3[l, 1])
                serve(pool, bag[:, 1:2], 2)
                pool.wait_ge(rows_free, 3 * l + 2)
                load_rows(rows2[2 * l + 1, 0], rows2[2 * l + 1, 1])
                serve(pool, ssq2, 2)
                serve(pool, st[:, 14:15], 2)
                pool.wait_ge(g_freed, l + 1)
                load_rows(rows2[2 * l + 2, 0], rows2[2 * l + 2, 1])
                serve(pool, st[:, 14:15], 2)
            pool.wait_ge(ev("out_ready"), 1)
            pool.dma_start(out.rearrange("(b p) d -> p b d", p=P), h[:, :, :]).then_inc(stored, 16)
            pool.wait_ge(stored, 16)

        @block.tensor
        def _(pe):
            def product_unit(G, i, out_, it=0, weights=True):
                w = G.unit(pe, i, it)
                for c in range(DC):
                    mm = pe.matmul(out_, lhsT=w[:, 128 * c:128 * c + 128], rhs=xT[:, c, :],
                                   start=(c == 0), stop=(c == DC - 1))
                mm.then_inc(unit_done, 1)

            def make_xT(part, src, name, count):
                G = Group(part, name)
                for c in range(DC):
                    G.claim(pe, c)
                    if c == 0:
                        pe.wait_ge(ev(count[0]), count[1])
                    for b in range(NB):
                        mm = pe.transpose(G.bank(c)[:, 128 * b:128 * b + 128], src[:, b, 128 * c:128 * c + 128], ident)
                    mm.then_inc(job_done, 1)
                for c in range(DC - 4, DC):
                    G.freed(pe, c)

            def down_unit(G, i, act, first, last, it=0):
                w = G.unit(pe, i, it)
                for b in range(NB):
                    for n in range(2):
                        mm = pe.matmul(ACC[2 * b + n][:, :], lhsT=act[:, 128 * b:128 * b + 128],
                                       rhs=w[:, 512 * n:512 * n + 512], start=first, stop=last)
                mm.then_inc(unit_done, 1)

            def ffn(part, n):
                make_xT(part, xs, "xT", ("xs_ready", n))
                G = Group(part, "ffn")

                def gate_up(t, it=0):
                    i = 3 * t - 1 if t else 0
                    for m in range(2):
                        G.claim(pe, 2 * t + m, it)
                        product_unit(G, i + m, G.bank(2 * t + m)[:, 0:T], 16 * it)

                def down(t, first, last, it=0):
                    G.freed(pe, 2 * t + 1, it)
                    down_unit(G, min(3 * t + 4, 3 * FT - 1), hid[:, 2 + t % 2, :], first, last, 16 * it)

                gate_up(0)
                gate_up(1)
                acc_claim(pe, part)
                down(0, True, False)
                gate_up(2)
                down(1, False, False)
                with pe.Fori(0, (FT - 4) // 2) as it:
                    for t in (3, 4):
                        gate_up(t, it)
                        down(t - 1, False, False, it)
                gate_up(FT - 1)
                down(FT - 2, False, False)
                down(FT - 1, False, True)

            def out_projection(part, n):
                make_xT(part, y, "yT", ("y_ready", n))
                G = Group(part, "wout")
                acc_claim(pe, part)
                for c in range(DC):
                    down_unit(G, c, xT[:, c, :], c == 0, c == DC - 1)

            def token_groups(part):
                G = Group(part, "tok")
                for g in range(4):
                    for b in range(NB):
                        G.claim(pe, 2 * g + b)
                    for i in range(4):
                        w = G.unit(pe, 4 * g + i)
                        for cc in range(2):
                            c = 2 * i + cc
                            for b in range(NB):
                                mm = pe.matmul(G.bank(2 * g + b)[:, :], lhsT=xT[:, c, 128 * b:128 * b + 128],
                                               rhs=w[:, 512 * cc:512 * cc + 512], start=(c == 0), stop=(c == DC - 1))
                        mm.then_inc(unit_done, 1)

            def mix1(part, l):
                make_xT(part, xs, "xT", ("xs_ready", 3 * l + 2))
                G = Group(part, "tt")
                for q in range(16):
                    G.claim(pe, q)
                    product_unit(G, q, G.bank(q)[:, 0:T])
                token_groups(part)
                G = Group(part, "small")
                G.claim(pe, 0)
                for b in range(NB):
                    for c in range(DC):
                        mm = pe.matmul(G.bank(0)[:, 16 * b:16 * b + 16], lhsT=xT[:, c, 128 * b:128 * b + 128],
                                       rhs=pr1[:, l, P_W16 + 16 * c:P_W16 + 16 * c + 16],
                                       start=(c == 0), stop=(c == DC - 1))
                mm.then_inc(job_done, 1)
                G = Group(part, "cums")
                G.claim(pe, 0)
                pe.wait_ge(ev("cg_ready"), l + 1)
                o = G.bank(0)
                pe.matmul(o[:, 0:8], lhsT=tri, rhs=cg[:, 0, :], start=True, stop=True)
                pe.matmul(o[:, 8:16], lhsT=tri, rhs=cg[:, 1, :], start=True, stop=False)
                pe.matmul(o[:, 8:12], lhsT=ones, rhs=cg[:, 0, 0:4], start=False, stop=True)
                pe.matmul(o[:, 16:20], lhsT=ones, rhs=cg[:, 0, 4:8], start=True, stop=True)
                pe.matmul(o[:, 20:24], lhsT=ones, rhs=cg[:, 1, 4:8], start=True, stop=True).then_inc(job_done, 1)
                G = Group(part, "rows")
                G.claim(pe, 0)
                pe.wait_ge(ev("pk_ready"), l + 1)
                for b in range(NB):
                    mm = pe.transpose(G.bank(0)[0:12, 128 * b:128 * b + 128], pk[:, b, :], ident)
                mm.then_inc(job_done, 1)
                G = Group(part, "mcols")
                G.claim(pe, 0)
                pe.wait_ge(ev("mrow_ready"), l + 1)
                for b in range(NB):
                    mm = pe.transpose(G.bank(0)[:, 4 * b:4 * b + 4], mrow[0:4, 128 * b:128 * b + 128], ident[0:4, 0:4])
                mm.then_inc(job_done, 1)

                def spread(name, src, first, n):
                    G = Group(part, name)
                    for q in range(2):
                        G.claim(pe, q)
                        for i in range(2):
                            r = first + 2 * q + i
                            mm = pe.matmul(G.bank(q)[:, T * i:T * i + T],
                                           lhsT=ident[0:n, r:r + 1].to_broadcast([n, P]), rhs=src[0:n, :],
                                           start=True, stop=True)
                        mm.then_inc(job_done, 1)

                spread("bM", mrow, 0, 4)

                def head_scores(name, qk, q0, k0):
                    G = Group(part, name)
                    for i in range(4):
                        s = slice(64 * (i % 2), 64 * (i % 2) + 64)
                        G.claim(pe, i)
                        kh, qh = qk[s, k0 + i // 2, :], qk[s, q0 + i // 2, :]
                        pe.matmul(G.bank(i)[:, 0:256], lhsT=kh[:, 0:128], rhs=qh, start=True, stop=True)
                        pe.matmul(G.bank(i)[:, 256:384], lhsT=kh[:, 128:256], rhs=qh[:, 128:256],
                                  start=True, stop=True).then_inc(job_done, 1)

                def head_out(name, p, v, n, of):
                    G, scores = Group(part, name), Group(part, of)
                    for b in range(NB):
                        G.claim(pe, b)
                        for i in range(4):
                            if b == 0:
                                scores.freed(pe, i)
                            o = G.bank(b)[:, n * i:n * i + n]
                            mm = pe.matmul(o, lhsT=p[:, i, 128 * b:128 * b + 128], rhs=v(0, i), start=True, stop=(b == 0))
                            if b:
                                mm = pe.matmul(o, lhsT=p[:, i, 256:384], rhs=v(1, i), start=False, stop=True)
                        mm.then_inc(job_done, 1)

                head_scores("msc", mqk, 0, 2)
                head_out("mout", pm, lambda b, i: vaug[:, b, i, :], 65, "msc")
                G = Group(part, "rtr")
                pe.wait_ge(ev("rope_ready"), l + 1)
                for q in range(4):
                    G.claim(pe, q)
                    for b in range(NB):
                        mm = pe.transpose(G.bank(q)[:, 128 * b:128 * b + 128], rope[:, b, 128 * q:128 * q + 128], ident)
                    mm.then_inc(job_done, 1)
                for q in range(4):
                    G.freed(pe, q)
                head_scores("rsc", rT, 0, 2)
                head_out("rout", rp, lambda b, i: tok[:, b, 1024 + 64 * i:1024 + 64 * i + 64], 64, "rsc")
                G = Group(part, "gss")
                pe.wait_ge(ev("gsq_ready"), l + 1)
                for q in range(4):
                    G.claim(pe, q)
                    pe.matmul(G.bank(q)[:, :], lhsT=ones, rhs=gsq[:, 2 * q:2 * q + 2, :], start=True, stop=True)\
                      .then_inc(job_done, 1)
                G = Group(part, "gtr")
                pe.wait_ge(ev("qkn_ready"), 4 * l + 4)
                for i in range(4):
                    G.claim(pe, i)
                    for b in range(NB):
                        pe.transpose(G.bank(i)[:, 128 * b:128 * b + 128], cT[:, 4 + i, 128 * b:128 * b + 128], ident)
                        mm = pe.transpose(G.bank(i)[:, 256 + 128 * b:384 + 128 * b],
                                          cT[:, 8 + i, 128 * b:128 * b + 128], ident)
                    mm.then_inc(job_done, 1)
                spread("bg", rows12, 4, 12)
                spread("bb", rows12, 8, 12)
                G = Group(part, "gkk")
                for i in range(4):
                    G.claim(pe, i)
                    for b in range(NB):
                        t = slice(128 * b, 128 * b + 128)
                        pe.matmul(G.bank(i)[:, t], lhsT=cT[:, 4 + i, t], rhs=cT[:, 4 + i, t], start=True, stop=True)
                        mm = pe.matmul(G.bank(i)[:, 256 + 128 * b:384 + 128 * b], lhsT=cT[:, 4 + i, t],
                                       rhs=cT[:, i, t], start=True, stop=True)
                    mm.then_inc(job_done, 1)
                G = Group(part, "inv")
                for n in range(LEVELS):
                    pe.wait_ge(ev("EL_ready"), LEVELS * l + n + 1)
                    for q, (lhs, rhs) in enumerate(((EL, TI), (WI, XI), (XI, WI))):
                        for half in range(2):
                            job = 6 * n + 2 * q + half
                            G.claim(pe, job)
                            if half == 0:
                                if q == 0 and n:
                                    for back in (4, 3, 2, 1):
                                        G.freed(pe, job - back)
                                if q == 1:
                                    G.freed(pe, job - 2)
                                    G.freed(pe, job - 1)
                            for m in range(4):
                                a = 4 * half + m
                                mm = pe.matmul(G.bank(job)[:, 128 * m:128 * m + 128], lhsT=lhs[:, a, :],
                                               rhs=rhs[:, a, :], start=True, stop=True)
                            mm.then_inc(job_done, 1)
                for back in (2, 1):
                    G.freed(pe, 6 * LEVELS - back)
                G = Group(part, "gout")

                def heads(job, pairs):
                    G.claim(pe, job)
                    for i in range(4):
                        for n, (lhs, rhs) in enumerate(pairs(i)):
                            mm = pe.matmul(G.bank(job)[:, 128 * i:128 * i + 128], lhsT=lhs, rhs=rhs,
                                           start=(n == 0), stop=(n == len(pairs(i)) - 1))
                    mm.then_inc(job_done, 1)

                pe.wait_ge(ev("vb_ready"), l + 1)
                pe.wait_ge(ev("kd_ready"), l + 1)
                heads(0, lambda i: [(WI[:, 2 * i, :], vb[:, i, 0, :])])
                heads(1, lambda i: [(WI[:, 2 * i + 1, :], vb[:, i, 1, :])])
                heads(2, lambda i: [(kbe[:, i, 1, :], WI[:, 2 * i + 1, :])])
                G.freed(pe, 0)
                heads(3, lambda i: [(kd[:, i, :], u0[:, i, :])])
                G.freed(pe, 2)
                G.freed(pe, 3)
                heads(4, lambda i: [(wT[:, i, :], S1[:, i, :])])
                heads(5, lambda i: [(QK[:, i, 0, :], u0[:, i, :])])
                G.freed(pe, 4)
                heads(6, lambda i: [(qe[:, i, :], S1[:, i, :]), (QK[:, i, 1, :], u1[:, i, :])])
                out_projection(part, l + 1)

            def mix2(part, l):
                make_xT(part, h, "xT", ("ln_ready", 2 * l + 1))
                G = Group(part, "tt")
                for q in range(4):
                    G.claim(pe, q)
                    product_unit(G, q, G.bank(q)[:, 0:T])
                token_groups(part)
                G = Group(part, "small")
                G.claim(pe, 0)
                pe.wait_ge(side_in, 16 + 48 * (l + 1))
                for c in range(DC):
                    mm = pe.matmul(G.bank(0)[0:16, 0:T], lhsT=wa_sb[:, c, :], rhs=xT[:, c, :],
                                   start=(c == 0), stop=(c == DC - 1))
                mm.then_inc(job_done, 1)
                G.freed(pe, 0)
                G = Group(part, "logg")
                G.claim(pe, 0)
                for m in range(2):
                    mm = pe.matmul(G.bank(0)[:, T * m:T * m + T], lhsT=wgu_sb[:, 128 * m:128 * m + 128],
                                   rhs=aT[0:16, :], start=True, stop=True)
                mm.then_inc(job_done, 1)
                G = Group(part, "lvl")
                for n in range(LEVELS + 2):
                    if n != LEVELS:
                        pe.wait_ge(ev("lv_ready"), (LEVELS + 1) * l + min(n, LEVELS) + 1)
                    qs, ks = (qkT[:, 0:2, :], qkT[:, 2:4, :]) if n == LEVELS else (lv_q[:, n % 2], lv_k[:, n % 2])
                    for odd in range(2):
                        job = 2 * n + odd
                        G.claim(pe, job)
                        s = slice(64 * odd, 64 * odd + 64)
                        pairs = [(0, 0), (1, 1)] if n <= LEVELS else [(0, 1)]
                        for m in range(2):
                            for b, (src, dst) in enumerate(pairs):
                                c = 128 * (len(pairs) * m + b)
                                mm = pe.matmul(G.bank(job)[:, c:c + 128], lhsT=ks[s, m, 128 * src:128 * src + 128],
                                               rhs=qs[s, m, 128 * dst:128 * dst + 128], start=True, stop=True)
                        mm.then_inc(job_done, 1)
                L = G
                G = Group(part, "gla")
                pe.wait_ge(ev("at_ready"), l + 1)
                L.freed(pe, 2 * LEVELS + 2)
                L.freed(pe, 2 * LEVELS + 3)
                for b in range(NB):
                    G.claim(pe, b)
                    for i in range(4):
                        o = G.bank(b)[:, 128 * i:128 * i + 128]
                        if b:
                            pe.matmul(o, lhsT=off[:, 2 * (i % 2) + i // 2, :], rhs=tok2[:, 0, 128 * i:128 * i + 128], start=True, stop=False)
                        mm = pe.matmul(o, lhsT=at[:, i % 2, 2 * (i // 2) + b, :], rhs=tok2[:, b, 128 * i:128 * i + 128],
                                       start=(b == 0), stop=True)
                    mm.then_inc(job_done, 1)
                G = Group(part, "sgu")
                pe.wait_ge(ev("sgv_ready"), l + 1)
                for b in range(NB):
                    G.claim(pe, b)
                    for i in range(4):
                        mm = pe.matmul(G.bank(b)[:, 128 * i:128 * i + 128], lhsT=swt_sb[:, i, :],
                                       rhs=tok2[:, b, 1536 + 128 * i:1664 + 128 * i], start=True, stop=True)
                    mm.then_inc(job_done, 1)
                out_projection(part, DEPTH + l + 1)

            def peer(part, l):
                make_xT(part, h, "xT", ("ln_ready", 2 * l + 2))
                G = Group(part, "tt")
                for q in range(16):
                    G.claim(pe, q)
                    product_unit(G, q, G.bank(q)[:, 0:T])
                for q in range(12, 16):
                    G.freed(pe, q)
                acc_claim(pe, part + "s")
                G = Group(part, "score")
                for b in range(NB):
                    for i in range(PH):
                        if b and i % 2 == 0:
                            G.claim(pe, i // 2)
                        o = (ACC[i // 2] if b == 0 else G.bank(i // 2))[:, 256 * (i % 2):256 * (i % 2) + 256]
                        for m in range(2):
                            mm = pe.matmul(o[:, 128 * m:128 * m + 128], lhsT=qT[:, 2 * i + m, 128 * b:128 * b + 128],
                                           rhs=pr2[:, l, Q_K1 + 128 * m:Q_K1 + 128 * m + 128], start=True, stop=True)
                        if b and i % 2:
                            mm.then_inc(job_done, 1)
                G = Group(part, "U")
                with pe.Fori(0, NKEYS // UNITS_BODY) as it:
                    for q in range(UNITS_BODY):
                        G.claim(pe, q, it * (UNITS_BODY // 4))
                        product_unit(G, q, G.bank(q)[:, 0:T], it * (16 * UNITS_BODY // RING))
                for q in range(NKEYS // UNITS_BODY * UNITS_BODY, NKEYS):
                    G.claim(pe, q)
                    product_unit(G, q, G.bank(q)[:, 0:T])
                G = Group(part, "selT")
                for b in range(NB):
                    G.claim(pe, b)
                    pe.wait_ge(ev("sel_ready"), NB * (l + 1))
                    for s in range(3):
                        mm = pe.transpose(G.bank(b)[:, 128 * s:128 * s + 128], selv[:, b, s, :], ident)
                    mm.then_inc(job_done, 1)
                G = Group(part, "G")
                with pe.Fori(0, 16) as it:
                    for q in range(4):
                        pe.wait_ge(oh2_done, it * 4 + (64 * l + q + 1))
                        G.claim(pe, q, it)
                        for t in range(4):
                            mm = pe.matmul(G.bank(q)[:, 128 * t:128 * t + 128], lhsT=oh[:, q % 2, 0, t, :],
                                           rhs=oh[:, q % 2, 1, t, :], start=True, stop=True)
                        mm.then_inc(job_done, 1)
                acc_claim(pe, part)
                G = Group(part, "V")

                def value_unit(i, first, last, it=None):
                    n = 0 if it is None else it
                    pe.wait_ge(stage_done, n * 6 + (NKEYS * l + i + 1))
                    down_unit(G, i, hid[:, i % 2, :], first, last, 16 * n)

                value_unit(0, True, False)
                value_unit(1, False, False)
                with pe.Fori(0, 20) as it:
                    for q in range(6):
                        value_unit(2 + q, False, False, it)
                for q in range(122, 128):
                    value_unit(q, False, q == 127)

            pe.wait_ge(const_in, 48)
            for l in range(DEPTH):
                ffn(f"ffn1{l}", 3 * l + 1)
                mix1(f"mix1{l}", l)
                ffn(f"ffn2{l}", 3 * l + 3)
            for l in range(DEPTH):
                mix2(f"mix2{l}", l)
                peer(f"peer{l}", l)

        @block.scalar
        def _(act):
            step = Chain(act, act_step)

            def xT_odd(part, name, gain):
                G = Group(part, name)
                for c in range(1, DC, 2):
                    G.ready(act, c)
                    kw = {} if gain is None else {"scale": gain[:, c:c + 1]}
                    G.free(act.activation(xT[:, c, :], G.bank(c)[:, 0:T], ACT.Copy, **kw), c)

            def squares(count):
                for b in range(NB):
                    act.activation(xs[:, b, :], h[:, b, :], ACT.Square, accum_out=st[:, b:b + 1])\
                       .then_inc(ev("sumsq"), 1)

            def ffn(part, l, gain):
                squares(0)
                xT_odd(part, "xT", pr1[:, l, gain:gain + 8])
                G = Group(part, "ffn")

                def gate(t, it=0):
                    G.ready_unit(act, 3 * t - 1 if t else 0, 6 * it)
                    if t >= 2:
                        G.freed(act, 2 * t - 3, it)
                    G.free(act.activation(hid[:, t % 2, :], G.bank(2 * t)[:, 0:T], ACT.Silu), 2 * t)

                for t in range(3):
                    gate(t)
                with act.Fori(0, (FT - 4) // 2) as it:
                    for t in (3, 4):
                        gate(t, it)
                gate(FT - 1)

            def mix1(part, l):
                squares(0)
                xT_odd(part, "xT", pr1[:, l, P_MIX:P_MIX + 8])
                G = Group(part, "tt")
                for q in range(16):
                    G.ready_unit(act, q)
                    src = G.bank(q)[:, 0:T]
                    if q < 4:
                        G.free(act.activation(mqk[:, q, :], src, ACT.Copy, scale=0.125 if q < 2 else 1.0), q)
                    else:
                        G.free(act.activation(cin[:, q - 4, 3:3 + T], src, ACT.Copy), q)
                G = Group(part, "tok")
                for q in range(8):
                    g, b = divmod(q, 2)
                    G.ready_unit(act, 4 * g + 3)
                    o = G.bank(q)
                    if g == 0:
                        act.activation(vaug[:, b, :, 0:64], o[:, 0:256].rearrange("p (h d) -> p h d", h=4), ACT.Copy)
                        G.free(act.activation(tok[:, b, 256:512], o[:, 256:512], ACT.Sigmoid), q)
                    elif g == 1:
                        G.free(act.activation(tok[:, b, 512:1024], o[:, :], ACT.Copy), q)
                    elif g == 2:
                        act.activation(tok[:, b, 1024:1280], o[:, 0:256], ACT.Copy)
                        G.free(act.activation(tok[:, b, 1280:1536], o[:, 256:512], ACT.Silu), q)
                    else:
                        G.free(act.activation(tok[:, b, 1536:2048], o[:, :], ACT.Silu), q)
                for m in range(3):
                    act.wait_ge(ev("conv_done"), 12 * l + 4 * m + 4)
                    act.activation(cT[:, 4 * m:4 * m + 4, :], cT[:, 4 * m:4 * m + 4, :], ACT.Silu)\
                       .then_inc(ev("conv_silu"), 1)
                act.wait_ge(ev("conv_silu"), 3 * l + 2)
                act.activation(gsq, cT[:, 0:8, :], ACT.Square).then_inc(ev("gsq_ready"), 1)
                act.wait_ge(ev("gate_abs"), l + 1)
                step(act.activation(lsg[:, 1], lsg[:, 0], ACT.Exp))
                act.activation(nea, pr1[:, l, P_ALOG:P_ALOG + 4], ACT.Exp)
                act.activation(lsg[:, 2], lsg[:, 1], ACT.Ln, bias=1.0).then_inc(ev("gate_ln"), 1)
                act.activation(pk[:, :, 8:12], g16[:, :, 12:16], ACT.Sigmoid).then_inc(ev("beta_ready"), 1)
                act.wait_ge(ev("gcols_ready"), l + 1)
                act.activation(eg, cs[:, :, 4:8], ACT.Exp).then_inc(ev("egel_ready"), 1)
                act.activation(el, el, ACT.Exp).then_inc(ev("egel_ready"), 1)
                act.wait_ge(ev("mm_ready"), l + 1)
                act.activation(guard, guard, ACT.Exp, scale=-1.0).then_inc(ev("guard_ready"), 1)
                G = Group(part, "bM")
                for q in range(2):
                    G.freed(act, q)
                    act.activation(ew[:, 2 * q:2 * q + 2, :], ew[:, 2 * q:2 * q + 2, :], ACT.Exp, scale=-1.0)\
                       .then_inc(ev("ew_ready"), 1)
                G = Group(part, "rtr")
                for q in range(4):
                    G.ready(act, q)
                    G.free(act.activation(rT[:, q, :], G.bank(q)[:, 0:T], ACT.Copy), q)
                G = Group(part, "gss")
                for q in range(4):
                    G.ready(act, q)
                    if q >= 2:
                        act.wait_ge(ev("qkn_ready"), 4 * l + q - 1)
                    G.free(act.activation(rn[:, q % 2, :], G.bank(q)[:, :], ACT.Sqrt, bias=eps1), q)
                G = Group(part, "gtr")
                for i in range(4):
                    G.ready(act, i)
                    act.activation(kt[:, i].rearrange("p b d -> p (b d)"), G.bank(i)[:, 0:256], ACT.Copy)
                    G.free(act.activation(vt[:, i].rearrange("p b d -> p (b d)"), G.bank(i)[:, 256:512], ACT.Copy), i)
                G = Group(part, "bg")
                for q in range(2):
                    G.ready(act, q)
                    for i in range(2):
                        act.activation(egb[:, 2 * q + i, :], G.bank(q)[:, T * i + 128:T * i + 256], ACT.Exp)\
                           .then_inc(ev("egb_ready"), 1)
                for q in range(2):
                    G.freed(act, q)
                    act.activation(dec[:, 2 * q:2 * q + 2], dec[:, 2 * q:2 * q + 2], ACT.Exp)\
                       .then_inc(ev("dec_exp"), 1)
                G = Group(part, "inv")
                for n in range(LEVELS):
                    for half in range(2):
                        job = 6 * n + half
                        G.ready(act, job)
                        G.free(act.activation(XI[:, 4 * half:4 * half + 4, :].rearrange("p a t -> p (a t)"),
                                              G.bank(job)[:, :], ACT.Copy), job)
                G = Group(part, "gout")
                for job, dst, scale in ((0, u0, 1.0), (2, wT, -1.0), (3, S1, 1.0)):
                    G.ready(act, job)
                    G.free(act.activation(dst.rearrange("p h t -> p (h t)"), G.bank(job)[:, :], ACT.Copy, scale=scale), job)
                xT_odd(part, "yT", pr1[:, l, P_Y:P_Y + 8])

            def mix2(part, l):
                xT_odd(part, "xT", None)
                G = Group(part, "tt")
                for q in range(4):
                    G.ready_unit(act, q)
                    G.free(act.activation(qkT[:, q, :], G.bank(q)[:, 0:T], ACT.Copy, scale=0.125 if q < 2 else 1.0), q)
                G = Group(part, "tok")
                for q in range(8):
                    g, b = divmod(q, 2)
                    G.ready_unit(act, 4 * g + 3)
                    func = (ACT.Copy, ACT.Silu, ACT.Gelu, ACT.Gelu)[g]
                    G.free(act.activation(tok2[:, b, 512 * g:512 * g + 512], G.bank(q)[:, :], func), q)
                G = Group(part, "small")
                G.ready(act, 0)
                G.free(act.activation(aT[0:16, :], G.bank(0)[0:16, 0:T], ACT.Copy), 0)
                act.wait_ge(ev("zabs_ready"), l + 1)
                step(act.activation(dff, dff, ACT.Exp))
                act.activation(lg, dff, ACT.Ln, bias=1.0).then_inc(ev("lg_ln"), 1)
                for m in range(LEVELS + 1):
                    act.wait_ge(ev("dabs_ready"), (LEVELS + 1) * l + m + 1)
                    act.activation(lv_e, dff, ACT.Exp, scale=-1.0 / 16.0).then_inc(ev("lv_exp"), 1)
                xT_odd(part, "yT", yg[:, l, :])

            def peer(part, l):
                xT_odd(part, "xT", None)
                G = Group(part, "tt")
                for q in range(16):
                    G.ready_unit(act, q)
                    G.free(act.activation(qT[:, q, :], G.bank(q)[:, 0:T], ACT.Copy), q)
                G = Group(part, "score")
                for q in range(4):
                    G.ready(act, q)
                    G.free(act.activation(sc1[:, 512 * q:512 * q + 512], G.bank(q)[:, :], ACT.Copy), q)
                G = Group(part, "U")
                with act.Fori(0, NKEYS // UNITS_BODY) as it:
                    for q in range(UNITS_BODY):
                        G.ready_unit(act, q, it * UNITS_BODY)
                        G.free(act.activation(arena[:, bass.ds(it * (UNITS_BODY * T) + q * T, T)],
                                              G.bank(q)[:, 0:T], ACT.Gelu), q)
                for q in range(NKEYS // UNITS_BODY * UNITS_BODY, NKEYS):
                    G.ready_unit(act, q)
                    G.free(act.activation(A[:, q, :], G.bank(q)[:, 0:T], ACT.Gelu), q)
                for b in range(NB):
                    act.wait_ge(ev("smx_ready"), NB * l + b + 1)
                    act.activation(selv[:, b, 2, :], selv[:, b, 2, :], ACT.Exp).then_inc(ev("smx_exp"), 1)
                act.wait_ge(g_freed, l + 1)
                G = Group(part, "V")

                def stage(j, it=0):
                    if j >= 2:
                        G.ready_unit(act, j - 2, it * 6)
                    act.activation(hid[:, j % 2, :], arena[:, bass.ds(it * (6 * T) + j * T, T)], ACT.Copy)\
                       .then_inc(stage_done, 1)

                stage(0)
                stage(1)
                with act.Fori(0, 21) as it:
                    for j in range(2, 8):
                        stage(j, it)

            yg = pr2[:, :, Q_GAIN:Q_GAIN + 8]
            act.wait_ge(const_in, 48)
            act.wait_ge(x_in, 16)
            for l in range(DEPTH):
                if l:
                    h_added(act, f"ffn2{l - 1}")
                ffn(f"ffn1{l}", l, P_FFN1)
                h_added(act, f"ffn1{l}")
                mix1(f"mix1{l}", l)
                h_added(act, f"mix1{l}")
                ffn(f"ffn2{l}", l, P_FFN2)
            h_added(act, f"ffn2{DEPTH - 1}")
            squares(0)
            for l in range(DEPTH):
                mix2(f"mix2{l}", l)
                peer(f"peer{l}", l)

        @block.vector
        def _(dve):
            step = Chain(dve, dve_step)
            ts, tt, stt = dve.tensor_scalar, dve.tensor_tensor, dve.scalar_tensor_tensor

            def xT_even(part, name, gain):
                G = Group(part, name)
                for c in range(0, DC, 2):
                    G.ready(dve, c)
                    if gain is None:
                        G.free(dve.tensor_copy(xT[:, c, :], G.bank(c)[:, 0:T]), c)
                    else:
                        G.free(ts(xT[:, c, :], G.bank(c)[:, 0:T], gain[:, c:c + 1], None, ALU.mult), c)

            norms = [0]
            asked = [0]

            def rsqrt(ins):
                ins.then_inc(ev("square_ready"), 1)
                asked[0] += 1
                dve.wait_ge(ev("rsqrt_ready"), asked[0])


            def rms_scale():
                norms[0] += 1
                dve.wait_ge(ev("sumsq"), NB * norms[0])
                rsqrt(ts(st[:, 2:4], st[:, 0:2], 1.0 / D, EPS1, ALU.mult, ALU.add))

            def rms(part, gain):
                rms_scale()
                for b in range(NB):
                    ins = ts(xs[:, b, :], h[:, b, :], st[:, 2 + b:3 + b], None, ALU.mult)
                ins.then_inc(ev("xs_ready"), 1)
                xT_even(part, "xT", gain)

            def add_to_h(part, last, scale_acc, scale_h):
                G, i = last
                G.ready_unit(dve, i)
                for b in range(NB):
                    for n in range(2):
                        hs = h[:, b, 512 * n:512 * n + 512]
                        if scale_h == 1.0:
                            ins = stt(hs, ACC[2 * b + n][:, :], scale_acc, hs, ALU.mult, ALU.add)
                        else:
                            ins = stt(hs, hs, scale_h, ACC[2 * b + n][:, :], ALU.mult, ALU.add)
                ins.then_inc(acc_free, 1)
                h_added(dve, part)

            def ffn(part, l, gain):
                rms(part, pr1[:, l, gain:gain + 8])
                G = Group(part, "ffn")

                def up(t, it=0):
                    G.ready_unit(dve, 3 * t if t else 1, 6 * it)
                    G.freed(dve, 2 * t, it)
                    if t >= 2:
                        G.ready_unit(dve, 3 * (t - 2) + 4, 6 * it)
                    G.free(tt(hid[:, 2 + t % 2, :], G.bank(2 * t + 1)[:, 0:T], hid[:, t % 2, :], ALU.mult), 2 * t + 1)

                for t in range(3):
                    up(t)
                with dve.Fori(0, (FT - 4) // 2) as it:
                    for t in (3, 4):
                        up(t, it)
                up(FT - 1)
                add_to_h(part, (G, 3 * FT - 1), 0.5, 1.0)

            def head_norm(src, n, d, eps, dst, gate, buf, sqb, ss, src_free=None):
                w = buf[:, 0:n * d].rearrange("p (h d) -> p h d", h=n)
                if src is not None:
                    ins = dve.tensor_copy(w, src)
                    if src_free is not None:
                        src_free[0].free(ins, src_free[1])
                        src_free[0].freed(dve, src_free[1])
                    else:
                        step(ins)
                s = sqb[:, 0:n * d].rearrange("p (h d) -> p h d", h=n)
                step(tt(s, w, w, ALU.mult))
                step(dve.tensor_reduce(ss[:, 0:n], s, AX_X, ALU.add))
                rsqrt(ts(ss[:, 0:n], ss[:, 0:n], 1.0 / d, eps, ALU.mult, ALU.add))
                step(tt(w, w, ss[:, 0:n].unsqueeze(2).broadcast_to([P, n, d]), ALU.mult))
                return tt(dst.rearrange("p (h d) -> p h d", h=n), w, gate.rearrange("p (h d) -> p h d", h=n), ALU.mult)

            def mix1(part, l):
                rms(part, pr1[:, l, P_MIX:P_MIX + 8])
                dve.memset(cin[:, :, 0:3], 0.0)
                step(dve.memset(vaug[:, :, :, 64:65], 1.0))
                G = Group(part, "tt")
                for q in range(12):
                    G.freed(dve, q + 4)
                    for tap in range(4):
                        w = pr1[:, l, P_CONV + 4 * q + tap:P_CONV + 4 * q + tap + 1]
                        src = cin[:, q, tap:tap + T]
                        if tap == 0:
                            step(ts(cT[:, q, :], src, w, None, ALU.mult))
                        elif tap < 3:
                            step(stt(cT[:, q, :], src, w, cT[:, q, :], ALU.mult, ALU.add))
                        else:
                            stt(cT[:, q, :], src, w, cT[:, q, :], ALU.mult, ALU.add).then_inc(ev("conv_done"), 1)
                G = Group(part, "small")
                G.ready(dve, 0)
                o = G.bank(0)[:, 0:32].rearrange("p (b n) -> p b n", b=NB)
                tt(g16[:, :, 0:12], o[:, :, 0:12],
                   pr1[:, l, P_BIAS:P_BIAS + 12].unsqueeze(1).broadcast_to([P, NB, 12]), ALU.add)
                G.free(dve.tensor_copy(g16[:, :, 12:16], o[:, :, 12:16]), 0)
                G.freed(dve, 0)
                stt(lsg[:, 0], g16[:, :, 4:12], -1.0, g16[:, :, 4:12], ALU.mult, ALU.min).then_inc(ev("gate_abs"), 1)
                dve.wait_ge(ev("gate_ln"), l + 1)
                stt(cg[:, :, 0:4], g16[:, :, 4:8], 0.0, lsg[:, 2, :, 0:4], ALU.min, ALU.subtract)
                step(stt(cg[:, :, 4:8], g16[:, :, 8:12], 0.0, lsg[:, 2, :, 4:8], ALU.max, ALU.add))
                stt(cg[:, :, 4:8], cg[:, :, 4:8], -1.0, nea.unsqueeze(1).broadcast_to([P, NB, 4]), ALU.mult, ALU.mult)\
                    .then_inc(ev("cg_ready"), 1)
                G = Group(part, "cums")
                G.ready(dve, 0)
                dve.tensor_copy(cs, G.bank(0)[:, 0:16].rearrange("p (b n) -> p b n", b=NB))
                G.free(dve.tensor_copy(gl, G.bank(0)[:, 16:24].rearrange("p (b n) -> p b n", b=NB)), 0)
                G.freed(dve, 0)
                tt(el, gl, cs[:, :, 4:8], ALU.subtract).then_inc(ev("gcols_ready"), 1)
                tt(pk[:, :, 0:4], g16[:, :, 0:4], cs[:, :, 0:4], ALU.subtract)
                dve.wait_ge(ev("beta_ready"), l + 1)
                dve.tensor_copy(pk[:, :, 4:8], cs[:, :, 4:8]).then_inc(ev("pk_ready"), 1)
                G = Group(part, "rows")
                G.ready(dve, 0)
                G.free(dve.tensor_copy(rows12[0:12, :], G.bank(0)[0:12, 0:T]), 0)
                G.freed(dve, 0)
                dve.tensor_tensor_scan(mrow[0:4, :], rows12[0:4, :], rows12[0:4, :], 0.0, ALU.max, ALU.max)\
                   .then_inc(ev("mrow_ready"), 1)
                G = Group(part, "mcols")
                G.ready(dve, 0)
                G.free(tt(guard, cs[:, :, 0:4], G.bank(0)[:, 0:8].rearrange("p (b n) -> p b n", b=NB), ALU.add), 0)
                G.freed(dve, 0)
                dve.tensor_copy(guard, guard).then_inc(ev("mm_ready"), 1)
                dve.wait_ge(ev("pk_ready"), l + 1)
                G = Group(part, "bM")
                for q in range(2):
                    G.ready(dve, q)
                    for i in range(2):
                        a = 2 * q + i
                        ts(ew[:, a, 0:256], G.bank(q)[:, T * i:T * i + T], pk[:, 0, a:a + 1], 0.0,
                           ALU.subtract, ALU.max)
                        ins = ts(ew[:, a, 256:384], G.bank(q)[:, T * i + 128:T * i + T], pk[:, 1, a:a + 1], 0.0,
                                 ALU.subtract, ALU.max)
                    G.free(ins, q)
                dve.wait_ge(ev("ew_ready"), 2 * l + 2)
                tri4 = tri.unsqueeze(1).broadcast_to([P, 4, P])
                tt(ew[:, :, 0:128], ew[:, :, 0:128], tri4, ALU.mult)
                step(tt(ew[:, :, 256:384], ew[:, :, 256:384], tri4, ALU.mult))
                G = Group(part, "msc")
                for i in range(4):
                    G.ready(dve, i)
                    G.free(tt(pm[:, i, :], G.bank(i)[:, 0:384], ew[:, i, :], ALU.mult), i)
                G = Group(part, "mout")
                dve.wait_ge(ev("guard_ready"), l + 1)
                for b in range(NB):
                    G.ready(dve, b)
                    o = G.bank(b)[:, 0:260].rearrange("p (h d) -> p h d", h=4)
                    den = o[:, :, 64:65].rearrange("p h d -> p (h d)")
                    step(tt(rden, den, guard[:, b, :], ALU.max))
                    step(stt(rden, den, -1.0, rden, ALU.mult, ALU.max))
                    step(dve.reciprocal(rden, rden))
                    G.free(tt(hh[:, 0:256].rearrange("p (h d) -> p h d", h=4), o[:, :, 0:64],
                              rden.unsqueeze(2).broadcast_to([P, 4, 64]), ALU.mult), b)
                    G.freed(dve, b)
                    step(head_norm(None, 4, 64, EPS1, y[:, b, 0:256], tok[:, b, 256:512], hh, sq, ssq))
                G = Group(part, "rsc")
                for i in range(4):
                    G.ready(dve, i)
                    dc = C_RET + 256 * i
                    tt(rp[:, i, 0:256], G.bank(i)[:, 0:256], cst[:, dc:dc + 256], ALU.mult)
                    G.free(tt(rp[:, i, 256:384], G.bank(i)[:, 256:384], cst[:, dc:dc + 128], ALU.mult), i)
                G = Group(part, "rout")
                for b in range(NB):
                    G.ready(dve, b)
                    step(head_norm(G.bank(b)[:, 0:256].rearrange("p (h d) -> p h d", h=4), 4, 64, EPS1,
                                   y[:, b, 256:512], tok[:, b, 1280:1536], hh, sq, ssq, (G, b)))
                dve.wait_ge(ev("conv_silu"), 3 * l + 3)
                G = Group(part, "gss")
                for q in range(4):
                    G.freed(dve, q)
                    step(dve.reciprocal(rn[:, q % 2, :], rn[:, q % 2, :]))
                    c2 = cT[:, 2 * q:2 * q + 2, :].rearrange("p a t -> p (a t)")
                    stt(c2, c2, 128.0 ** -0.5 if q < 2 else 1.0, rn[:, q % 2, :], ALU.mult, ALU.mult)\
                        .then_inc(ev("qkn_ready"), 1)
                    dve.wait_ge(ev("qkn_ready"), 4 * l + q + 1)
                G = Group(part, "bg")
                for q in range(2):
                    G.ready(dve, q)
                    dve.wait_ge(ev("egb_ready"), 4 * l + 2 * q + 2)
                    for i in range(2):
                        for b in range(NB):
                            a = 2 * q + i
                            ins = ts(dec[:, a, b, :], G.bank(q)[:, T * i + 128 * b:T * i + 128 * b + 128],
                                     pk[:, b, 4 + a:5 + a], 0.0, ALU.subtract, ALU.min)
                    G.free(ins, q)
                dve.wait_ge(ev("dec_ready"), l + 1)
                G = Group(part, "bb")
                for q in range(2):
                    G.ready(dve, q)
                    G.free(tt(NT[:, 2 * q:2 * q + 2].rearrange("p h b t -> p (h b t)"),
                              dec[:, 2 * q:2 * q + 2].rearrange("p h b t -> p (h b t)"), G.bank(q)[:, :], ALU.mult), q)
                    G.freed(dve, q)
                G = Group(part, "gkk")
                for i in range(4):
                    G.ready(dve, i)
                    n2 = NT[:, i].rearrange("p b t -> p (b t)")
                    tt(n2, n2, G.bank(i)[:, 0:256], ALU.mult)
                    G.free(tt(QK[:, i].rearrange("p b t -> p (b t)"), dec[:, i].rearrange("p b t -> p (b t)"),
                              G.bank(i)[:, 256:512], ALU.mult), i)
                G = Group(part, "inv")
                dve.wait_ge(ev("EL_ready"), LEVELS * l + 1)
                for n in range(LEVELS):
                    for q, buf in ((1, TI), (2, WI)):
                        for half in range(2):
                            job = 6 * n + 2 * q + half
                            G.ready(dve, job)
                            if n:
                                G.freed(dve, job - 6)
                            b2 = buf[:, 4 * half:4 * half + 4, :].rearrange("p a t -> p (a t)")
                            G.free(tt(b2, b2, G.bank(job)[:, :], ALU.subtract), job)
                G = Group(part, "gout")
                G.ready(dve, 1)
                G.free(dve.tensor_copy(uv1.rearrange("p h t -> p (h t)"), G.bank(1)[:, :]), 1)
                G.freed(dve, 1)
                G.ready(dve, 4)
                G.free(tt(u1.rearrange("p h t -> p (h t)"), uv1.rearrange("p h t -> p (h t)"), G.bank(4)[:, :], ALU.add), 4)
                for b in range(NB):
                    G.ready(dve, 5 + b)
                    ins = head_norm(G.bank(5 + b)[:, :].rearrange("p (h d) -> p h d", h=4), 4, 128, EPS1,
                                    y[:, b, 512:1024], tok[:, b, 1536:2048], hh, sq, ssq, (G, 5 + b))
                    if b == 0:
                        step(ins)
                ins.then_inc(ev("y_ready"), 1)
                xT_even(part, "yT", pr1[:, l, P_Y:P_Y + 8])
                add_to_h(part, (Group(part, "wout"), DC - 1), 1.0, 1.0)

            def layer_norm(n):
                dve.wait_ge(rows_in, 32 * (n + 1))
                for b in range(NB):
                    hb = h[:, b, :]
                    for m in range(2):
                        ins = dve.bn_stats(st[:, 6 * m:6 * m + 6], h[:, b, 512 * m:512 * m + 512])
                    step(ins)
                    step(dve.bn_aggr(st[:, 12:14], st[:, 0:12].rearrange("p (m s) -> p m s", m=2)))
                    rsqrt(ts(st[:, 14:15], st[:, 13:14], EPS2, None, ALU.add))
                    step(ts(hb, hb, st[:, 12:13], st[:, 14:15], ALU.subtract, ALU.mult))
                    step(tt(hb, hb, rows[:, 0:1024], ALU.mult))
                    ins = tt(hb, hb, rows[:, 1024:2048], ALU.add)
                    if b == 0:
                        step(ins)
                step(ins)
                dve.memset(st[:, 31:32], 0.0).then_inc(rows_free, 1)
                dve.memset(st[:, 30:31], 0.0).then_inc(ev("ln_ready" if n < 3 * DEPTH else "out_ready"), 1)

            def mix2(part, l):
                xT_even(part, "xT", None)
                G = Group(part, "logg")
                G.ready(dve, 0)
                for m in range(2):
                    ins = ts(zg[:, m, :], G.bank(0)[:, T * m:T * m + T], pr2[:, l, Q_BG + m:Q_BG + m + 1], None, ALU.add)
                G.free(ins, 0)
                G.freed(dve, 0)
                stt(dff, zg, -1.0, zg, ALU.mult, ALU.min).then_inc(ev("zabs_ready"), 1)
                step(ts(zg, zg, 0.0, None, ALU.min))
                dve.wait_ge(ev("lg_ln"), l + 1)
                for m in range(2):
                    ins = dve.tensor_tensor_scan(bc[:, m, :], zg[:, m, :], lg[:, m, :], 0.0, ALU.add, ALU.subtract)
                step(ins)
                tt4 = Group(part, "tt")
                for q in range(4):
                    tt4.freed(dve, q)
                G = Group(part, "lvl")
                lm = [lvl(n).unsqueeze(1).broadcast_to([P, 4, P]) for n in range(LEVELS)] + \
                     [ident.unsqueeze(1).broadcast_to([P, 4, P])]

                def level(m):
                    s = 1 << m
                    n = m if m < LEVELS else LEVELS + 1
                    if m:
                        dve.wait_ge(ev("lv_exp"), (LEVELS + 1) * l + m)
                    b4 = bc.rearrange("p m (k s) -> p (m k) s", s=2 * s)
                    step(tt(dff.rearrange("p m (k s) -> p (m k) s", s=2 * s), b4,
                            b4[:, :, s - 1:s].broadcast_to([P, T // s, 2 * s]), ALU.subtract))
                    stt(dff, dff, -1.0, dff, ALU.mult, ALU.max).then_inc(ev("dabs_ready"), 1)
                    if n >= 2:
                        G.ready(dve, 2 * (n - 2) + 1 if n <= LEVELS else 2 * LEVELS - 1)
                    dve.wait_ge(ev("lv_exp"), (LEVELS + 1) * l + m + 1)
                    tt(lv_q[:, n % 2], qkT[:, 0:2, :], lv_e, ALU.mult)
                    tt(lv_k[:, n % 2], qkT[:, 2:4, :], lv_e, ALU.mult).then_inc(ev("lv_ready"), 1)

                def gather(n):
                    for b in range(NB):
                        job = 2 * n + b
                        G.ready(dve, job)
                        o = G.bank(job)[:, :].rearrange("p (h t) -> p h t", h=4)
                        if n == 0:
                            G.free(tt(at[:, b], o, lm[0], ALU.mult), job)
                            G.freed(dve, job)
                        else:
                            t3 = lvt.rearrange("p (h t) -> p h t", h=4)
                            G.free(tt(t3, o, lm[n], ALU.mult), job)
                            G.freed(dve, job)
                            step(tt(at[:, b], at[:, b], t3, ALU.add))

                level(0)
                for m in range(1, LEVELS + 1):
                    level(m)
                    gather(m - 1)
                gather(LEVELS)
                dve.tensor_copy(st[:, 29:30], ident[:, 0:1]).then_inc(ev("at_ready"), 1)
                for odd in range(2):
                    job = 2 * LEVELS + 2 + odd
                    G.ready(dve, job)
                    G.free(dve.tensor_copy(off[:, 2 * odd:2 * odd + 2, :].rearrange("p h t -> p (h t)"),
                                           G.bank(job)[:, 0:256]), job)
                K = Group(part, "tok")
                for q in range(4, 8):
                    K.freed(dve, q)
                dve.wait_ge(rows_in, 32 * (3 * l + 2))
                for b in range(NB):
                    v = tok2[:, b, 1536:2048]
                    step(dve.bn_stats(bst, v))
                    step(dve.bn_aggr(bag, bst))
                    rsqrt(ts(bag[:, 1:2], bag[:, 1:2], EPS2, None, ALU.add))
                    step(ts(v, v, bag[:, 0:1], bag[:, 1:2], ALU.subtract, ALU.mult))
                    step(tt(v, v, rows[:, 0:512], ALU.mult))
                    step(tt(v, v, rows[:, 1024:1536], ALU.add))
                dve.memset(st[:, 31:32], 0.0).then_inc(rows_free, 1)
                dve.wait_ge(side_in, 16 + 48 * (l + 1))
                dve.memset(swt_sb[64:128, :, 0:64], 0.0).then_inc(ev("sgv_ready"), 1)
                G = Group(part, "gla")
                for b in range(NB):
                    G.ready(dve, b)
                    step(head_norm(G.bank(b)[:, :].rearrange("p (h d) -> p h d", h=4), 4, 128, EPS2,
                                   y[:, b, 0:512], tok2[:, b, 512:1024], hh2, sq2, ssq2, (G, b)))
                G = Group(part, "sgu")
                for b in range(NB):
                    G.ready(dve, b)
                    for i in range(4):
                        c = slice(128 * i, 128 * i + 128)
                        ins = stt(y[:, b, 512 + 128 * i:640 + 128 * i], G.bank(b)[:, c], pr2[:, l, Q_SB + i:Q_SB + i + 1],
                                  tok2[:, b, 1024 + 128 * i:1152 + 128 * i], ALU.add, ALU.mult)
                    G.free(ins, b)
                    G.freed(dve, b)
                dve.memset(st[:, 30:31], 0.0).then_inc(ev("y_ready"), 1)
                xT_even(part, "yT", yg[:, l, :])
                add_to_h(part, (Group(part, "wout"), DC - 1), 1.0, ALPHA)
                layer_norm(3 * l + 2)

            def top16(vals, idx, src, tmp):
                step(dve.max(vals[:, 0:8], src))
                step(dve.max_index(idx[:, 0:8], vals[:, 0:8], src))
                step(dve.match_replace(tmp, vals[:, 0:8], src, LOWEST))
                step(dve.max(vals[:, 8:16], tmp))
                step(dve.max_index(idx[:, 8:16], vals[:, 8:16], tmp))

            def peer(part, l):
                xT_even(part, "xT", None)
                for q in range(4):
                    Group(part, "score").freed(dve, q)
                for b in range(NB):
                    for i in range(PH):
                        for m in range(2):
                            c = 128 * m
                            src = ACC[i // 2][:, 256 * (i % 2) + c:256 * (i % 2) + c + 128] if b == 0 \
                                else sc1[:, 256 * i + c:256 * i + c + 128]
                            top16(topv[:, 2 * i + m, :], topi[:, 2 * i + m, :], src, cand[:, 0:128])
                        c3 = cand.rearrange("p (a c) -> p a c", a=TOPK)
                        step(tt(c3, topv[:, 2 * i, :].unsqueeze(2).broadcast_to([P, TOPK, TOPK]),
                                topv[:, 2 * i + 1, :].unsqueeze(1).broadcast_to([P, TOPK, TOPK]), ALU.add))
                        top16(selv[:, b, 2, 16 * i:16 * i + 16], posi[:, i, :], cand, cand2)
                    if b == 0:
                        dve.memset(st[:, 31:32], 0.0).then_inc(acc_free, 1)
                    else:
                        dve.memset(st[:, 31:32], 0.0).then_inc(side_free, 1)
                    step(dve.tensor_copy(topf, topi))
                    step(ts(posa, posi, 4, None, ALU.logical_shift_right))
                    step(ts(posi, posi, 15, None, ALU.bitwise_and))
                    step(dve.tensor_copy(pfa, posa))
                    step(dve.tensor_copy(pfb, posi))
                    io16 = iota[:, 0:TOPK].unsqueeze(1).broadcast_to([P, TOPK, TOPK])
                    c3 = cand.rearrange("p (a c) -> p a c", a=TOPK)
                    for i in range(PH):
                        for m, place in ((0, pfa), (1, pfb)):
                            step(tt(c3, place[:, i, :].unsqueeze(2).broadcast_to([P, TOPK, TOPK]), io16, ALU.is_equal))
                            step(tt(c3, c3, topf[:, 2 * i + m, :].unsqueeze(1).broadcast_to([P, TOPK, TOPK]), ALU.mult))
                            step(dve.tensor_reduce(selv[:, b, m, 16 * i:16 * i + 16], c3, AX_X, ALU.add))
                    g3 = selv[:, b, 2, :].rearrange("p (h k) -> p h k", h=PH)
                    step(dve.tensor_copy(gmx[:, 0:PH], g3[:, :, 0:1].rearrange("p h k -> p (h k)")))
                    tt(g3, g3, gmx[:, 0:PH].unsqueeze(2).broadcast_to([P, PH, TOPK]), ALU.subtract)\
                        .then_inc(ev("smx_ready"), 1)
                    dve.wait_ge(ev("smx_ready"), NB * l + b + 1)
                for b in range(NB):
                    g3 = selv[:, b, 2, :].rearrange("p (h k) -> p h k", h=PH)
                    dve.wait_ge(ev("smx_exp"), NB * l + b + 1)
                    step(dve.tensor_reduce(gmx[:, 0:PH], g3, AX_X, ALU.add))
                    step(dve.reciprocal(gmx[:, 0:PH], gmx[:, 0:PH]))
                    tt(g3, g3, gmx[:, 0:PH].unsqueeze(2).broadcast_to([P, PH, TOPK]), ALU.mult)\
                        .then_inc(ev("sel_ready"), 1)
                    dve.wait_ge(ev("sel_ready"), NB * l + b + 1)
                S = Group(part, "selT")
                for b in range(NB):
                    S.ready(dve, b)
                    S.free(dve.tensor_copy(selT[:, :, 128 * b:128 * b + 128],
                                           S.bank(b)[:, 0:384].rearrange("p (s t) -> p s t", s=3)), b)
                    S.freed(dve, b)
                G = Group(part, "G")
                U = Group(part, "U")
                for q in range(NKEYS - 4, NKEYS):
                    U.freed(dve, q)

                def one_hot(r, it, static):
                    dve.wait_ge(job_done, it * 4 + (G.j + static - 1))
                    for t in range(4):
                        ts(oh[:, r, 0, t, :], iota, selT[:, 0, bass.ds(it * 16 + (4 * static + t), 1)], None,
                           ALU.is_equal)
                    for t in range(4):
                        ins = ts(oh[:, r, 1, t, :], iota, selT[:, 1, bass.ds(it * 16 + (4 * static + t), 1)],
                                 selT[:, 2, bass.ds(it * 16 + (4 * static + t), 1)], ALU.is_equal, ALU.mult)
                    ins.then_inc(oh2_done, 1)

                def gate(q, it):
                    dve.wait_ge(job_done, it * 4 + (G.j + q + 1))
                    a3 = A[:, :, bass.ds(it * 16 + 4 * q, 4)]
                    G.free(tt(a3, a3, G.bank(q)[:, :].rearrange("p (t j) -> p j t", t=4), ALU.mult), q)

                with dve.Fori(0, 16) as it:
                    for q in range(4):
                        one_hot(q % 2, it, q)
                        if q:
                            gate(q - 1, it)
                    gate(3, it)
                for q in range(4):
                    G.freed(dve, 60 + q)
                dve.memset(st[:, 31:32], 0.0).then_inc(g_freed, 1)
                add_to_h(part, (Group(part, "V"), NKEYS - 1), 1.0, ALPHA)
                layer_norm(3 * l + 3)

            yg = pr2[:, :, Q_GAIN:Q_GAIN + 8]
            dve.wait_ge(const_in, 48)
            dve.wait_ge(x_in, 16)
            for l in range(DEPTH):
                ffn(f"ffn1{l}", l, P_FFN1)
                mix1(f"mix1{l}", l)
                ffn(f"ffn2{l}", l, P_FFN2)
            rms_scale()
            dve.wait_ge(side_in, 16)
            for b in range(NB):
                ins = stt(h[:, b, :], h[:, b, :], st[:, 2 + b:3 + b], side[:, 0:1024], ALU.mult, ALU.mult)
            step(ins)
            dve.memset(st[:, 31:32], 0.0).then_inc(side_free, 1)
            layer_norm(0)
            for l in range(DEPTH):
                mix2(f"mix2{l}", l)
                peer(f"peer{l}", l)


def tables():
    c = np.zeros((P, C_N), np.float32)
    i = np.arange(P)
    c[:, C_ID:C_ID + 128] = np.eye(P)
    c[:, C_TRI:C_TRI + 128] = i[:, None] <= i[None, :]
    c[:, C_ONE:C_ONE + 128] = 1.0
    for n in range(LEVELS):
        s = 1 << n
        m = (i[:, None] // (2 * s) == i[None, :] // (2 * s)) & (i[:, None] % (2 * s) < s) & (i[None, :] % (2 * s) >= s)
        c[:, C_LVL + 128 * n:C_LVL + 128 * (n + 1)] = m
    for a in range(4):
        lg = np.log1p(-np.exp2(-5.0 - a))
        for b in range(2):
            rel = i[None, :] + 128.0 * b - i[:, None]
            c[:, C_RET + 256 * a + 128 * b:C_RET + 256 * a + 128 * b + 128] = \
                np.where(rel >= 0, np.exp(np.maximum(rel, 0) * lg), 0.0) * 0.125
    inv = (np.float32(10000.0) ** (-np.arange(0, 64, 2, dtype=np.float32) / np.float32(64))).astype(np.float32)
    for b in range(NB):
        ang = ((i + 128 * b).astype(np.float32)[:, None] * inv[None, :]).astype(np.float32).astype(np.float64)
        c[:, C_COS + 32 * b:C_COS + 32 * b + 32] = np.cos(ang)
        c[:, C_SIN + 32 * b:C_SIN + 32 * b + 32] = np.sin(ang)
    c[:, C_IOTA:C_IOTA + 128] = i[None, :]
    return c


def columns(w):
    n = w.shape[1] // 128
    return w.reshape(DC, P, n, 128).transpose(2, 1, 0, 3).reshape(n, P, 1024)


def wide_columns(w):
    n = w.shape[1] // 512
    return w.reshape(4, 2, P, n, 512).transpose(3, 0, 2, 1, 4).reshape(4 * n, P, 1024)


def lay_out(v):
    units = np.empty((UNITS, P, 1024), np.float32)
    first = {n: u for n, (_, _, u) in BASE.items()}

    def put(part, name, a, i=0, step=1):
        u = first[part, name] + i
        units[u:u + step * (len(a) - 1) + 1:step] = a

    def ffn(part, gate, up, down):
        g, u, d = columns(gate), columns(up), down.reshape(FT, P, 1024)
        put(part, "ffn", g[:1], 0)
        put(part, "ffn", u[:1], 1)
        put(part, "ffn", g[1:], 2, 3)
        put(part, "ffn", u[1:], 3, 3)
        put(part, "ffn", d[:-1], 4, 3)
        put(part, "ffn", d[-1:], 3 * FT - 1)

    off = np.cumsum([0, 256, 256, 256, 256, 4, 4, 256, 256, 256, 256, 512, 512, 512, 512, 4, 4])
    off2 = np.cumsum([0, 256, 256, 512, 512, 16, 512, 512])
    p1 = np.zeros((DEPTH, P, P_N), np.float32)
    p2 = np.zeros((DEPTH, P, Q_N), np.float32)
    wa = np.zeros((DEPTH, P, DC, 16), np.float32)
    for l in range(DEPTH):
        ffn(f"ffn1{l}", v["ffn1_w_gate"][l], v["ffn1_w_up"][l], v["ffn1_w_down"][l])
        ffn(f"ffn2{l}", v["ffn2_w_gate"][l], v["ffn2_w_up"][l], v["ffn2_w_down"][l])
        w = v["w_in"][l]
        s = [w[:, off[n]:off[n + 1]] for n in range(16)]
        put(f"mix1{l}", "tt", columns(np.concatenate([s[0], s[1], s[10], s[11], s[12]], 1)))
        put(f"mix1{l}", "tok", wide_columns(np.concatenate([s[2], s[3], s[6], s[7], s[8], s[9], s[13]], 1)))
        put(f"mix1{l}", "wout", v["w_out"][l].reshape(DC, P, D))
        for at, name in ((P_FFN1, "ffn1_norm"), (P_MIX, "mix_norm"), (P_FFN2, "ffn2_norm")):
            p1[l, :, at:at + 8] = v[name][l].reshape(DC, P).T
        gains = np.concatenate([v["m_out_norm"][l], v["r_out_norm"][l], v["g_out_norm"][l]])
        p1[l, :, P_Y:P_Y + 8] = gains.reshape(DC, P).T
        p1[l, :, P_CONV:P_CONV + 48] = v["g_conv"][l].reshape(4, 12, P).transpose(2, 1, 0).reshape(P, 48)
        p1[l, :, P_BIAS:P_BIAS + 12] = np.concatenate([v["m_i_bias"][l], v["m_f_bias"][l], v["g_dt_bias"][l]])
        p1[l, :, P_ALOG:P_ALOG + 4] = v["g_a_log"][l]
        gates = np.concatenate([s[4], s[5], s[14], s[15]], 1)
        p1[l, :, P_W16:P_W16 + 128] = gates.reshape(DC, P, 16).transpose(1, 0, 2).reshape(P, 128)

        w = v["w_in_2"][l]
        s = [w[:, off2[n]:off2[n + 1]] for n in range(7)]
        put(f"mix2{l}", "tt", columns(np.concatenate([s[0], s[1]], 1)))
        put(f"mix2{l}", "tok", wide_columns(np.concatenate([s[2], s[3], s[5], s[6]], 1)))
        put(f"mix2{l}", "wout", v["w_out_2"][l].reshape(DC, P, D))
        wa[l] = s[4].reshape(DC, P, 16).transpose(1, 0, 2)
        put(f"peer{l}", "tt", columns(v["peer_wq_2"][l]))
        u = v["peer_u_2"][l].reshape(NKEYS, NKEYS, DC, P)
        put(f"peer{l}", "U", u.transpose(1, 3, 2, 0).reshape(NKEYS, P, 1024))
        put(f"peer{l}", "V", v["peer_v_2"][l].reshape(NKEYS, NKEYS, D).transpose(1, 0, 2))
        p2[l, :, Q_GAIN:Q_GAIN + 4] = v["gla_norm_g_2"][l][:, None]
        p2[l, :, Q_GAIN + 4:Q_GAIN + 8] = 1.0
        p2[l, :, Q_BG:Q_BG + 2] = v["b_gate_2"][l].reshape(2, P).T
        p2[l, :, Q_SB:Q_SB + 4] = v["sgu_b_2"][l].T
        p2[l, :, Q_K1:Q_K1 + 128] = v["peer_k1_2"][l].T
        p2[l, :, Q_K1 + 128:Q_K1 + 256] = v["peer_k2_2"][l].T
    swt = np.ascontiguousarray(v["sgu_w_2"].transpose(0, 3, 1, 2))
    rows2 = np.stack([np.stack([v["ln_in_g_2"], v["ln_in_b_2"]])] +
                     [np.stack([v[f"ln{n}_g_2"][l], v[f"ln{n}_b_2"][l]]) for l in range(DEPTH) for n in (1, 2)])
    rows3 = np.stack([v["sgu_ln_g_2"], v["sgu_ln_b_2"]], 1)
    return {
        "x": np.ascontiguousarray(v["x"][0]), "stream": units, "consts": tables(), "p1": p1, "p2": p2,
        "swt": swt, "wa": wa, "wgu": np.ascontiguousarray(v["w_gate_up_2"]),
        "rows1": np.ascontiguousarray(v["final_norm"]), "rows2": rows2, "rows3": rows3,
    }


def kernel(**inputs):
    import concourse.bacc as bacc
    from concourse.bass_utils import run_bass_kernel_spmd

    arrays = lay_out({k: np.asarray(a) for k, a in inputs.items()})
    nc = bacc.Bacc("TRN2", target_bir_lowering=False, num_devices=1)
    args = [nc.dram_tensor(f"in_{n}", a.shape, F32, kind="ExternalInput").ap() for n, a in arrays.items()]
    out = nc.dram_tensor("out", (T, D), F32, kind="ExternalOutput").ap()
    build_program(nc, *args, out)
    r = run_bass_kernel_spmd(nc, [{f"in_{n}": a for n, a in arrays.items()}], core_ids=[0])
    return r.results[0]["out"].reshape(1, T, D)
```

```python
from contextlib import ExitStack

import numpy as np

import concourse.bass as bass
from concourse import mybir

F32 = mybir.dt.float32
U32 = mybir.dt.uint32
F32R = mybir.dt.float32r
ALU = mybir.AluOpType
ACT = mybir.ActivationFunctionType
AX_X = mybir.AxisListType.X

P = 128
D = 1024
T = 256
NB = T // P
DC = D // P
DEPTH = 2
D_FF = 2816
FT = D_FF // P
SBUF_BASE = 16512
RING = 3
SPLIT = 3
NKEYS = 128
TOPK = 16
PH = 8
HK = PH * TOPK
EPS1 = 1e-6
EPS2 = 1e-5
ALPHA = (2.0 * DEPTH) ** 0.25
LOWEST = -3.0e38
LEVELS = 7
UNITS_BODY = 12

C_ID, C_TRI, C_ONE, C_IOTA = 0, 128, 256, 384
C_N = C_IOTA + 128
C_RET, C_COS, C_SIN, C_N1 = 0, 1024, 1088, 1152
P_FFN1, P_MIX, P_FFN2, P_Y, P_CONV = 0, 8, 16, 24, 32
P_BIAS = P_CONV + 48
P_ALOG = P_BIAS + 12
P_W16 = P_ALOG + 4
P_N = P_W16 + 128
Q_GAIN, Q_BG, Q_SB, Q_K1 = 0, 8, 10, 14
Q_N = Q_K1 + 256

FFN_STAGES = [("xT", 8, 0), ("ffn", 2 * FT, 3 * FT)]
MIX1_STAGES = [("xT", 8, 0), ("tt", 16, 16), ("tok", 8, 16), ("small", 1, 0), ("cums", 1, 0), ("rows", 1, 0),
               ("mcols", 1, 0), ("bM", 2, 0), ("msc", 4, 0), ("mout", 2, 0), ("rtr", 4, 0), ("rsc", 4, 0),
               ("rout", 2, 0), ("gss", 4, 0), ("gtr", 4, 0), ("bg", 2, 0), ("bb", 2, 0), ("gkk", 4, 0),
               ("inv", 6 * LEVELS, 0), ("gout", 7, 0), ("yT", 8, 0), ("wout", 0, 8)]
MIX2_STAGES = [("xT", 8, 0), ("tt", 4, 4), ("tok", 8, 16), ("small", 1, 0), ("logg", 1, 0), ("lvl", 2 * LEVELS + 4, 0),
               ("gla", 2, 0), ("sgu", 2, 0), ("yT", 8, 0), ("wout", 0, 8)]
PEER_STAGES = [("xT", 8, 0), ("tt", 16, 16), ("score", 4, 0), ("U", NKEYS, NKEYS), ("selT", 2, 0), ("G", 64, 0),
               ("V", 0, NKEYS)]


def plan():
    base, k, j, u = {}, 0, 0, 0
    parts = []
    for l in range(DEPTH):
        parts += [(f"ffn1{l}", FFN_STAGES), (f"mix1{l}", MIX1_STAGES), (f"ffn2{l}", FFN_STAGES)]
    for l in range(DEPTH):
        parts += [(f"mix2{l}", MIX2_STAGES), (f"peer{l}", PEER_STAGES)]
    for part, stages in parts:
        for name, jobs, units in stages:
            base[part, name] = (k, j, u)
            k, u = k + jobs, u + units
            if not units:
                j += jobs
    return base, u


BASE, UNITS = plan()
HELD = [BASE[f"peer{l}", "V"][2] for l in range(DEPTH)]


def build_program(nc, x, stream, consts, consts1, levels, p1, p2, swt, wa, wgu, rows1, rows2, rows3, out):
    ctx = ExitStack()
    with ctx:
        def sb(name, shape, dt=F32):
            return ctx.enter_context(nc.sbuf_tensor(name, shape, dt))[tuple(slice(0, n) for n in shape)]

        def sem(name):
            return ctx.enter_context(nc.semaphore(name))

        def at(name, place, shape, dt=F32):
            t = nc.alloc_sbuf_tensor_at(name, shape, dt, offset=SBUF_BASE + place)
            return t[tuple(slice(0, n) for n in shape)]

        arena = at("arena", 0, [P, NKEYS * T])
        scratch = at("scratch", 0, [P, NKEYS * T])
        place = 4 * NKEYS * T
        ring = at("ring", place, [P, RING, 1024])
        place += 4 * RING * 1024
        wsp = at("wsp", place, [P, SPLIT, 2, 1024], F32R)
        oh = at("one_hots", place, [P, 4, 2, 4, NKEYS])
        place += 4 * SPLIT * 2048
        xsp = at("xsp", place, [P, 2, DC, T], F32R)
        place += 16384
        h = at("h", place, [P, NB, D])
        sc1 = at("scores", place, [P, 2048])
        rows = at("rows_sb", place + 8192, [P, 2048])
        cst = at("cst", place + 16384, [P, C_N])
        place += 16384 + 4 * C_N
        hsp = at("hsp", place, [P, 2, 2, T], F32R)
        topv = at("topv", place, [P, 2 * PH, TOPK])
        topi = at("topi", place + 1024, [P, 2 * PH, TOPK], U32)
        topf = at("topf", place + 2048, [P, 2 * PH, TOPK])
        posi = at("posi", place + 3072, [P, PH, TOPK], U32)
        posa = at("posa", place + 3584, [P, PH, TOPK], U32)
        pfa = at("pfa", place + 4096, [P, PH, TOPK])
        pfb = at("pfb", place + 4608, [P, PH, TOPK])
        place += 5120
        pr2 = at("pr2", place, [P, DEPTH, Q_N])
        place += -(-4 * DEPTH * Q_N // 32) * 32
        st = at("st", place, [P, 32])
        gmx = at("gmx", place + 128, [P, PH])
        mhalf = at("mhalf", place + 160, [P, 1])
        eps1 = at("eps1", place + 192, [P, 1])
        assert SBUF_BASE + place + 224 <= nc.sbuf_usable_end and SBUF_BASE >= nc.sbuf_base
        W = [ctx.enter_context(nc.psum_tensor(f"work{i}", [P, 512], F32)) for i in range(4)]
        ACC = [ctx.enter_context(nc.psum_tensor(f"acc{i}", [P, 512], F32)) for i in range(4)]

        ident = cst[:, C_ID:C_ID + 128]
        tri = cst[:, C_TRI:C_TRI + 128]
        ones = cst[:, C_ONE:C_ONE + 128]
        iota = cst[:, C_IOTA:C_IOTA + 128]

        used = [0]

        def area(*shape):
            n = int(np.prod(shape))
            a = scratch[:, used[0]:used[0] + n]
            used[0] += n
            assert used[0] <= NKEYS * T
            if len(shape) == 1:
                return a
            names = "abcd"[:len(shape)]
            return a.rearrange(f"p ({' '.join(names)}) -> p {' '.join(names)}",
                               **{m: s for m, s in zip(names, shape)})

        xs = area(NB, D)
        y = area(NB, D)
        sil = area(2, T)
        prod = area(2, T)
        masks = area(LEVELS, P)

        def lvl(n):
            return masks[:, n, :]

        mark = used[0]
        cst1 = area(C_N1)
        pr1 = area(DEPTH, P_N)
        mqk = area(4, T)
        cin = area(12, T + 4)
        cT = area(12, T)
        tok = area(NB, 1792)
        vaug = area(NB, 4, 65)
        g16 = area(NB, 16)
        lsg = area(3, NB, 8)
        nea = area(4)
        cg = area(NB, 8)
        cs = area(NB, 8)
        gl = area(NB, 4)
        pk = area(NB, 12)
        rows12 = area(T)
        mrow = area(T)
        mcol = area(NB, 4)
        guard = area(NB, 4)
        ew = area(4, 384)
        pm = area(4, 384)
        rden = area(4)
        hh = area(512)
        sq = area(512)
        ssq = area(4)
        rope = area(NB, 512)
        ropt = area(4, 512)
        rT = area(4, T)
        eg = area(NB, 4)
        el = area(NB, 4)
        QK = area(4, NB, P)
        qe = area(4, P)

        def over(old, pattern, start=0, **sizes):
            names = "abc"[:len(old.shape) - 1]
            n = int(np.prod(list(sizes.values())))
            flat = old.rearrange(f"p {' '.join(names)} -> p ({' '.join(names)})") if len(names) > 1 else old
            return flat[:, start:start + n].rearrange(pattern, **sizes)

        gsq = over(cin, "p (a t) -> p a t", a=8, t=T)
        vt = over(cin, "p (h b t) -> p h b t", h=4, b=NB, t=P)
        vb = over(cin, "p (h b t) -> p h b t", start=1024, h=4, b=NB, t=P)
        u1 = over(cin, "p (a t) -> p a t", start=1024, a=4, t=P)
        kd = over(cin, "p (a t) -> p a t", start=2048, a=4, t=P)
        egb = over(cin, "p (a t) -> p a t", start=2560, a=4, t=P)
        final_row = over(cin, "p (a t) -> p (a t)", a=1, t=D)
        kt = over(mqk, "p (h b t) -> p h b t", h=4, b=NB, t=P)
        kbe = over(rT, "p (h b t) -> p h b t", h=4, b=NB, t=P)
        dec = over(ew, "p (h b t) -> p h b t", h=4, b=NB, t=P)
        rp = pm
        NT = over(pm, "p (h b t) -> p h b t", h=4, b=NB, t=P)
        TI = over(xs[:, 0:1, :], "p (a t) -> p a t", a=8, t=P)
        WI = over(xs[:, 1:2, :], "p (a t) -> p a t", a=8, t=P)
        EL = over(ropt[:, 0:2, :], "p (a t) -> p a t", a=8, t=P)
        XI = over(ropt[:, 2:4, :], "p (a t) -> p a t", a=8, t=P)
        rn = rope
        u0 = over(rope[:, 0:1, :], "p (a t) -> p a t", a=4, t=P)
        uv1 = over(rope[:, 1:2, :], "p (a t) -> p a t", a=4, t=P)
        wT = tok[:, 0, 256:768].rearrange("p (a t) -> p a t", a=4)
        S1 = tok[:, 1, 256:768].rearrange("p (a t) -> p a t", a=4)
        used[0] = mark
        swt_sb = area(4, P)
        wa_sb = area(DC, 16)
        wgu_sb = area(256)[0:16, :]
        qkT = area(4, T)
        tok2 = area(NB, 2048)
        aT = area(T)
        zg = area(2, T)
        lg = area(2, T)
        bc = area(2, T)
        dff = area(2, T)
        lv_e = area(2, T)
        lv_q = area(2, 2, T)
        lv_k = area(2, 2, T)
        at_ = area(2, 4, P)
        off = area(4, P)
        lvt = area(512)
        hh2 = area(512)
        sq2 = area(512)
        ssq2 = area(4)
        bst = area(6)
        bag = area(2)
        qT = arena[:, 0:16 * T].rearrange("p (a t) -> p a t", a=16)
        A = arena[:, :].rearrange("p (j t) -> p j t", j=NKEYS)
        selv = rows[:, 0:3 * 2 * HK].rearrange("p (b s k) -> p b s k", b=NB, s=3)
        selT = rows[:, 768:768 + 3 * T].rearrange("p (s t) -> p s t", s=3)
        cand = rows[:, 1536:1792]
        cand2 = rows[:, 1792:2048]

        slot_loaded = [sem(f"slot_loaded{i}") for i in range(RING)]
        unit_done = sem("unit_done")
        job_done = sem("job_done")
        bank_free = [sem(f"bank_free{i}") for i in range(4)]
        acc_free = sem("acc_free")
        const_in = sem("const_in")
        x_in = sem("x_in")
        rows_in = sem("rows_in")
        side_in = sem("side_in")
        dve_step = sem("dve_step")
        act_step = sem("act_step")
        pool_step = sem("pool_step")
        stored = sem("stored")
        h_saved = sem("h_saved")
        h_back = sem("h_back")
        saved = nc.dram_tensor("h_saved_dram", (P, NB, D), F32, kind="Internal").ap()
        oh_equal = sem("oh_equal")
        oh_done = sem("oh_done")
        high_done = sem("high_done")
        low_done = sem("low_done")
        act_high = sem("act_high")
        act_low = sem("act_low")
        xsp_high = sem("xsp_high")
        g_freed = sem("g_freed")
        rows_free = sem("rows_free")
        side_free = sem("side_free")
        named = {}

        def ev(name):
            if name not in named:
                named[name] = sem(name)
            return named[name]

        class Group:

            def __init__(self, part, name):
                self.k, self.j, self.u = BASE[part, name]

            def bank(self, q):
                return W[(self.k + q) % 4]

            def claim(self, pe, q, it=0):
                n = (self.k + q) // 4
                if n > 0:
                    pe.wait_ge(bank_free[(self.k + q) % 4], n + it)

            def ready(self, eng, q):
                eng.wait_ge(job_done, self.j + q + 1)

            def ready_unit(self, eng, i, it=0):
                eng.wait_ge(unit_done, self.u + i + 1 + it)

            def free(self, ins, q):
                ins.then_inc(bank_free[(self.k + q) % 4], 1)

            def freed(self, eng, q, it=0):
                eng.wait_ge(bank_free[(self.k + q) % 4], (self.k + q) // 4 + 1 + it)

            def unit(self, pe, i, it=0):
                n = self.u + i
                pe.wait_ge(low_done, n + 1 + it)
                return wsp[:, n % SPLIT, :, :]

        class Chain:

            def __init__(self, eng, semaphore):
                self.eng, self.sem, self.n = eng, semaphore, 0

            def __call__(self, ins):
                ins.then_inc(self.sem, 1)
                self.n += 1
                self.eng.wait_ge(self.sem, self.n)

        class Splitter:

            def __init__(self, eng, high):
                self.eng, self.high, self.next = eng, high, 0

            def one(self, n, it=0, body=6):
                src, dst = ring[:, n % RING, :], wsp[:, n % SPLIT, :, :]
                if self.high:
                    self.eng.wait_ge(slot_loaded[n % RING], 16 * (n // RING + 1) + (16 * body // RING) * it)
                    if n >= SPLIT:
                        self.eng.wait_ge(unit_done, n - SPLIT + 1 + body * it)
                    self.eng.activation(dst[:, 0, :], src, ACT.Copy).then_inc(high_done, 1)
                else:
                    self.eng.wait_ge(high_done, n + 1 + body * it)
                    self.eng.tensor_tensor(dst[:, 1, :], src, dst[:, 0, :].bitcast(F32), ALU.subtract)\
                        .then_inc(low_done, 1)

            def upto(self, n):
                while self.next <= min(n, UNITS - 1) and self.next not in HELD:
                    self.one(self.next)
                    self.next += 1

        TILES = 2 * DEPTH * FT
        acc_use = {}
        for l in range(DEPTH):
            for part in (f"ffn1{l}", f"mix1{l}", f"ffn2{l}"):
                acc_use[part] = len(acc_use)
        for l in range(DEPTH):
            for part in (f"mix2{l}", f"peer{l}s", f"peer{l}"):
                acc_use[part] = len(acc_use)

        def acc_claim(pe, part):
            if acc_use[part]:
                pe.wait_ge(acc_free, acc_use[part])

        def h_added(eng, part):
            eng.wait_ge(acc_free, acc_use[part] + 1)

        block = ctx.enter_context(nc.Block())

        @block.sync
        def _(sp):
            for n in range(RING):
                sp.dma_start(ring[:, n, :], stream[n]).then_inc(slot_loaded[n], 16)
            rounds = UNITS // RING - 1
            with sp.Fori(0, rounds) as it:
                for s in range(RING):
                    sp.wait_ge(low_done, it * RING + s + 1)
                    sp.dma_start(ring[:, s, :], stream[bass.ds(it * RING + RING + s, 1)].rearrange("a p n -> p (a n)"))\
                      .then_inc(slot_loaded[s], 16)
            for n in range(RING * (rounds + 1), UNITS):
                sp.wait_ge(low_done, n - RING + 1)
                sp.dma_start(ring[:, n % RING, :], stream[n]).then_inc(slot_loaded[n % RING], 16)

        served = [0]

        def serve(pool, a, times=1):
            for _ in range(times):
                served[0] += 1
                pool.wait_ge(ev("square_ready"), served[0])
                pool.tensor_tensor(a, a, mhalf.broadcast_to(a.shape), ALU.pow).then_inc(ev("rsqrt_ready"), 1)

        def pool_mix1(pool, step, part, l):
            serve(pool, st[:, 2:4])
            G = Group(part, "tok")
            G.freed(pool, 2)
            G.freed(pool, 3)
            qk = tok[:, :, 256:768].rearrange("p b (h m j) -> p b h m j", h=8, m=2)
            ro = rope.rearrange("p b (h m j) -> p b h m j", h=8, m=2)
            cos = cst1[:, C_COS:C_COS + 64].rearrange("p (b j) -> p b j", b=NB).unsqueeze(2).broadcast_to([P, NB, 8, 32])
            sin = cst1[:, C_SIN:C_SIN + 64].rearrange("p (b j) -> p b j", b=NB).unsqueeze(2).broadcast_to([P, NB, 8, 32])
            r4 = [ropt[:, m, :].rearrange("p (b h j) -> p b h j", b=NB, h=8) for m in range(4)]
            for m, (half, table) in enumerate(((0, cos), (1, sin), (0, sin), (1, cos))):
                ins = pool.tensor_tensor(r4[m], qk[:, :, :, half, :], table, ALU.mult)
            step(ins)
            pool.tensor_tensor(ro[:, :, :, 0, :], r4[0], r4[1], ALU.subtract)
            pool.tensor_tensor(ro[:, :, :, 1, :], r4[2], r4[3], ALU.add).then_inc(ev("rope_ready"), 1)
            serve(pool, ssq, 4)
            G = Group(part, "gtr")
            for i in range(4):
                G.freed(pool, i)
            pool.wait_ge(ev("beta_ready"), l + 1)
            pool.wait_ge(ev("pk_ready"), l + 1)
            pool.wait_ge(ev("egel_ready"), 2 * l + 2)
            beta = pk[:, :, 8:12].rearrange("p b h -> p h b").unsqueeze(3).broadcast_to([P, 4, NB, P])
            pool.tensor_tensor(vb, vt, beta, ALU.mult)
            step(pool.tensor_tensor(kbe, kt, beta, ALU.mult))
            pool.tensor_tensor(kbe, kbe, eg.rearrange("p b h -> p h b").unsqueeze(3).broadcast_to([P, 4, NB, P]),
                               ALU.mult).then_inc(ev("vb_ready"), 1)
            pool.tensor_tensor(kd, kt[:, :, 0, :], el[:, 0, :].unsqueeze(2).broadcast_to([P, 4, P]), ALU.mult)
            pool.wait_ge(ev("qkn_ready"), 4 * l + 4)
            pool.wait_ge(ev("egb_ready"), 4 * l + 4)
            pool.tensor_tensor(qe, cT[:, 0:4, 128:256], egb, ALU.mult).then_inc(ev("kd_ready"), 1)
            pool.wait_ge(ev("dec_exp"), 2 * l + 2)
            d8 = dec.rearrange("p h b t -> p (h b) t")
            pool.tensor_tensor(d8, d8, tri.unsqueeze(1).broadcast_to([P, 8, P]), ALU.mult)\
                .then_inc(ev("dec_ready"), 1)
            i8 = ident.unsqueeze(1).broadcast_to([P, 8, P])
            if l:
                pool.wait_ge(ev("y_ready"), l)
            pool.tensor_copy(TI, i8)
            pool.tensor_copy(WI, i8)
            G = Group(part, "gkk")
            for i in range(4):
                G.freed(pool, i)
            n8 = NT.rearrange("p h b t -> p (h b) t")
            G = Group(part, "inv")
            for n in range(LEVELS):
                if n:
                    G.ready(pool, 6 * (n - 1) + 1)
                pool.tensor_tensor(EL, n8, lvl(n).unsqueeze(1).broadcast_to([P, 8, P]), ALU.mult)\
                    .then_inc(ev("EL_ready"), 1)
            serve(pool, ssq, 2)

        @block.gpsimd
        def _(pool):
            pool.dma_start(h[:, :, :], x.rearrange("(b p) d -> p b d", p=P)).then_inc(x_in, 16)
            pool.dma_start(cst[:, :], consts).then_inc(const_in, 16)
            pool.dma_start(masks, levels.rearrange("n p t -> p n t")).then_inc(const_in, 16)
            pool.dma_start(cst1, consts1).then_inc(const_in, 16)
            pool.dma_start(pr1[:, :, :], p1.rearrange("l p n -> p l n")).then_inc(const_in, 16)
            pool.dma_start(pr2[:, :, :], p2.rearrange("l p n -> p l n")).then_inc(const_in, 16)

            def load_rows(a, b):
                pool.dma_start(rows[:, 0:a.shape[0]], a.partition_broadcast(P)).then_inc(rows_in, 16)
                pool.dma_start(rows[:, 1024:1024 + b.shape[0]], b.partition_broadcast(P)).then_inc(rows_in, 16)

            step = Chain(pool, pool_step)
            pool.memset(eps1, EPS1)
            step(pool.memset(mhalf, -0.5))
            pool.wait_ge(const_in, 80)
            load_rows(rows2[0, 0], rows2[0, 1])
            for l in range(DEPTH):
                serve(pool, st[:, 2:4])
                pool_mix1(pool, step, f"mix1{l}", l)
                serve(pool, st[:, 2:4])
            h_added(pool, f"mix1{DEPTH - 1}")
            pool.dma_start(final_row, rows1.partition_broadcast(P)).then_inc(side_in, 16)
            serve(pool, st[:, 2:4])
            serve(pool, st[:, 14:15], 2)
            for l in range(DEPTH):
                pool.wait_ge(side_free, l + 1)
                pool.dma_start(swt_sb, swt[l]).then_inc(side_in, 16)
                pool.dma_start(masks, levels.rearrange("n p t -> p n t")).then_inc(side_in, 16)
                pool.dma_start(wa_sb, wa[l]).then_inc(side_in, 16)
                pool.dma_start(wgu_sb, wgu[l]).then_inc(side_in, 16)
                pool.wait_ge(rows_free, 3 * l + 1)
                load_rows(rows3[l, 0], rows3[l, 1])
                serve(pool, bag[:, 1:2], 2)
                pool.wait_ge(rows_free, 3 * l + 2)
                load_rows(rows2[2 * l + 1, 0], rows2[2 * l + 1, 1])
                serve(pool, ssq2, 2)
                serve(pool, st[:, 14:15], 2)
                pool.wait_ge(ev("ln_ready"), 2 * l + 2)
                pool.dma_start(saved, h).then_inc(h_saved, 16)
                pool.wait_ge(h_saved, 16 * (l + 1))
                pool.wait_ge(ev("scores_read"), l + 1)
                pool.dma_start(h, saved).then_inc(h_back, 16)
                pool.wait_ge(g_freed, l + 1)
                load_rows(rows2[2 * l + 2, 0], rows2[2 * l + 2, 1])
                serve(pool, st[:, 14:15], 2)
            pool.wait_ge(ev("out_ready"), 1)
            pool.dma_start(out.rearrange("(b p) d -> p b d", p=P), h[:, :, :]).then_inc(stored, 16)
            pool.wait_ge(stored, 16)

        @block.tensor
        def _(pe):
            PARTS = ((0, 0), (0, 1), (1, 0))

            def product_unit(G, i, out_, it=0):
                w = G.unit(pe, i, it)
                for c in range(DC):
                    for n, (a, b) in enumerate(PARTS):
                        mm = pe.matmul(out_, lhsT=w[:, a, 128 * c:128 * c + 128], rhs=xsp[:, b, c, :],
                                       start=(c == 0 and n == 0), stop=(c == DC - 1 and n == 2))
                mm.then_inc(unit_done, 1)

            def make_xT(part, src, name, count):
                G = Group(part, name)
                for c in range(DC):
                    G.claim(pe, c)
                    if c == 0:
                        pe.wait_ge(ev(count[0]), count[1])
                    for b in range(NB):
                        mm = pe.transpose(G.bank(c)[:, 128 * b:128 * b + 128], src[:, b, 128 * c:128 * c + 128], ident)
                    mm.then_inc(job_done, 1)
                for c in range(DC - 4, DC):
                    G.freed(pe, c)

            def down_unit(G, i, act, first, last, it=0):
                w = G.unit(pe, i, it)
                for b in range(NB):
                    for m, (pa, pw) in enumerate(PARTS):
                        for n in range(2):
                            mm = pe.matmul(ACC[2 * b + n][:, :], lhsT=act[:, pa, 128 * b:128 * b + 128],
                                           rhs=w[:, pw, 512 * n:512 * n + 512],
                                           start=(first and m == 0), stop=(last and m == 2))
                mm.then_inc(unit_done, 1)

            def ffn(part, n, tiles):
                make_xT(part, xs, "xT", ("xs_ready", n))
                G = Group(part, "ffn")

                def gate_up(t, it=0):
                    i = 3 * t - 1 if t else 0
                    for m in range(2):
                        G.claim(pe, 2 * t + m, it)
                        product_unit(G, i + m, G.bank(2 * t + m)[:, 0:T], 6 * it)

                def down(t, first, last, it=0):
                    pe.wait_ge(act_low, tiles + t + 1 + 2 * it)
                    down_unit(G, min(3 * t + 4, 3 * FT - 1), hsp[:, t % 2, :, :], first, last, 6 * it)

                gate_up(0)
                gate_up(1)
                acc_claim(pe, part)
                down(0, True, False)
                gate_up(2)
                down(1, False, False)
                with pe.Fori(0, (FT - 4) // 2) as it:
                    for t in (3, 4):
                        gate_up(t, it)
                        down(t - 1, False, False, it)
                gate_up(FT - 1)
                down(FT - 2, False, False)
                down(FT - 1, False, True)

            def out_projection(part, n):
                make_xT(part, y, "yT", ("y_ready", n))
                G = Group(part, "wout")
                acc_claim(pe, part)
                for c in range(DC):
                    down_unit(G, c, xsp[:, :, c, :], c == 0, c == DC - 1)

            def token_groups(part):
                G = Group(part, "tok")
                for g in range(4):
                    for b in range(NB):
                        G.claim(pe, 2 * g + b)
                    for i in range(4):
                        w = G.unit(pe, 4 * g + i)
                        for cc in range(2):
                            c = 2 * i + cc
                            for b in range(NB):
                                for n, (px, pw) in enumerate(PARTS):
                                    mm = pe.matmul(G.bank(2 * g + b)[:, :], lhsT=xsp[:, px, c, 128 * b:128 * b + 128],
                                                   rhs=w[:, pw, 512 * cc:512 * cc + 512],
                                                   start=(c == 0 and n == 0), stop=(c == DC - 1 and n == 2))
                        mm.then_inc(unit_done, 1)

            def mix1(part, l):
                make_xT(part, xs, "xT", ("xs_ready", 3 * l + 2))
                G = Group(part, "tt")
                for q in range(16):
                    G.claim(pe, q)
                    product_unit(G, q, G.bank(q)[:, 0:T])
                token_groups(part)
                G = Group(part, "small")
                G.claim(pe, 0)
                for b in range(NB):
                    for c in range(DC):
                        for m in range(2):
                            mm = pe.matmul(G.bank(0)[:, 16 * b:16 * b + 16],
                                           lhsT=xsp[:, m, c, 128 * b:128 * b + 128].bitcast(F32),
                                           rhs=pr1[:, l, P_W16 + 16 * c:P_W16 + 16 * c + 16],
                                           start=(c == 0 and m == 0), stop=(c == DC - 1 and m == 1))
                mm.then_inc(job_done, 1)
                G = Group(part, "cums")
                G.claim(pe, 0)
                pe.wait_ge(ev("cg_ready"), l + 1)
                o = G.bank(0)
                pe.matmul(o[:, 0:8], lhsT=tri, rhs=cg[:, 0, :], start=True, stop=True)
                pe.matmul(o[:, 8:16], lhsT=tri, rhs=cg[:, 1, :], start=True, stop=False)
                pe.matmul(o[:, 8:12], lhsT=ones, rhs=cg[:, 0, 0:4], start=False, stop=True)
                pe.matmul(o[:, 16:20], lhsT=ones, rhs=cg[:, 0, 4:8], start=True, stop=True)
                pe.matmul(o[:, 20:24], lhsT=ones, rhs=cg[:, 1, 4:8], start=True, stop=True).then_inc(job_done, 1)
                G = Group(part, "rows")
                G.claim(pe, 0)
                pe.wait_ge(ev("pk_ready"), l + 1)
                for b in range(NB):
                    mm = pe.transpose(G.bank(0)[0:12, 128 * b:128 * b + 128], pk[:, b, :], ident)
                mm.then_inc(job_done, 1)
                G = Group(part, "mcols")
                G.claim(pe, 0)
                pe.wait_ge(ev("mrow_ready"), l + 1)
                for b in range(NB):
                    mm = pe.transpose(G.bank(0)[:, 4 * b:4 * b + 4], mrow[0:4, 128 * b:128 * b + 128], ident[0:4, 0:4])
                mm.then_inc(job_done, 1)

                def spread(name, src, first, n):
                    G = Group(part, name)
                    for q in range(2):
                        G.claim(pe, q)
                        for i in range(2):
                            r = first + 2 * q + i
                            mm = pe.matmul(G.bank(q)[:, T * i:T * i + T],
                                           lhsT=ident[0:n, r:r + 1].to_broadcast([n, P]), rhs=src[0:n, :],
                                           start=True, stop=True)
                        mm.then_inc(job_done, 1)

                spread("bM", mrow, 0, 4)

                def head_scores(name, qk, q0, k0):
                    G = Group(part, name)
                    for i in range(4):
                        s = slice(64 * (i % 2), 64 * (i % 2) + 64)
                        G.claim(pe, i)
                        kh, qh = qk[s, k0 + i // 2, :], qk[s, q0 + i // 2, :]
                        pe.matmul(G.bank(i)[:, 0:256], lhsT=kh[:, 0:128], rhs=qh, start=True, stop=True)
                        pe.matmul(G.bank(i)[:, 256:384], lhsT=kh[:, 128:256], rhs=qh[:, 128:256],
                                  start=True, stop=True).then_inc(job_done, 1)

                def head_out(name, p, v, n, of):
                    G, scores = Group(part, name), Group(part, of)
                    for b in range(NB):
                        G.claim(pe, b)
                        for i in range(4):
                            if b == 0:
                                scores.freed(pe, i)
                            o = G.bank(b)[:, n * i:n * i + n]
                            mm = pe.matmul(o, lhsT=p[:, i, 128 * b:128 * b + 128], rhs=v(0, i), start=True, stop=(b == 0))
                            if b:
                                mm = pe.matmul(o, lhsT=p[:, i, 256:384], rhs=v(1, i), start=False, stop=True)
                        mm.then_inc(job_done, 1)

                head_scores("msc", mqk, 0, 2)
                head_out("mout", pm, lambda b, i: vaug[:, b, i, :], 65, "msc")
                G = Group(part, "rtr")
                pe.wait_ge(ev("rope_ready"), l + 1)
                for q in range(4):
                    G.claim(pe, q)
                    for b in range(NB):
                        mm = pe.transpose(G.bank(q)[:, 128 * b:128 * b + 128], rope[:, b, 128 * q:128 * q + 128], ident)
                    mm.then_inc(job_done, 1)
                for q in range(4):
                    G.freed(pe, q)
                head_scores("rsc", rT, 0, 2)
                head_out("rout", rp, lambda b, i: tok[:, b, 768 + 64 * i:832 + 64 * i], 64, "rsc")
                G = Group(part, "gss")
                pe.wait_ge(ev("gsq_ready"), l + 1)
                for q in range(4):
                    G.claim(pe, q)
                    pe.matmul(G.bank(q)[:, :], lhsT=ones, rhs=gsq[:, 2 * q:2 * q + 2, :], start=True, stop=True)\
                      .then_inc(job_done, 1)
                G = Group(part, "gtr")
                pe.wait_ge(ev("qkn_ready"), 4 * l + 4)
                for i in range(4):
                    G.claim(pe, i)
                    for b in range(NB):
                        pe.transpose(G.bank(i)[:, 128 * b:128 * b + 128], cT[:, 4 + i, 128 * b:128 * b + 128], ident)
                        mm = pe.transpose(G.bank(i)[:, 256 + 128 * b:384 + 128 * b],
                                          cT[:, 8 + i, 128 * b:128 * b + 128], ident)
                    mm.then_inc(job_done, 1)
                spread("bg", rows12, 4, 12)
                spread("bb", rows12, 8, 12)
                G = Group(part, "gkk")
                for i in range(4):
                    G.claim(pe, i)
                    for b in range(NB):
                        t = slice(128 * b, 128 * b + 128)
                        pe.matmul(G.bank(i)[:, t], lhsT=cT[:, 4 + i, t], rhs=cT[:, 4 + i, t], start=True, stop=True)
                        mm = pe.matmul(G.bank(i)[:, 256 + 128 * b:384 + 128 * b], lhsT=cT[:, 4 + i, t],
                                       rhs=cT[:, i, t], start=True, stop=True)
                    mm.then_inc(job_done, 1)
                G = Group(part, "inv")
                for n in range(LEVELS):
                    pe.wait_ge(ev("EL_ready"), LEVELS * l + n + 1)
                    for q, (lhs, rhs) in enumerate(((EL, TI), (WI, XI), (XI, WI))):
                        for half in range(2):
                            job = 6 * n + 2 * q + half
                            G.claim(pe, job)
                            if half == 0:
                                if q == 0 and n:
                                    for back in (4, 3, 2, 1):
                                        G.freed(pe, job - back)
                                if q == 1:
                                    G.freed(pe, job - 2)
                                    G.freed(pe, job - 1)
                            for m in range(4):
                                a = 4 * half + m
                                mm = pe.matmul(G.bank(job)[:, 128 * m:128 * m + 128], lhsT=lhs[:, a, :],
                                               rhs=rhs[:, a, :], start=True, stop=True)
                            mm.then_inc(job_done, 1)
                for back in (2, 1):
                    G.freed(pe, 6 * LEVELS - back)
                G = Group(part, "gout")

                def heads(job, pairs):
                    G.claim(pe, job)
                    for i in range(4):
                        for n, (lhs, rhs) in enumerate(pairs(i)):
                            mm = pe.matmul(G.bank(job)[:, 128 * i:128 * i + 128], lhsT=lhs, rhs=rhs,
                                           start=(n == 0), stop=(n == len(pairs(i)) - 1))
                    mm.then_inc(job_done, 1)

                pe.wait_ge(ev("vb_ready"), l + 1)
                pe.wait_ge(ev("kd_ready"), l + 1)
                heads(0, lambda i: [(WI[:, 2 * i, :], vb[:, i, 0, :])])
                heads(1, lambda i: [(WI[:, 2 * i + 1, :], vb[:, i, 1, :])])
                heads(2, lambda i: [(kbe[:, i, 1, :], WI[:, 2 * i + 1, :])])
                G.freed(pe, 0)
                heads(3, lambda i: [(kd[:, i, :], u0[:, i, :])])
                G.freed(pe, 2)
                G.freed(pe, 3)
                heads(4, lambda i: [(wT[:, i, :], S1[:, i, :])])
                heads(5, lambda i: [(QK[:, i, 0, :], u0[:, i, :])])
                G.freed(pe, 4)
                heads(6, lambda i: [(qe[:, i, :], S1[:, i, :]), (QK[:, i, 1, :], u1[:, i, :])])
                out_projection(part, l + 1)

            def mix2(part, l):
                make_xT(part, h, "xT", ("ln_ready", 2 * l + 1))
                G = Group(part, "tt")
                for q in range(4):
                    G.claim(pe, q)
                    product_unit(G, q, G.bank(q)[:, 0:T])
                token_groups(part)
                G = Group(part, "small")
                G.claim(pe, 0)
                pe.wait_ge(side_in, 16 + 64 * (l + 1))
                for c in range(DC):
                    for m in range(2):
                        mm = pe.matmul(G.bank(0)[0:16, 0:T], lhsT=wa_sb[:, c, :], rhs=xsp[:, m, c, :].bitcast(F32),
                                       start=(c == 0 and m == 0), stop=(c == DC - 1 and m == 1))
                mm.then_inc(job_done, 1)
                G.freed(pe, 0)
                G = Group(part, "logg")
                G.claim(pe, 0)
                for m in range(2):
                    mm = pe.matmul(G.bank(0)[:, T * m:T * m + T], lhsT=wgu_sb[:, 128 * m:128 * m + 128],
                                   rhs=aT[0:16, :], start=True, stop=True)
                mm.then_inc(job_done, 1)
                G = Group(part, "lvl")
                for n in range(LEVELS + 2):
                    if n != LEVELS:
                        pe.wait_ge(ev("lv_ready"), (LEVELS + 1) * l + min(n, LEVELS) + 1)
                    qs, ks = (qkT[:, 0:2, :], qkT[:, 2:4, :]) if n == LEVELS else (lv_q[:, n % 2], lv_k[:, n % 2])
                    for odd in range(2):
                        job = 2 * n + odd
                        G.claim(pe, job)
                        s = slice(64 * odd, 64 * odd + 64)
                        pairs = [(0, 0), (1, 1)] if n <= LEVELS else [(0, 1)]
                        for m in range(2):
                            for b, (src, dst) in enumerate(pairs):
                                c = 128 * (len(pairs) * m + b)
                                mm = pe.matmul(G.bank(job)[:, c:c + 128], lhsT=ks[s, m, 128 * src:128 * src + 128],
                                               rhs=qs[s, m, 128 * dst:128 * dst + 128], start=True, stop=True)
                        mm.then_inc(job_done, 1)
                L = G
                G = Group(part, "gla")
                pe.wait_ge(ev("at_ready"), l + 1)
                L.freed(pe, 2 * LEVELS + 2)
                L.freed(pe, 2 * LEVELS + 3)
                for b in range(NB):
                    G.claim(pe, b)
                    for i in range(4):
                        o = G.bank(b)[:, 128 * i:128 * i + 128]
                        if b:
                            pe.matmul(o, lhsT=off[:, 2 * (i % 2) + i // 2, :], rhs=tok2[:, 0, 128 * i:128 * i + 128], start=True, stop=False)
                        mm = pe.matmul(o, lhsT=at_[:, i % 2, 2 * (i // 2) + b, :], rhs=tok2[:, b, 128 * i:128 * i + 128],
                                       start=(b == 0), stop=True)
                    mm.then_inc(job_done, 1)
                G = Group(part, "sgu")
                pe.wait_ge(ev("sgv_ready"), l + 1)
                for b in range(NB):
                    G.claim(pe, b)
                    for i in range(4):
                        mm = pe.matmul(G.bank(b)[:, 128 * i:128 * i + 128], lhsT=swt_sb[:, i, :],
                                       rhs=tok2[:, b, 1536 + 128 * i:1664 + 128 * i], start=True, stop=True)
                    mm.then_inc(job_done, 1)
                out_projection(part, DEPTH + l + 1)

            def peer(part, l):
                make_xT(part, h, "xT", ("ln_ready", 2 * l + 2))
                G = Group(part, "tt")
                for q in range(16):
                    G.claim(pe, q)
                    product_unit(G, q, G.bank(q)[:, 0:T])
                for q in range(12, 16):
                    G.freed(pe, q)
                acc_claim(pe, part + "s")
                G = Group(part, "score")
                for b in range(NB):
                    for i in range(PH):
                        if b and i % 2 == 0:
                            G.claim(pe, i // 2)
                        o = (ACC[i // 2] if b == 0 else G.bank(i // 2))[:, 256 * (i % 2):256 * (i % 2) + 256]
                        for m in range(2):
                            mm = pe.matmul(o[:, 128 * m:128 * m + 128], lhsT=qT[:, 2 * i + m, 128 * b:128 * b + 128],
                                           rhs=pr2[:, l, Q_K1 + 128 * m:Q_K1 + 128 * m + 128], start=True, stop=True)
                        if b and i % 2:
                            mm.then_inc(job_done, 1)
                G = Group(part, "U")
                with pe.Fori(0, NKEYS // UNITS_BODY) as it:
                    for q in range(UNITS_BODY):
                        G.claim(pe, q, it * (UNITS_BODY // 4))
                        product_unit(G, q, G.bank(q)[:, 0:T], it * UNITS_BODY)
                for q in range(NKEYS // UNITS_BODY * UNITS_BODY, NKEYS):
                    G.claim(pe, q)
                    product_unit(G, q, G.bank(q)[:, 0:T])
                G = Group(part, "selT")
                for b in range(NB):
                    G.claim(pe, b)
                    pe.wait_ge(ev("sel_ready"), NB * (l + 1))
                    for s in range(3):
                        mm = pe.transpose(G.bank(b)[:, 128 * s:128 * s + 128], selv[:, b, s, :], ident)
                    mm.then_inc(job_done, 1)
                G = Group(part, "G")
                with pe.Fori(0, 16) as it:
                    for q in range(4):
                        pe.wait_ge(oh_done, it * 4 + (64 * l + q + 1))
                        G.claim(pe, q, it)
                        for t in range(4):
                            mm = pe.matmul(G.bank(q)[:, 128 * t:128 * t + 128], lhsT=oh[:, q, 0, t, :],
                                           rhs=oh[:, q, 1, t, :], start=True, stop=True)
                        mm.then_inc(job_done, 1)
                acc_claim(pe, part)
                G = Group(part, "V")

                def value_unit(i, first, last, it=None):
                    n = 0 if it is None else it
                    pe.wait_ge(act_low, n * 6 + (TILES + NKEYS * l + i + 1))
                    down_unit(G, i, hsp[:, i % 2, :, :], first, last, 6 * n)

                value_unit(0, True, False)
                value_unit(1, False, False)
                with pe.Fori(0, 20) as it:
                    for q in range(6):
                        value_unit(2 + q, False, False, it)
                for q in range(122, 128):
                    value_unit(q, False, q == 127)

            pe.wait_ge(const_in, 80)
            for l in range(DEPTH):
                ffn(f"ffn1{l}", 3 * l + 1, 2 * l * FT)
                mix1(f"mix1{l}", l)
                ffn(f"ffn2{l}", 3 * l + 3, (2 * l + 1) * FT)
            for l in range(DEPTH):
                mix2(f"mix2{l}", l)
                peer(f"peer{l}", l)

        @block.scalar
        def _(act):
            step = Chain(act, act_step)
            split = Splitter(act, True)

            def xsp_highs(part, name, gain):
                G = Group(part, name)
                for c in range(DC):
                    G.ready(act, c)
                    act.activation(xsp[:, 0, c, :], G.bank(c)[:, 0:T], ACT.Copy,
                                   scale=1.0 if gain is None else gain[:, c:c + 1]).then_inc(xsp_high, 1)

            def squares(count):
                for b in range(NB):
                    act.activation(xs[:, b, :], h[:, b, :], ACT.Square, accum_out=st[:, b:b + 1])\
                       .then_inc(ev("sumsq"), 1)

            def ffn(part, l, gain):
                squares(0)
                xsp_highs(part, "xT", pr1[:, l, gain:gain + 8])
                G = Group(part, "ffn")

                def gate(t, it=0):
                    G.ready_unit(act, 3 * t - 1 if t else 0, 6 * it)
                    if t >= 2:
                        G.freed(act, 2 * t - 3, it)
                    G.free(act.activation(sil[:, t % 2, :], G.bank(2 * t)[:, 0:T], ACT.Silu), 2 * t)

                def high(t, it=0):
                    G.freed(act, 2 * t + 1, it)
                    if t >= 2:
                        G.ready_unit(act, 3 * (t - 2) + 4, 6 * it)
                    act.activation(hsp[:, t % 2, 0, :], prod[:, t % 2, :], ACT.Copy).then_inc(act_high, 1)

                for t in range(3):
                    split.upto(G.u + (3 * t + 1 if t else 2))
                    gate(t)
                    split.upto(G.u + (3 * t + 2 if t else 3))
                    high(t)
                with act.Fori(0, (FT - 4) // 2) as it:
                    for t in (3, 4):
                        split.one(G.u + 3 * t, it)
                        split.one(G.u + 3 * t + 1, it)
                        gate(t, it)
                        split.one(G.u + 3 * t + 2, it)
                        high(t, it)
                split.next = G.u + 3 * (FT - 1)
                split.upto(G.u + 3 * FT - 2)
                gate(FT - 1)
                split.upto(G.u + 3 * FT - 1)
                high(FT - 1)
                split.upto(G.u + 3 * FT + 1)

            def mix1(part, l):
                squares(0)
                xsp_highs(part, "xT", pr1[:, l, P_MIX:P_MIX + 8])
                G = Group(part, "tt")
                for q in range(16):
                    split.upto(G.u + q + 2)
                    G.ready_unit(act, q)
                    src = G.bank(q)[:, 0:T]
                    if q < 4:
                        G.free(act.activation(mqk[:, q, :], src, ACT.Copy, scale=0.125 if q < 2 else 1.0), q)
                    else:
                        G.free(act.activation(cin[:, q - 4, 3:3 + T], src, ACT.Copy), q)
                G = Group(part, "tok")
                for q in range(8):
                    g, b = divmod(q, 2)
                    split.upto(G.u + 4 * g + 5)
                    G.ready_unit(act, 4 * g + 3)
                    o = G.bank(q)
                    if g == 0:
                        act.activation(vaug[:, b, :, 0:64], o[:, 0:256].rearrange("p (h d) -> p h d", h=4), ACT.Copy)
                        G.free(act.activation(tok[:, b, 0:256], o[:, 256:512], ACT.Sigmoid), q)
                    elif g == 1:
                        G.free(act.activation(tok[:, b, 256:768], o[:, :], ACT.Copy), q)
                    elif g == 2:
                        act.activation(tok[:, b, 768:1024], o[:, 0:256], ACT.Copy)
                        G.free(act.activation(tok[:, b, 1024:1280], o[:, 256:512], ACT.Silu), q)
                    else:
                        G.free(act.activation(tok[:, b, 1280:1792], o[:, :], ACT.Silu), q)
                for m in range(3):
                    act.wait_ge(ev("conv_done"), 12 * l + 4 * m + 4)
                    act.activation(cT[:, 4 * m:4 * m + 4, :], cT[:, 4 * m:4 * m + 4, :], ACT.Silu)\
                       .then_inc(ev("conv_silu"), 1)
                act.wait_ge(ev("conv_silu"), 3 * l + 2)
                act.activation(gsq, cT[:, 0:8, :], ACT.Square).then_inc(ev("gsq_ready"), 1)
                act.wait_ge(ev("gate_abs"), l + 1)
                step(act.activation(lsg[:, 1], lsg[:, 0], ACT.Exp))
                act.activation(nea, pr1[:, l, P_ALOG:P_ALOG + 4], ACT.Exp)
                act.activation(lsg[:, 2], lsg[:, 1], ACT.Ln, bias=1.0).then_inc(ev("gate_ln"), 1)
                act.activation(pk[:, :, 8:12], g16[:, :, 12:16], ACT.Sigmoid).then_inc(ev("beta_ready"), 1)
                act.wait_ge(ev("gcols_ready"), l + 1)
                act.activation(eg, cs[:, :, 4:8], ACT.Exp).then_inc(ev("egel_ready"), 1)
                act.activation(el, el, ACT.Exp).then_inc(ev("egel_ready"), 1)
                act.wait_ge(ev("mm_ready"), l + 1)
                act.activation(guard, guard, ACT.Exp, scale=-1.0).then_inc(ev("guard_ready"), 1)
                G = Group(part, "bM")
                for q in range(2):
                    G.freed(act, q)
                    act.activation(ew[:, 2 * q:2 * q + 2, :], ew[:, 2 * q:2 * q + 2, :], ACT.Exp, scale=-1.0)\
                       .then_inc(ev("ew_ready"), 1)
                G = Group(part, "rtr")
                for q in range(4):
                    G.ready(act, q)
                    G.free(act.activation(rT[:, q, :], G.bank(q)[:, 0:T], ACT.Copy), q)
                G = Group(part, "gss")
                for q in range(4):
                    G.ready(act, q)
                    if q >= 2:
                        act.wait_ge(ev("qkn_ready"), 4 * l + q - 1)
                    G.free(act.activation(rn[:, q % 2, :], G.bank(q)[:, :], ACT.Sqrt, bias=eps1), q)
                G = Group(part, "gtr")
                for i in range(4):
                    G.ready(act, i)
                    act.activation(kt[:, i].rearrange("p b d -> p (b d)"), G.bank(i)[:, 0:256], ACT.Copy)
                    G.free(act.activation(vt[:, i].rearrange("p b d -> p (b d)"), G.bank(i)[:, 256:512], ACT.Copy), i)
                G = Group(part, "bg")
                for q in range(2):
                    G.ready(act, q)
                    for i in range(2):
                        act.activation(egb[:, 2 * q + i, :], G.bank(q)[:, T * i + 128:T * i + 256], ACT.Exp)\
                           .then_inc(ev("egb_ready"), 1)
                for q in range(2):
                    G.freed(act, q)
                    act.activation(dec[:, 2 * q:2 * q + 2], dec[:, 2 * q:2 * q + 2], ACT.Exp)\
                       .then_inc(ev("dec_exp"), 1)
                G = Group(part, "inv")
                for n in range(LEVELS):
                    for half in range(2):
                        job = 6 * n + half
                        G.ready(act, job)
                        G.free(act.activation(XI[:, 4 * half:4 * half + 4, :].rearrange("p a t -> p (a t)"),
                                              G.bank(job)[:, :], ACT.Copy), job)
                G = Group(part, "gout")
                for job, dst, scale in ((0, u0, 1.0), (2, wT, -1.0), (3, S1, 1.0)):
                    G.ready(act, job)
                    G.free(act.activation(dst.rearrange("p h t -> p (h t)"), G.bank(job)[:, :], ACT.Copy, scale=scale), job)
                xsp_highs(part, "yT", pr1[:, l, P_Y:P_Y + 8])
                split.upto(Group(part, "wout").u + DC + 1)

            def mix2(part, l):
                xsp_highs(part, "xT", None)
                G = Group(part, "tt")
                for q in range(4):
                    split.upto(G.u + q + 2)
                    G.ready_unit(act, q)
                    G.free(act.activation(qkT[:, q, :], G.bank(q)[:, 0:T], ACT.Copy, scale=0.125 if q < 2 else 1.0), q)
                G = Group(part, "tok")
                for q in range(8):
                    g, b = divmod(q, 2)
                    split.upto(G.u + 4 * g + 5)
                    G.ready_unit(act, 4 * g + 3)
                    func = (ACT.Copy, ACT.Silu, ACT.Gelu, ACT.Gelu)[g]
                    G.free(act.activation(tok2[:, b, 512 * g:512 * g + 512], G.bank(q)[:, :], func), q)
                G = Group(part, "small")
                G.ready(act, 0)
                G.free(act.activation(aT[0:16, :], G.bank(0)[0:16, 0:T], ACT.Copy), 0)
                act.wait_ge(ev("zabs_ready"), l + 1)
                step(act.activation(dff, dff, ACT.Exp))
                act.activation(lg, dff, ACT.Ln, bias=1.0).then_inc(ev("lg_ln"), 1)
                for m in range(LEVELS + 1):
                    act.wait_ge(ev("dabs_ready"), (LEVELS + 1) * l + m + 1)
                    act.activation(lv_e, dff, ACT.Exp, scale=-1.0 / 16.0).then_inc(ev("lv_exp"), 1)
                xsp_highs(part, "yT", yg[:, l, :])
                split.upto(Group(part, "wout").u + DC + 1)

            def peer(part, l):
                xsp_highs(part, "xT", None)
                G = Group(part, "tt")
                for q in range(16):
                    split.upto(G.u + q + 2)
                    G.ready_unit(act, q)
                    G.free(act.activation(qT[:, q, :], G.bank(q)[:, 0:T], ACT.Copy), q)
                G = Group(part, "score")
                split.upto(G.u + 2)
                act.wait_ge(h_saved, 16 * (l + 1))
                for q in range(4):
                    G.ready(act, q)
                    G.free(act.activation(sc1[:, 512 * q:512 * q + 512], G.bank(q)[:, :], ACT.Copy), q)
                G = Group(part, "U")
                with act.Fori(0, NKEYS // UNITS_BODY) as it:
                    for q in range(UNITS_BODY):
                        split.one(G.u + q + 3, it, UNITS_BODY)
                        G.ready_unit(act, q, it * UNITS_BODY)
                        G.free(act.activation(arena[:, bass.ds(it * (UNITS_BODY * T) + q * T, T)],
                                              G.bank(q)[:, 0:T], ACT.Gelu), q)
                split.next = G.u + NKEYS // UNITS_BODY * UNITS_BODY + 3
                for q in range(NKEYS // UNITS_BODY * UNITS_BODY, NKEYS):
                    split.upto(G.u + q + 3)
                    G.ready_unit(act, q)
                    G.free(act.activation(A[:, q, :], G.bank(q)[:, 0:T], ACT.Gelu), q)
                for b in range(NB):
                    act.wait_ge(ev("smx_ready"), NB * l + b + 1)
                    act.activation(selv[:, b, 2, :], selv[:, b, 2, :], ACT.Exp).then_inc(ev("smx_exp"), 1)
                for b in range(NB):
                    Group(part, "selT").freed(act, b)
                with act.Fori(0, 16) as it:
                    for g in range(4):
                        act.wait_ge(oh_equal, it * 4 + (64 * l + g + 1))
                        for t in range(4):
                            ins = act.activation(oh[:, g, 1, t, :], oh[:, g, 1, t, :], ACT.Copy,
                                                 scale=selT[:, 2, bass.ds(it * 16 + (4 * g + t), 1)])
                        ins.then_inc(oh_done, 1)
                act.wait_ge(g_freed, l + 1)
                G = Group(part, "V")

                def stage(j, it=0):
                    if j >= 2:
                        G.ready_unit(act, j - 2, it * 6)
                    act.activation(hsp[:, j % 2, 0, :], arena[:, bass.ds(it * (6 * T) + j * T, T)], ACT.Copy)\
                       .then_inc(act_high, 1)

                for n in range(3):
                    split.one(G.u + n)
                stage(0)
                stage(1)
                with act.Fori(0, 20) as it:
                    for j in range(2, 8):
                        stage(j, it)
                        split.one(G.u + j + 1, it)
                split.next = G.u + 123
                for j in range(122, 128):
                    stage(j)
                    split.upto(G.u + j + 1)
                split.upto(G.u + 129)

            yg = pr2[:, :, Q_GAIN:Q_GAIN + 8]
            split.upto(2)
            act.wait_ge(const_in, 80)
            act.wait_ge(x_in, 16)
            for l in range(DEPTH):
                if l:
                    h_added(act, f"ffn2{l - 1}")
                ffn(f"ffn1{l}", l, P_FFN1)
                h_added(act, f"ffn1{l}")
                mix1(f"mix1{l}", l)
                h_added(act, f"mix1{l}")
                ffn(f"ffn2{l}", l, P_FFN2)
            h_added(act, f"ffn2{DEPTH - 1}")
            squares(0)
            for l in range(DEPTH):
                mix2(f"mix2{l}", l)
                peer(f"peer{l}", l)

        @block.vector
        def _(dve):
            step = Chain(dve, dve_step)
            ts, tt, stt = dve.tensor_scalar, dve.tensor_tensor, dve.scalar_tensor_tensor

            split = Splitter(dve, False)
            lows = [0]

            def xsp_lows(part, name, gain):
                G = Group(part, name)
                for c in range(DC):
                    lows[0] += 1
                    dve.wait_ge(xsp_high, lows[0])
                    G.free(stt(xsp[:, 1, c, :], G.bank(c)[:, 0:T], 1.0 if gain is None else gain[:, c:c + 1],
                               xsp[:, 0, c, :].bitcast(F32), ALU.mult, ALU.subtract), c)

            norms = [0]
            asked = [0]

            def rsqrt(ins):
                ins.then_inc(ev("square_ready"), 1)
                asked[0] += 1
                dve.wait_ge(ev("rsqrt_ready"), asked[0])


            def rms_scale():
                norms[0] += 1
                dve.wait_ge(ev("sumsq"), NB * norms[0])
                rsqrt(ts(st[:, 2:4], st[:, 0:2], 1.0 / D, EPS1, ALU.mult, ALU.add))

            def rms(part, gain):
                rms_scale()
                for b in range(NB):
                    ins = ts(xs[:, b, :], h[:, b, :], st[:, 2 + b:3 + b], None, ALU.mult)
                ins.then_inc(ev("xs_ready"), 1)
                xsp_lows(part, "xT", gain)

            def add_to_h(part, last, scale_acc, scale_h):
                G, i = last
                G.ready_unit(dve, i)
                for b in range(NB):
                    for n in range(2):
                        hs = h[:, b, 512 * n:512 * n + 512]
                        if scale_h == 1.0:
                            ins = stt(hs, ACC[2 * b + n][:, :], scale_acc, hs, ALU.mult, ALU.add)
                        else:
                            ins = stt(hs, hs, scale_h, ACC[2 * b + n][:, :], ALU.mult, ALU.add)
                ins.then_inc(acc_free, 1)
                h_added(dve, part)

            def ffn(part, l, gain, tiles):
                rms(part, pr1[:, l, gain:gain + 8])
                G = Group(part, "ffn")

                def up(t, it=0):
                    G.ready_unit(dve, 3 * t if t else 1, 6 * it)
                    G.freed(dve, 2 * t, it)
                    if tiles + t >= 2:
                        dve.wait_ge(act_low, tiles + t - 1 + 2 * it)
                    G.free(tt(prod[:, t % 2, :], G.bank(2 * t + 1)[:, 0:T], sil[:, t % 2, :], ALU.mult), 2 * t + 1)

                def low(t, it=0):
                    G.freed(dve, 2 * t + 1, it)
                    dve.wait_ge(act_high, tiles + t + 1 + 2 * it)
                    tt(hsp[:, t % 2, 1, :], prod[:, t % 2, :], hsp[:, t % 2, 0, :].bitcast(F32), ALU.subtract)\
                        .then_inc(act_low, 1)

                for t in range(3):
                    split.upto(G.u + (3 * t + 2 if t else 3))
                    up(t)
                    low(t)
                with dve.Fori(0, (FT - 4) // 2) as it:
                    for t in (3, 4):
                        for n in range(3):
                            split.one(G.u + 3 * t + n, it)
                        up(t, it)
                        low(t, it)
                split.next = G.u + 3 * (FT - 1)
                split.upto(G.u + 3 * FT - 1)
                up(FT - 1)
                low(FT - 1)
                split.upto(G.u + 3 * FT + 1)
                add_to_h(part, (G, 3 * FT - 1), 0.5, 1.0)

            def head_norm(src, n, d, eps, dst, gate, buf, sqb, ss, src_free=None):
                w = buf[:, 0:n * d].rearrange("p (h d) -> p h d", h=n)
                if src is not None:
                    ins = dve.tensor_copy(w, src)
                    if src_free is not None:
                        src_free[0].free(ins, src_free[1])
                        src_free[0].freed(dve, src_free[1])
                    else:
                        step(ins)
                s = sqb[:, 0:n * d].rearrange("p (h d) -> p h d", h=n)
                step(tt(s, w, w, ALU.mult))
                step(dve.tensor_reduce(ss[:, 0:n], s, AX_X, ALU.add))
                rsqrt(ts(ss[:, 0:n], ss[:, 0:n], 1.0 / d, eps, ALU.mult, ALU.add))
                step(tt(w, w, ss[:, 0:n].unsqueeze(2).broadcast_to([P, n, d]), ALU.mult))
                return tt(dst.rearrange("p (h d) -> p h d", h=n), w, gate.rearrange("p (h d) -> p h d", h=n), ALU.mult)

            def mix1(part, l):
                rms(part, pr1[:, l, P_MIX:P_MIX + 8])
                dve.memset(cin[:, :, 0:3], 0.0)
                step(dve.memset(vaug[:, :, :, 64:65], 1.0))
                G = Group(part, "tt")
                for q in range(12):
                    split.upto(G.u + q + 6)
                    G.freed(dve, q + 4)
                    for tap in range(4):
                        w = pr1[:, l, P_CONV + 4 * q + tap:P_CONV + 4 * q + tap + 1]
                        src = cin[:, q, tap:tap + T]
                        if tap == 0:
                            step(ts(cT[:, q, :], src, w, None, ALU.mult))
                        elif tap < 3:
                            step(stt(cT[:, q, :], src, w, cT[:, q, :], ALU.mult, ALU.add))
                        else:
                            stt(cT[:, q, :], src, w, cT[:, q, :], ALU.mult, ALU.add).then_inc(ev("conv_done"), 1)
                split.upto(Group(part, "tok").u + 17)
                G = Group(part, "small")
                G.ready(dve, 0)
                o = G.bank(0)[:, 0:32].rearrange("p (b n) -> p b n", b=NB)
                tt(g16[:, :, 0:12], o[:, :, 0:12],
                   pr1[:, l, P_BIAS:P_BIAS + 12].unsqueeze(1).broadcast_to([P, NB, 12]), ALU.add)
                G.free(dve.tensor_copy(g16[:, :, 12:16], o[:, :, 12:16]), 0)
                G.freed(dve, 0)
                stt(lsg[:, 0], g16[:, :, 4:12], -1.0, g16[:, :, 4:12], ALU.mult, ALU.min).then_inc(ev("gate_abs"), 1)
                dve.wait_ge(ev("gate_ln"), l + 1)
                stt(cg[:, :, 0:4], g16[:, :, 4:8], 0.0, lsg[:, 2, :, 0:4], ALU.min, ALU.subtract)
                step(stt(cg[:, :, 4:8], g16[:, :, 8:12], 0.0, lsg[:, 2, :, 4:8], ALU.max, ALU.add))
                stt(cg[:, :, 4:8], cg[:, :, 4:8], -1.0, nea.unsqueeze(1).broadcast_to([P, NB, 4]), ALU.mult, ALU.mult)\
                    .then_inc(ev("cg_ready"), 1)
                G = Group(part, "cums")
                G.ready(dve, 0)
                dve.tensor_copy(cs, G.bank(0)[:, 0:16].rearrange("p (b n) -> p b n", b=NB))
                G.free(dve.tensor_copy(gl, G.bank(0)[:, 16:24].rearrange("p (b n) -> p b n", b=NB)), 0)
                G.freed(dve, 0)
                tt(el, gl, cs[:, :, 4:8], ALU.subtract).then_inc(ev("gcols_ready"), 1)
                tt(pk[:, :, 0:4], g16[:, :, 0:4], cs[:, :, 0:4], ALU.subtract)
                dve.wait_ge(ev("beta_ready"), l + 1)
                dve.tensor_copy(pk[:, :, 4:8], cs[:, :, 4:8]).then_inc(ev("pk_ready"), 1)
                G = Group(part, "rows")
                G.ready(dve, 0)
                G.free(dve.tensor_copy(rows12[0:12, :], G.bank(0)[0:12, 0:T]), 0)
                G.freed(dve, 0)
                dve.tensor_tensor_scan(mrow[0:4, :], rows12[0:4, :], rows12[0:4, :], 0.0, ALU.max, ALU.max)\
                   .then_inc(ev("mrow_ready"), 1)
                G = Group(part, "mcols")
                G.ready(dve, 0)
                G.free(tt(guard, cs[:, :, 0:4], G.bank(0)[:, 0:8].rearrange("p (b n) -> p b n", b=NB), ALU.add), 0)
                G.freed(dve, 0)
                dve.tensor_copy(guard, guard).then_inc(ev("mm_ready"), 1)
                dve.wait_ge(ev("pk_ready"), l + 1)
                G = Group(part, "bM")
                for q in range(2):
                    G.ready(dve, q)
                    for i in range(2):
                        a = 2 * q + i
                        ts(ew[:, a, 0:256], G.bank(q)[:, T * i:T * i + T], pk[:, 0, a:a + 1], 0.0,
                           ALU.subtract, ALU.max)
                        ins = ts(ew[:, a, 256:384], G.bank(q)[:, T * i + 128:T * i + T], pk[:, 1, a:a + 1], 0.0,
                                 ALU.subtract, ALU.max)
                    G.free(ins, q)
                dve.wait_ge(ev("ew_ready"), 2 * l + 2)
                tri4 = tri.unsqueeze(1).broadcast_to([P, 4, P])
                tt(ew[:, :, 0:128], ew[:, :, 0:128], tri4, ALU.mult)
                step(tt(ew[:, :, 256:384], ew[:, :, 256:384], tri4, ALU.mult))
                G = Group(part, "msc")
                for i in range(4):
                    G.ready(dve, i)
                    G.free(tt(pm[:, i, :], G.bank(i)[:, 0:384], ew[:, i, :], ALU.mult), i)
                G = Group(part, "mout")
                dve.wait_ge(ev("guard_ready"), l + 1)
                for b in range(NB):
                    G.ready(dve, b)
                    o = G.bank(b)[:, 0:260].rearrange("p (h d) -> p h d", h=4)
                    den = o[:, :, 64:65].rearrange("p h d -> p (h d)")
                    step(tt(rden, den, guard[:, b, :], ALU.max))
                    step(stt(rden, den, -1.0, rden, ALU.mult, ALU.max))
                    step(dve.reciprocal(rden, rden))
                    G.free(tt(hh[:, 0:256].rearrange("p (h d) -> p h d", h=4), o[:, :, 0:64],
                              rden.unsqueeze(2).broadcast_to([P, 4, 64]), ALU.mult), b)
                    G.freed(dve, b)
                    step(head_norm(None, 4, 64, EPS1, y[:, b, 0:256], tok[:, b, 0:256], hh, sq, ssq))
                G = Group(part, "rsc")
                for i in range(4):
                    G.ready(dve, i)
                    dc = C_RET + 256 * i
                    tt(rp[:, i, 0:256], G.bank(i)[:, 0:256], cst1[:, dc:dc + 256], ALU.mult)
                    G.free(tt(rp[:, i, 256:384], G.bank(i)[:, 256:384], cst1[:, dc:dc + 128], ALU.mult), i)
                G = Group(part, "rout")
                for b in range(NB):
                    G.ready(dve, b)
                    step(head_norm(G.bank(b)[:, 0:256].rearrange("p (h d) -> p h d", h=4), 4, 64, EPS1,
                                   y[:, b, 256:512], tok[:, b, 1024:1280], hh, sq, ssq, (G, b)))
                dve.wait_ge(ev("conv_silu"), 3 * l + 3)
                G = Group(part, "gss")
                for q in range(4):
                    G.freed(dve, q)
                    step(dve.reciprocal(rn[:, q % 2, :], rn[:, q % 2, :]))
                    c2 = cT[:, 2 * q:2 * q + 2, :].rearrange("p a t -> p (a t)")
                    stt(c2, c2, 128.0 ** -0.5 if q < 2 else 1.0, rn[:, q % 2, :], ALU.mult, ALU.mult)\
                        .then_inc(ev("qkn_ready"), 1)
                    dve.wait_ge(ev("qkn_ready"), 4 * l + q + 1)
                G = Group(part, "bg")
                for q in range(2):
                    G.ready(dve, q)
                    dve.wait_ge(ev("egb_ready"), 4 * l + 2 * q + 2)
                    for i in range(2):
                        for b in range(NB):
                            a = 2 * q + i
                            ins = ts(dec[:, a, b, :], G.bank(q)[:, T * i + 128 * b:T * i + 128 * b + 128],
                                     pk[:, b, 4 + a:5 + a], 0.0, ALU.subtract, ALU.min)
                    G.free(ins, q)
                dve.wait_ge(ev("dec_ready"), l + 1)
                G = Group(part, "bb")
                for q in range(2):
                    G.ready(dve, q)
                    G.free(tt(NT[:, 2 * q:2 * q + 2].rearrange("p h b t -> p (h b t)"),
                              dec[:, 2 * q:2 * q + 2].rearrange("p h b t -> p (h b t)"), G.bank(q)[:, :], ALU.mult), q)
                    G.freed(dve, q)
                G = Group(part, "gkk")
                for i in range(4):
                    G.ready(dve, i)
                    n2 = NT[:, i].rearrange("p b t -> p (b t)")
                    tt(n2, n2, G.bank(i)[:, 0:256], ALU.mult)
                    G.free(tt(QK[:, i].rearrange("p b t -> p (b t)"), dec[:, i].rearrange("p b t -> p (b t)"),
                              G.bank(i)[:, 256:512], ALU.mult), i)
                G = Group(part, "inv")
                dve.wait_ge(ev("EL_ready"), LEVELS * l + 1)
                for n in range(LEVELS):
                    for q, buf in ((1, TI), (2, WI)):
                        for half in range(2):
                            job = 6 * n + 2 * q + half
                            G.ready(dve, job)
                            if n:
                                G.freed(dve, job - 6)
                            b2 = buf[:, 4 * half:4 * half + 4, :].rearrange("p a t -> p (a t)")
                            G.free(tt(b2, b2, G.bank(job)[:, :], ALU.subtract), job)
                G = Group(part, "gout")
                G.ready(dve, 1)
                G.free(dve.tensor_copy(uv1.rearrange("p h t -> p (h t)"), G.bank(1)[:, :]), 1)
                G.freed(dve, 1)
                G.ready(dve, 4)
                G.free(tt(u1.rearrange("p h t -> p (h t)"), uv1.rearrange("p h t -> p (h t)"), G.bank(4)[:, :], ALU.add), 4)
                for b in range(NB):
                    G.ready(dve, 5 + b)
                    ins = head_norm(G.bank(5 + b)[:, :].rearrange("p (h d) -> p h d", h=4), 4, 128, EPS1,
                                    y[:, b, 512:1024], tok[:, b, 1280:1792], hh, sq, ssq, (G, 5 + b))
                    if b == 0:
                        step(ins)
                ins.then_inc(ev("y_ready"), 1)
                xsp_lows(part, "yT", pr1[:, l, P_Y:P_Y + 8])
                split.upto(Group(part, "wout").u + DC + 1)
                add_to_h(part, (Group(part, "wout"), DC - 1), 1.0, 1.0)

            def layer_norm(n):
                dve.wait_ge(rows_in, 32 * (n + 1))
                for b in range(NB):
                    hb = h[:, b, :]
                    for m in range(2):
                        ins = dve.bn_stats(st[:, 6 * m:6 * m + 6], h[:, b, 512 * m:512 * m + 512])
                    step(ins)
                    step(dve.bn_aggr(st[:, 12:14], st[:, 0:12].rearrange("p (m s) -> p m s", m=2)))
                    rsqrt(ts(st[:, 14:15], st[:, 13:14], EPS2, None, ALU.add))
                    step(ts(hb, hb, st[:, 12:13], st[:, 14:15], ALU.subtract, ALU.mult))
                    step(tt(hb, hb, rows[:, 0:1024], ALU.mult))
                    ins = tt(hb, hb, rows[:, 1024:2048], ALU.add)
                    if b == 0:
                        step(ins)
                step(ins)
                dve.memset(st[:, 31:32], 0.0).then_inc(rows_free, 1)
                dve.memset(st[:, 30:31], 0.0).then_inc(ev("ln_ready" if n < 3 * DEPTH else "out_ready"), 1)

            def mix2(part, l):
                xsp_lows(part, "xT", None)
                split.upto(Group(part, "tok").u + 17)
                G = Group(part, "logg")
                G.ready(dve, 0)
                for m in range(2):
                    ins = ts(zg[:, m, :], G.bank(0)[:, T * m:T * m + T], pr2[:, l, Q_BG + m:Q_BG + m + 1], None, ALU.add)
                G.free(ins, 0)
                G.freed(dve, 0)
                stt(dff, zg, -1.0, zg, ALU.mult, ALU.min).then_inc(ev("zabs_ready"), 1)
                step(ts(zg, zg, 0.0, None, ALU.min))
                dve.wait_ge(ev("lg_ln"), l + 1)
                for m in range(2):
                    ins = dve.tensor_tensor_scan(bc[:, m, :], zg[:, m, :], lg[:, m, :], 0.0, ALU.add, ALU.subtract)
                step(ins)
                tt4 = Group(part, "tt")
                for q in range(4):
                    tt4.freed(dve, q)
                G = Group(part, "lvl")
                lm = [lvl(n).unsqueeze(1).broadcast_to([P, 4, P]) for n in range(LEVELS)] + \
                     [ident.unsqueeze(1).broadcast_to([P, 4, P])]

                def level(m):
                    s = 1 << m
                    n = m if m < LEVELS else LEVELS + 1
                    if m:
                        dve.wait_ge(ev("lv_exp"), (LEVELS + 1) * l + m)
                    b4 = bc.rearrange("p m (k s) -> p (m k) s", s=2 * s)
                    step(tt(dff.rearrange("p m (k s) -> p (m k) s", s=2 * s), b4,
                            b4[:, :, s - 1:s].broadcast_to([P, T // s, 2 * s]), ALU.subtract))
                    stt(dff, dff, -1.0, dff, ALU.mult, ALU.max).then_inc(ev("dabs_ready"), 1)
                    if n >= 2:
                        G.ready(dve, 2 * (n - 2) + 1 if n <= LEVELS else 2 * LEVELS - 1)
                    dve.wait_ge(ev("lv_exp"), (LEVELS + 1) * l + m + 1)
                    tt(lv_q[:, n % 2], qkT[:, 0:2, :], lv_e, ALU.mult)
                    tt(lv_k[:, n % 2], qkT[:, 2:4, :], lv_e, ALU.mult).then_inc(ev("lv_ready"), 1)

                def gather(n):
                    for b in range(NB):
                        job = 2 * n + b
                        G.ready(dve, job)
                        o = G.bank(job)[:, :].rearrange("p (h t) -> p h t", h=4)
                        if n == 0:
                            G.free(tt(at_[:, b], o, lm[0], ALU.mult), job)
                            G.freed(dve, job)
                        else:
                            t3 = lvt.rearrange("p (h t) -> p h t", h=4)
                            G.free(tt(t3, o, lm[n], ALU.mult), job)
                            G.freed(dve, job)
                            step(tt(at_[:, b], at_[:, b], t3, ALU.add))

                level(0)
                for m in range(1, LEVELS + 1):
                    level(m)
                    gather(m - 1)
                gather(LEVELS)
                dve.tensor_copy(st[:, 29:30], ident[:, 0:1]).then_inc(ev("at_ready"), 1)
                for odd in range(2):
                    job = 2 * LEVELS + 2 + odd
                    G.ready(dve, job)
                    G.free(dve.tensor_copy(off[:, 2 * odd:2 * odd + 2, :].rearrange("p h t -> p (h t)"),
                                           G.bank(job)[:, 0:256]), job)
                K = Group(part, "tok")
                for q in range(4, 8):
                    K.freed(dve, q)
                dve.wait_ge(rows_in, 32 * (3 * l + 2))
                for b in range(NB):
                    v = tok2[:, b, 1536:2048]
                    step(dve.bn_stats(bst, v))
                    step(dve.bn_aggr(bag, bst))
                    rsqrt(ts(bag[:, 1:2], bag[:, 1:2], EPS2, None, ALU.add))
                    step(ts(v, v, bag[:, 0:1], bag[:, 1:2], ALU.subtract, ALU.mult))
                    step(tt(v, v, rows[:, 0:512], ALU.mult))
                    step(tt(v, v, rows[:, 1024:1536], ALU.add))
                dve.memset(st[:, 31:32], 0.0).then_inc(rows_free, 1)
                dve.wait_ge(side_in, 16 + 64 * (l + 1))
                dve.memset(swt_sb[64:128, :, 0:64], 0.0).then_inc(ev("sgv_ready"), 1)
                G = Group(part, "gla")
                for b in range(NB):
                    G.ready(dve, b)
                    step(head_norm(G.bank(b)[:, :].rearrange("p (h d) -> p h d", h=4), 4, 128, EPS2,
                                   y[:, b, 0:512], tok2[:, b, 512:1024], hh2, sq2, ssq2, (G, b)))
                G = Group(part, "sgu")
                for b in range(NB):
                    G.ready(dve, b)
                    for i in range(4):
                        c = slice(128 * i, 128 * i + 128)
                        ins = stt(y[:, b, 512 + 128 * i:640 + 128 * i], G.bank(b)[:, c], pr2[:, l, Q_SB + i:Q_SB + i + 1],
                                  tok2[:, b, 1024 + 128 * i:1152 + 128 * i], ALU.add, ALU.mult)
                    G.free(ins, b)
                    G.freed(dve, b)
                dve.memset(st[:, 30:31], 0.0).then_inc(ev("y_ready"), 1)
                xsp_lows(part, "yT", yg[:, l, :])
                split.upto(Group(part, "wout").u + DC + 1)
                add_to_h(part, (Group(part, "wout"), DC - 1), 1.0, ALPHA)
                layer_norm(3 * l + 2)

            def top16(vals, idx, src, tmp):
                step(dve.max(vals[:, 0:8], src))
                step(dve.max_index(idx[:, 0:8], vals[:, 0:8], src))
                step(dve.match_replace(tmp, vals[:, 0:8], src, LOWEST))
                split.upto(split.next)
                step(dve.max(vals[:, 8:16], tmp))
                step(dve.max_index(idx[:, 8:16], vals[:, 8:16], tmp))
                split.upto(split.next)

            def peer(part, l):
                xsp_lows(part, "xT", None)
                U = Group(part, "U")
                split.upto(U.u + 2)
                for q in range(4):
                    Group(part, "score").freed(dve, q)
                for b in range(NB):
                    for i in range(PH):
                        for m in range(2):
                            c = 128 * m
                            src = ACC[i // 2][:, 256 * (i % 2) + c:256 * (i % 2) + c + 128] if b == 0 \
                                else sc1[:, 256 * i + c:256 * i + c + 128]
                            top16(topv[:, 2 * i + m, :], topi[:, 2 * i + m, :], src, cand[:, 0:128])
                        c3 = cand.rearrange("p (a c) -> p a c", a=TOPK)
                        step(tt(c3, topv[:, 2 * i, :].unsqueeze(2).broadcast_to([P, TOPK, TOPK]),
                                topv[:, 2 * i + 1, :].unsqueeze(1).broadcast_to([P, TOPK, TOPK]), ALU.add))
                        top16(selv[:, b, 2, 16 * i:16 * i + 16], posi[:, i, :], cand, cand2)
                    if b == 0:
                        dve.memset(st[:, 31:32], 0.0).then_inc(acc_free, 1)
                    else:
                        dve.memset(st[:, 31:32], 0.0).then_inc(ev("scores_read"), 1)
                    step(dve.tensor_copy(topf, topi))
                    step(ts(posa, posi, 4, None, ALU.logical_shift_right))
                    step(ts(posi, posi, 15, None, ALU.bitwise_and))
                    step(dve.tensor_copy(pfa, posa))
                    step(dve.tensor_copy(pfb, posi))
                    io16 = iota[:, 0:TOPK].unsqueeze(1).broadcast_to([P, TOPK, TOPK])
                    c3 = cand.rearrange("p (a c) -> p a c", a=TOPK)
                    for i in range(PH):
                        for m, place in ((0, pfa), (1, pfb)):
                            step(tt(c3, place[:, i, :].unsqueeze(2).broadcast_to([P, TOPK, TOPK]), io16, ALU.is_equal))
                            step(tt(c3, c3, topf[:, 2 * i + m, :].unsqueeze(1).broadcast_to([P, TOPK, TOPK]), ALU.mult))
                            step(dve.tensor_reduce(selv[:, b, m, 16 * i:16 * i + 16], c3, AX_X, ALU.add))
                            split.upto(split.next)
                    g3 = selv[:, b, 2, :].rearrange("p (h k) -> p h k", h=PH)
                    step(dve.tensor_copy(gmx[:, 0:PH], g3[:, :, 0:1].rearrange("p h k -> p (h k)")))
                    tt(g3, g3, gmx[:, 0:PH].unsqueeze(2).broadcast_to([P, PH, TOPK]), ALU.subtract)\
                        .then_inc(ev("smx_ready"), 1)
                    dve.wait_ge(ev("smx_ready"), NB * l + b + 1)
                split.upto(U.u + NKEYS - 1)
                for b in range(NB):
                    g3 = selv[:, b, 2, :].rearrange("p (h k) -> p h k", h=PH)
                    dve.wait_ge(ev("smx_exp"), NB * l + b + 1)
                    step(dve.tensor_reduce(gmx[:, 0:PH], g3, AX_X, ALU.add))
                    step(dve.reciprocal(gmx[:, 0:PH], gmx[:, 0:PH]))
                    tt(g3, g3, gmx[:, 0:PH].unsqueeze(2).broadcast_to([P, PH, TOPK]), ALU.mult)\
                        .then_inc(ev("sel_ready"), 1)
                    dve.wait_ge(ev("sel_ready"), NB * l + b + 1)
                S = Group(part, "selT")
                for b in range(NB):
                    S.ready(dve, b)
                    S.free(dve.tensor_copy(selT[:, :, 128 * b:128 * b + 128],
                                           S.bank(b)[:, 0:384].rearrange("p (s t) -> p s t", s=3)), b)
                    S.freed(dve, b)
                G = Group(part, "G")
                for q in range(NKEYS - 4, NKEYS):
                    U.freed(dve, q)

                def one_hot(g, it=0):
                    dve.wait_ge(job_done, it * 4 + (G.j + g - 3))
                    tt(oh[:, g % 4], iota.unsqueeze(1).unsqueeze(1).broadcast_to([P, 2, 4, NKEYS]),
                       selT[:, 0:2, bass.ds(it * 16 + 4 * g, 4)].unsqueeze(3).broadcast_to([P, 2, 4, NKEYS]),
                       ALU.is_equal).then_inc(oh_equal, 1)

                def gate(g, it=0):
                    dve.wait_ge(job_done, it * 4 + (G.j + g + 1))
                    a3 = A[:, :, bass.ds(it * 16 + 4 * g, 4)]
                    G.free(tt(a3, a3, G.bank(g)[:, :].rearrange("p (t j) -> p j t", t=4), ALU.mult), g)

                one_hot(0)
                one_hot(1)
                with dve.Fori(0, 15) as it:
                    for g in range(4):
                        one_hot(g + 2, it)
                        gate(g, it)
                for g in range(60, 64):
                    if g < 62:
                        one_hot(g + 2)
                    gate(g)
                for q in range(4):
                    G.freed(dve, 60 + q)
                dve.memset(st[:, 31:32], 0.0).then_inc(g_freed, 1)
                V = Group(part, "V")

                def low(j, it=0):
                    dve.wait_ge(act_high, it * 6 + (TILES + NKEYS * l + j + 1))
                    tt(hsp[:, j % 2, 1, :], arena[:, bass.ds(it * (6 * T) + j * T, T)],
                       hsp[:, j % 2, 0, :].bitcast(F32), ALU.subtract).then_inc(act_low, 1)

                for n in range(3):
                    split.one(V.u + n)
                low(0)
                low(1)
                with dve.Fori(0, 20) as it:
                    for j in range(2, 8):
                        low(j, it)
                        split.one(V.u + j + 1, it)
                split.next = V.u + 123
                for j in range(122, 128):
                    low(j)
                    split.upto(V.u + j + 1)
                split.upto(V.u + 129)
                dve.wait_ge(h_back, 16 * (l + 1))
                add_to_h(part, (V, NKEYS - 1), 1.0, ALPHA)
                dve.memset(st[:, 31:32], 0.0).then_inc(side_free, 1)
                layer_norm(3 * l + 3)

            yg = pr2[:, :, Q_GAIN:Q_GAIN + 8]
            split.upto(2)
            dve.wait_ge(const_in, 80)
            dve.wait_ge(x_in, 16)
            for l in range(DEPTH):
                ffn(f"ffn1{l}", l, P_FFN1, 2 * l * FT)
                mix1(f"mix1{l}", l)
                ffn(f"ffn2{l}", l, P_FFN2, (2 * l + 1) * FT)
            rms_scale()
            dve.wait_ge(side_in, 16)
            for b in range(NB):
                ins = stt(h[:, b, :], h[:, b, :], st[:, 2 + b:3 + b], final_row, ALU.mult, ALU.mult)
            step(ins)
            dve.memset(st[:, 31:32], 0.0).then_inc(side_free, 1)
            layer_norm(0)
            for l in range(DEPTH):
                mix2(f"mix2{l}", l)
                peer(f"peer{l}", l)


def tables():
    c = np.zeros((P, C_N), np.float32)
    i = np.arange(P)
    c[:, C_ID:C_ID + 128] = np.eye(P)
    c[:, C_TRI:C_TRI + 128] = i[:, None] <= i[None, :]
    c[:, C_ONE:C_ONE + 128] = 1.0
    masks = np.zeros((LEVELS, P, P), np.float32)
    for n in range(LEVELS):
        s = 1 << n
        m = (i[:, None] // (2 * s) == i[None, :] // (2 * s)) & (i[:, None] % (2 * s) < s) & (i[None, :] % (2 * s) >= s)
        masks[n] = m
    c1 = np.zeros((P, C_N1), np.float32)
    for a in range(4):
        lg = np.log1p(-np.exp2(-5.0 - a))
        for b in range(2):
            rel = i[None, :] + 128.0 * b - i[:, None]
            c1[:, C_RET + 256 * a + 128 * b:C_RET + 256 * a + 128 * b + 128] = \
                np.where(rel >= 0, np.exp(np.maximum(rel, 0) * lg), 0.0) * 0.125
    inv = (np.float32(10000.0) ** (-np.arange(0, 64, 2, dtype=np.float32) / np.float32(64))).astype(np.float32)
    for b in range(NB):
        ang = ((i + 128 * b).astype(np.float32)[:, None] * inv[None, :]).astype(np.float32).astype(np.float64)
        c1[:, C_COS + 32 * b:C_COS + 32 * b + 32] = np.cos(ang)
        c1[:, C_SIN + 32 * b:C_SIN + 32 * b + 32] = np.sin(ang)
    c[:, C_IOTA:C_IOTA + 128] = i[None, :]
    return c, c1, masks


def columns(w):
    n = w.shape[1] // 128
    return w.reshape(DC, P, n, 128).transpose(2, 1, 0, 3).reshape(n, P, 1024)


def wide_columns(w):
    n = w.shape[1] // 512
    return w.reshape(4, 2, P, n, 512).transpose(3, 0, 2, 1, 4).reshape(4 * n, P, 1024)


def lay_out(v):
    units = np.empty((UNITS, P, 1024), np.float32)
    first = {n: u for n, (_, _, u) in BASE.items()}

    def put(part, name, a, i=0, step=1):
        u = first[part, name] + i
        units[u:u + step * (len(a) - 1) + 1:step] = a

    def ffn(part, gate, up, down):
        g, u, d = columns(gate), columns(up), down.reshape(FT, P, 1024)
        put(part, "ffn", g[:1], 0)
        put(part, "ffn", u[:1], 1)
        put(part, "ffn", g[1:], 2, 3)
        put(part, "ffn", u[1:], 3, 3)
        put(part, "ffn", d[:-1], 4, 3)
        put(part, "ffn", d[-1:], 3 * FT - 1)

    off = np.cumsum([0, 256, 256, 256, 256, 4, 4, 256, 256, 256, 256, 512, 512, 512, 512, 4, 4])
    off2 = np.cumsum([0, 256, 256, 512, 512, 16, 512, 512])
    p1 = np.zeros((DEPTH, P, P_N), np.float32)
    p2 = np.zeros((DEPTH, P, Q_N), np.float32)
    wa = np.zeros((DEPTH, P, DC, 16), np.float32)
    for l in range(DEPTH):
        ffn(f"ffn1{l}", v["ffn1_w_gate"][l], v["ffn1_w_up"][l], v["ffn1_w_down"][l])
        ffn(f"ffn2{l}", v["ffn2_w_gate"][l], v["ffn2_w_up"][l], v["ffn2_w_down"][l])
        w = v["w_in"][l]
        s = [w[:, off[n]:off[n + 1]] for n in range(16)]
        put(f"mix1{l}", "tt", columns(np.concatenate([s[0], s[1], s[10], s[11], s[12]], 1)))
        put(f"mix1{l}", "tok", wide_columns(np.concatenate([s[2], s[3], s[6], s[7], s[8], s[9], s[13]], 1)))
        put(f"mix1{l}", "wout", v["w_out"][l].reshape(DC, P, D))
        for at, name in ((P_FFN1, "ffn1_norm"), (P_MIX, "mix_norm"), (P_FFN2, "ffn2_norm")):
            p1[l, :, at:at + 8] = v[name][l].reshape(DC, P).T
        gains = np.concatenate([v["m_out_norm"][l], v["r_out_norm"][l], v["g_out_norm"][l]])
        p1[l, :, P_Y:P_Y + 8] = gains.reshape(DC, P).T
        p1[l, :, P_CONV:P_CONV + 48] = v["g_conv"][l].reshape(4, 12, P).transpose(2, 1, 0).reshape(P, 48)
        p1[l, :, P_BIAS:P_BIAS + 12] = np.concatenate([v["m_i_bias"][l], v["m_f_bias"][l], v["g_dt_bias"][l]])
        p1[l, :, P_ALOG:P_ALOG + 4] = v["g_a_log"][l]
        gates = np.concatenate([s[4], s[5], s[14], s[15]], 1)
        p1[l, :, P_W16:P_W16 + 128] = gates.reshape(DC, P, 16).transpose(1, 0, 2).reshape(P, 128)

        w = v["w_in_2"][l]
        s = [w[:, off2[n]:off2[n + 1]] for n in range(7)]
        put(f"mix2{l}", "tt", columns(np.concatenate([s[0], s[1]], 1)))
        put(f"mix2{l}", "tok", wide_columns(np.concatenate([s[2], s[3], s[5], s[6]], 1)))
        put(f"mix2{l}", "wout", v["w_out_2"][l].reshape(DC, P, D))
        wa[l] = s[4].reshape(DC, P, 16).transpose(1, 0, 2)
        put(f"peer{l}", "tt", columns(v["peer_wq_2"][l]))
        u = v["peer_u_2"][l].reshape(NKEYS, NKEYS, DC, P)
        put(f"peer{l}", "U", u.transpose(1, 3, 2, 0).reshape(NKEYS, P, 1024))
        put(f"peer{l}", "V", v["peer_v_2"][l].reshape(NKEYS, NKEYS, D).transpose(1, 0, 2))
        p2[l, :, Q_GAIN:Q_GAIN + 4] = v["gla_norm_g_2"][l][:, None]
        p2[l, :, Q_GAIN + 4:Q_GAIN + 8] = 1.0
        p2[l, :, Q_BG:Q_BG + 2] = v["b_gate_2"][l].reshape(2, P).T
        p2[l, :, Q_SB:Q_SB + 4] = v["sgu_b_2"][l].T
        p2[l, :, Q_K1:Q_K1 + 128] = v["peer_k1_2"][l].T
        p2[l, :, Q_K1 + 128:Q_K1 + 256] = v["peer_k2_2"][l].T
    swt = np.ascontiguousarray(v["sgu_w_2"].transpose(0, 3, 1, 2))
    rows2 = np.stack([np.stack([v["ln_in_g_2"], v["ln_in_b_2"]])] +
                     [np.stack([v[f"ln{n}_g_2"][l], v[f"ln{n}_b_2"][l]]) for l in range(DEPTH) for n in (1, 2)])
    rows3 = np.stack([v["sgu_ln_g_2"], v["sgu_ln_b_2"]], 1)
    consts, consts1, levels = tables()
    return {
        "x": np.ascontiguousarray(v["x"][0]), "stream": units, "consts": consts, "consts1": consts1, "levels": levels, "p1": p1, "p2": p2,
        "swt": swt, "wa": wa, "wgu": np.ascontiguousarray(v["w_gate_up_2"]),
        "rows1": np.ascontiguousarray(v["final_norm"]), "rows2": rows2, "rows3": rows3,
    }


def kernel(**inputs):
    import concourse.bacc as bacc
    from concourse.bass_utils import run_bass_kernel_spmd

    arrays = lay_out({k: np.asarray(a) for k, a in inputs.items()})
    nc = bacc.Bacc("TRN2", target_bir_lowering=False, num_devices=1)
    args = [nc.dram_tensor(f"in_{n}", a.shape, F32, kind="ExternalInput").ap() for n, a in arrays.items()]
    out = nc.dram_tensor("out", (T, D), F32, kind="ExternalOutput").ap()
    build_program(nc, *args, out)
    r = run_bass_kernel_spmd(nc, [{f"in_{n}": a for n, a in arrays.items()}], core_ids=[0])
    return r.results[0]["out"].reshape(1, T, D)
```

```python
from contextlib import ExitStack

import numpy as np

import concourse.bass as bass
from concourse import mybir

F32 = mybir.dt.float32
U32 = mybir.dt.uint32
F32R = mybir.dt.float32r
ALU = mybir.AluOpType
ACT = mybir.ActivationFunctionType
AX_X = mybir.AxisListType.X

P = 128
D = 1024
T = 256
NB = T // P
DC = D // P
DEPTH = 2
D_FF = 2816
FT = D_FF // P
SBUF_BASE = 16512
RING = 3
SPLIT = 3
NKEYS = 128
TOPK = 16
PH = 8
HK = PH * TOPK
EPS1 = 1e-6
EPS2 = 1e-5
ALPHA = (2.0 * DEPTH) ** 0.25
LOWEST = -3.0e38
LEVELS = 7
UNITS_BODY = 12

C_ID, C_TRI, C_ONE, C_IOTA = 0, 128, 256, 384
C_N = C_IOTA + 128
C_RET, C_COS, C_SIN, C_N1 = 0, 1024, 1088, 1152
P_FFN1, P_MIX, P_FFN2, P_Y, P_CONV = 0, 8, 16, 24, 32
P_BIAS = P_CONV + 48
P_ALOG = P_BIAS + 12
P_W16 = P_ALOG + 4
P_N = P_W16 + 128
Q_GAIN, Q_BG, Q_SB, Q_K1 = 0, 8, 10, 14
Q_N = Q_K1 + 256

FFN_STAGES = [("xT", 8, 0), ("ffn", 2 * FT, 3 * FT)]
MIX1_STAGES = [("xT", 8, 0), ("small", 1, 0), ("tt0", 4, 4), ("cums", 1, 0), ("tt1", 4, 4), ("rows", 1, 0),
               ("tt2", 4, 4), ("mcols", 1, 0), ("tt3", 4, 4), ("tok0", 2, 4), ("tok1", 2, 4), ("gss", 4, 0),
               ("tok2", 2, 4), ("tok3", 2, 4), ("bM", 2, 0), ("msc", 4, 0), ("mout", 2, 0), ("rtr", 4, 0), ("rsc", 4, 0),
               ("rout", 2, 0), ("gtr", 4, 0), ("bg", 2, 0), ("bb", 2, 0), ("gkk", 4, 0),
               ("inv", 6 * LEVELS - 6, 0), ("gout", 7, 0), ("yT", 8, 0), ("wout", 0, 8)]
LEVEL_ORDER = [[7, 0], [1, 2], [3, 4], [5, 6, 8]]
MIX2_STAGES = [("xT", 8, 0), ("small", 1, 0), ("tt", 4, 4), ("logg", 1, 0)]
for g in range(4):
    MIX2_STAGES += [(f"tok{g}", 2, 4)] + [(f"lvl{n}", 2, 0) for n in LEVEL_ORDER[g]]
MIX2_STAGES += [("gla", 2, 0), ("sgu", 2, 0), ("yT", 8, 0), ("wout", 0, 8)]
PEER_STAGES = [("xT", 8, 0), ("tt", 16, 16), ("score", 4, 0), ("U", NKEYS, NKEYS), ("selT", 2, 0), ("G", 64, 0),
               ("V", 0, NKEYS)]


def inverse_job(n, q, half):
    return half if n == 0 else 2 + 6 * (n - 1) + 2 * (1 if n == LEVELS - 1 and q == 2 else q) + half


def plan():
    base, k, j, u = {}, 0, 0, 0
    parts = []
    for l in range(DEPTH):
        parts += [(f"ffn1{l}", FFN_STAGES), (f"mix1{l}", MIX1_STAGES), (f"ffn2{l}", FFN_STAGES)]
    for l in range(DEPTH):
        parts += [(f"mix2{l}", MIX2_STAGES), (f"peer{l}", PEER_STAGES)]
    for part, stages in parts:
        for name, jobs, units in stages:
            base[part, name] = (k, j, u)
            k, u = k + jobs, u + units
            if not units:
                j += jobs
    return base, u


BASE, UNITS = plan()
HELD = [BASE[f"peer{l}", "V"][2] for l in range(DEPTH)]


def build_program(nc, x, stream, consts, consts1, levels, p1, p2, swt, wa, wgu, rows1, rows2, rows3, out):
    ctx = ExitStack()
    with ctx:
        def sem(name):
            return ctx.enter_context(nc.semaphore(name))

        def at(name, place, shape, dt=F32):
            t = nc.alloc_sbuf_tensor_at(name, shape, dt, offset=SBUF_BASE + place)
            return t[tuple(slice(0, n) for n in shape)]

        arena = at("arena", 0, [P, NKEYS * T])
        scratch = at("scratch", 0, [P, NKEYS * T])
        place = 4 * NKEYS * T
        ring = at("ring", place, [P, RING, 1024])
        place += 4 * RING * 1024
        wsp = at("wsp", place, [P, SPLIT, 2, 1024], F32R)
        oh = at("one_hots", place, [P, 4, 2, 4, NKEYS])
        place += 4 * SPLIT * 2048
        xsp = at("xsp", place, [P, 2, DC, T], F32R)
        place += 16384
        h = at("h", place, [P, NB, D])
        sc1 = at("scores", place, [P, 2048])
        rows = at("rows_sb", place + 8192, [P, 2048])
        cst = at("cst", place + 16384, [P, C_N])
        place += 16384 + 4 * C_N
        hsp = at("hsp", place, [P, 2, 2, T], F32R)
        topv = at("topv", place, [P, 2 * PH, TOPK])
        topi = at("topi", place + 1024, [P, 2 * PH, TOPK], U32)
        topf = at("topf", place + 2048, [P, 2 * PH, TOPK])
        posi = at("posi", place + 3072, [P, PH, TOPK], U32)
        posa = at("posa", place + 3584, [P, PH, TOPK], U32)
        pfa = at("pfa", place + 4096, [P, PH, TOPK])
        pfb = at("pfb", place + 4608, [P, PH, TOPK])
        place += 5120
        pr2 = at("pr2", place, [P, DEPTH, Q_N])
        place += -(-4 * DEPTH * Q_N // 32) * 32
        st = at("st", place, [P, 32])
        moments = st[:, 24:28].rearrange("p (b s) -> p b s", b=NB)
        gmx = at("gmx", place + 128, [P, PH])
        mhalf = at("mhalf", place + 160, [P, 1])
        eps1 = at("eps1", place + 192, [P, 1])
        w16 = at("w16", place + 224, [P, 2, 128], F32R)
        assert SBUF_BASE + place + 224 + 1024 <= nc.sbuf_usable_end and SBUF_BASE >= nc.sbuf_base
        W = [ctx.enter_context(nc.psum_tensor(f"work{i}", [P, 512], F32)) for i in range(4)]
        ACC = [ctx.enter_context(nc.psum_tensor(f"acc{i}", [P, 512], F32)) for i in range(4)]

        ident = cst[:, C_ID:C_ID + 128]
        tri = cst[:, C_TRI:C_TRI + 128]
        ones = cst[:, C_ONE:C_ONE + 128]
        iota = cst[:, C_IOTA:C_IOTA + 128]

        used = [0]

        def area(*shape):
            n = int(np.prod(shape))
            a = scratch[:, used[0]:used[0] + n]
            used[0] += n
            assert used[0] <= NKEYS * T
            if len(shape) == 1:
                return a
            names = "abcd"[:len(shape)]
            return a.rearrange(f"p ({' '.join(names)}) -> p {' '.join(names)}",
                               **{m: s for m, s in zip(names, shape)})

        xs = area(NB, D)
        y = area(NB, D)
        sil = area(2, T)
        prod = area(2, T)
        masks = area(LEVELS, P)

        def lvl(n):
            return masks[:, n, :]

        mark = used[0]
        cst1 = area(C_N1)
        pr1 = area(DEPTH, P_N)
        mqk = area(4, T)
        cin = area(12, T + 4)
        cT = area(12, T)
        tok = area(NB, 1792)
        vaug = area(NB, 4, 65)
        g16 = area(NB, 16)
        lsg = area(3, NB, 8)
        nea = area(4)
        cg = area(NB, 8)
        cs = area(NB, 8)
        gl = area(NB, 4)
        pk = area(NB, 12)
        rows12 = area(T)
        mrow = area(T)
        guard = area(NB, 4)
        ew = area(4, 384)
        pm = area(4, 384)
        rden = area(4)
        hh = area(512)
        sq = area(512)
        ssq = area(NB, 4)
        rope = area(NB, 512)
        ropt = area(4, 512)
        rT = area(4, T)
        eg = area(NB, 4)
        el = area(NB, 4)
        QK = area(4, NB, P)
        qe = area(4, P)

        def over(old, pattern, start=0, **sizes):
            names = "abc"[:len(old.shape) - 1]
            n = int(np.prod(list(sizes.values())))
            flat = old.rearrange(f"p {' '.join(names)} -> p ({' '.join(names)})") if len(names) > 1 else old
            return flat[:, start:start + n].rearrange(pattern, **sizes)

        gsq = over(cin, "p (a t) -> p a t", a=8, t=T)
        vt = over(cin, "p (h b t) -> p h b t", h=4, b=NB, t=P)
        vb = over(cin, "p (h b t) -> p h b t", start=1024, h=4, b=NB, t=P)
        u1 = over(cin, "p (a t) -> p a t", start=1024, a=4, t=P)
        kd = over(cin, "p (a t) -> p a t", start=2048, a=4, t=P)
        egb = over(cin, "p (a t) -> p a t", start=2560, a=4, t=P)
        final_row = over(cin, "p (a t) -> p (a t)", a=1, t=D)
        kt = over(mqk, "p (h b t) -> p h b t", h=4, b=NB, t=P)
        kbe = over(rT, "p (h b t) -> p h b t", h=4, b=NB, t=P)
        dec = over(ew, "p (h b t) -> p h b t", h=4, b=NB, t=P)
        rp = pm
        NT = over(pm, "p (h b t) -> p h b t", h=4, b=NB, t=P)
        TI = over(xs[:, 0:1, :], "p (a t) -> p a t", a=8, t=P)
        WI = over(xs[:, 1:2, :], "p (a t) -> p a t", a=8, t=P)
        EL = over(ropt[:, 0:2, :], "p (a t) -> p a t", a=8, t=P)
        XI = over(ropt[:, 2:4, :], "p (a t) -> p a t", a=8, t=P)
        rn = over(y[:, 1:2, :], "p (a t) -> p a t", a=2, t=512)
        u0 = over(rope[:, 0:1, :], "p (a t) -> p a t", a=4, t=P)
        uv1 = over(rope[:, 1:2, :], "p (a t) -> p a t", a=4, t=P)
        wT = tok[:, 0, 256:768].rearrange("p (a t) -> p a t", a=4)
        S1 = tok[:, 1, 256:768].rearrange("p (a t) -> p a t", a=4)
        used[0] = mark
        swt_sb = area(4, P)
        wa_sb = area(DC, 16)
        wgu_sb = area(256)[0:16, :]
        qkT = area(4, T)
        tok2 = area(NB, 2048)
        aT = area(T)
        zg = area(2, T)
        lg = area(2, T)
        bc = area(2, T)
        dff = area(2, T)
        lv_e = area(2, T)
        lv_q = area(2, 2, T)
        lv_k = area(2, 2, T)
        at_ = area(2, 4, P)
        off = area(4, P)
        hh2 = area(512)
        sq2 = area(512)
        ssq2 = area(NB, 4)
        bst = area(NB, 6)
        bag = area(NB, 2)
        qT = arena[:, 0:16 * T].rearrange("p (a t) -> p a t", a=16)
        A = arena[:, :].rearrange("p (j t) -> p j t", j=NKEYS)
        selv = rows[:, 0:3 * 2 * HK].rearrange("p (b s k) -> p b s k", b=NB, s=3)
        selT = rows[:, 768:768 + 3 * T].rearrange("p (s t) -> p s t", s=3)
        cand = rows[:, 1536:1792]
        cand2 = rows[:, 1792:2048]

        slot_loaded = [sem(f"slot_loaded{i}") for i in range(RING)]
        unit_done = sem("unit_done")
        job_done = sem("job_done")
        bank_free = [sem(f"bank_free{i}") for i in range(4)]
        acc_free = sem("acc_free")
        first_in = sem("first_in")
        const_in = sem("const_in")
        x_in = sem("x_in")
        rows_in = sem("rows_in")
        side_in = sem("side_in")
        dve_step = sem("dve_step")
        act_step = sem("act_step")
        pool_step = sem("pool_step")
        stored = sem("stored")
        h_saved = sem("h_saved")
        h_back = sem("h_back")
        saved = nc.dram_tensor("h_saved_dram", (P, NB, D), F32, kind="Internal").ap()
        oh_square = sem("oh_square")
        oh_equal = sem("oh_equal")
        oh_first = sem("oh_first")
        oh_second = sem("oh_second")
        high_done = sem("high_done")
        low_done = sem("low_done")
        act_high = sem("act_high")
        act_low = sem("act_low")
        xsp_high = sem("xsp_high")
        g_freed = sem("g_freed")
        rows_free = sem("rows_free")
        side_free = sem("side_free")
        named = {}

        def ev(name):
            if name not in named:
                named[name] = sem(name)
            return named[name]

        def lv_buf(n):
            return 1 if n > LEVELS else n % 2

        class Group:

            def __init__(self, part, name):
                self.k, self.j, self.u = BASE[part, name]

            def bank(self, q):
                return W[(self.k + q) % 4]

            def claim(self, pe, q, it=0):
                n = (self.k + q) // 4
                if n > 0:
                    pe.wait_ge(bank_free[(self.k + q) % 4], n + it)

            def ready(self, eng, q):
                eng.wait_ge(job_done, self.j + q + 1)

            def ready_unit(self, eng, i, it=0):
                eng.wait_ge(unit_done, self.u + i + 1 + it)

            def free(self, ins, q):
                ins.then_inc(bank_free[(self.k + q) % 4], 1)

            def freed(self, eng, q, it=0):
                eng.wait_ge(bank_free[(self.k + q) % 4], (self.k + q) // 4 + 1 + it)

            def unit(self, pe, i, it=0):
                n = self.u + i
                pe.wait_ge(low_done, n + 1 + it)
                return wsp[:, n % SPLIT, :, :]

        class Chain:

            def __init__(self, eng, semaphore):
                self.eng, self.sem, self.n = eng, semaphore, 0

            def __call__(self, ins):
                ins.then_inc(self.sem, 1)
                self.n += 1
                self.eng.wait_ge(self.sem, self.n)

        class Splitter:

            def __init__(self, eng, high):
                self.eng, self.high, self.next = eng, high, 0

            def one(self, n, it=0, body=6):
                src, dst = ring[:, n % RING, :], wsp[:, n % SPLIT, :, :]
                if self.high:
                    self.eng.wait_ge(slot_loaded[n % RING], 16 * (n // RING + 1) + (16 * body // RING) * it)
                    if n >= SPLIT:
                        self.eng.wait_ge(unit_done, n - SPLIT + 1 + body * it)
                    self.eng.activation(dst[:, 0, :], src, ACT.Copy).then_inc(high_done, 1)
                else:
                    self.eng.wait_ge(high_done, n + 1 + body * it)
                    self.eng.tensor_tensor(dst[:, 1, :], src, dst[:, 0, :].bitcast(F32), ALU.subtract)\
                        .then_inc(low_done, 1)

            def upto(self, n):
                while self.next <= min(n, UNITS - 1) and self.next not in HELD:
                    self.one(self.next)
                    self.next += 1

        TILES = 2 * DEPTH * FT
        acc_use = {}
        for l in range(DEPTH):
            for part in (f"ffn1{l}", f"mix1{l}", f"ffn2{l}"):
                acc_use[part] = len(acc_use)
        for l in range(DEPTH):
            for part in (f"mix2{l}", f"peer{l}s", f"peer{l}"):
                acc_use[part] = len(acc_use)

        def acc_claim(pe, part):
            if acc_use[part]:
                pe.wait_ge(acc_free, acc_use[part])

        def h_added(eng, part):
            eng.wait_ge(acc_free, acc_use[part] + 1)

        block = ctx.enter_context(nc.Block())

        @block.sync
        def _(sp):
            sp.dma_start(h[:, 0, :], x[0:P, :]).then_inc(x_in, 16)
            sp.dma_start(h[:, 1, :], x[P:T, :]).then_inc(x_in, 16)
            sp.dma_start(cst[:, :], consts).then_inc(first_in, 16)
            sp.dma_start(pr1[:, :, :], p1.rearrange("l p n -> p l n")).then_inc(first_in, 16)
            for n in range(RING):
                sp.dma_start(ring[:, n, :], stream[n]).then_inc(slot_loaded[n], 16)
            rounds = UNITS // RING - 1
            with sp.Fori(0, rounds) as it:
                for s in range(RING):
                    sp.wait_ge(low_done, it * RING + s + 1)
                    sp.dma_start(ring[:, s, :], stream[bass.ds(it * RING + RING + s, 1)].rearrange("a p n -> p (a n)"))\
                      .then_inc(slot_loaded[s], 16)
            for n in range(RING * (rounds + 1), UNITS):
                sp.wait_ge(low_done, n - RING + 1)
                sp.dma_start(ring[:, n % RING, :], stream[n]).then_inc(slot_loaded[n % RING], 16)

        served = [0]

        def serve(pool, a, times=1):
            for _ in range(times):
                served[0] += 1
                pool.wait_ge(ev("square_ready"), served[0])
                pool.tensor_tensor(a, a, mhalf.broadcast_to(a.shape), ALU.pow).then_inc(ev("rsqrt_ready"), 1)

        def pool_mix1(pool, step, part, l):
            serve(pool, st[:, 2:4])
            G = Group(part, "tok1")
            G.freed(pool, 0)
            G.freed(pool, 1)
            qk = tok[:, :, 256:768].rearrange("p b (h m j) -> p b h m j", h=8, m=2)
            ro = rope.rearrange("p b (h m j) -> p b h m j", h=8, m=2)
            cos = cst1[:, C_COS:C_COS + 64].rearrange("p (b j) -> p b j", b=NB).unsqueeze(2).broadcast_to([P, NB, 8, 32])
            sin = cst1[:, C_SIN:C_SIN + 64].rearrange("p (b j) -> p b j", b=NB).unsqueeze(2).broadcast_to([P, NB, 8, 32])
            r4 = [ropt[:, m, :].rearrange("p (b h j) -> p b h j", b=NB, h=8) for m in range(4)]
            for m, (half, table) in enumerate(((0, cos), (1, sin), (0, sin), (1, cos))):
                ins = pool.tensor_tensor(r4[m], qk[:, :, :, half, :], table, ALU.mult)
            step(ins)
            pool.tensor_tensor(ro[:, :, :, 0, :], r4[0], r4[1], ALU.subtract)
            pool.tensor_tensor(ro[:, :, :, 1, :], r4[2], r4[3], ALU.add).then_inc(ev("rope_ready"), 1)
            serve(pool, ssq[:, 0, :], 2)
            serve(pool, ssq[:, 0, :])
            serve(pool, ssq[:, 1, :])
            pool.wait_ge(ev("NT_ready"), l + 1)
            n8 = NT.rearrange("p h b t -> p (h b) t")
            G = Group(part, "inv")
            for n in range(LEVELS):
                if n:
                    G.ready(pool, inverse_job(n - 1, 0, 1))
                pool.tensor_tensor(EL, n8, lvl(n).unsqueeze(1).broadcast_to([P, 8, P]), ALU.mult)\
                    .then_inc(ev("EL_ready"), 1)
                if n == 0:
                    pool.wait_ge(ev("W_ready"), l + 1)
                if n == 1:
                    for i in range(4):
                        Group(part, "gtr").freed(pool, i)
                    pool.wait_ge(ev("beta_ready"), l + 1)
                    pool.wait_ge(ev("pk_ready"), l + 1)
                    pool.wait_ge(ev("egel_ready"), 2 * l + 2)
                    beta = pk[:, :, 8:12].rearrange("p b h -> p h b").unsqueeze(3).broadcast_to([P, 4, NB, P])
                    pool.tensor_tensor(vb, vt, beta, ALU.mult)
                    step(pool.tensor_tensor(kbe, kt, beta, ALU.mult))
                    pool.tensor_tensor(kbe, kbe, eg.rearrange("p b h -> p h b").unsqueeze(3).broadcast_to([P, 4, NB, P]),
                                       ALU.mult).then_inc(ev("vb_ready"), 1)
                if n == 2:
                    pool.tensor_tensor(kd, kt[:, :, 0, :], el[:, 0, :].unsqueeze(2).broadcast_to([P, 4, P]), ALU.mult)
                    pool.wait_ge(ev("qkn_ready"), 4 * l + 4)
                    pool.wait_ge(ev("egb_ready"), 4 * l + 4)
                    pool.tensor_tensor(qe, cT[:, 0:4, 128:256], egb, ALU.mult).then_inc(ev("kd_ready"), 1)
            serve(pool, ssq[:, 0, :])
            serve(pool, ssq[:, 1, :])

        @block.gpsimd
        def _(pool):
            pool.dma_start(masks, levels.rearrange("n p t -> p n t")).then_inc(const_in, 16)
            pool.dma_start(cst1, consts1).then_inc(const_in, 16)
            pool.dma_start(pr2[:, :, :], p2.rearrange("l p n -> p l n")).then_inc(const_in, 16)

            def load_rows(a, b):
                pool.dma_start(rows[:, 0:a.shape[0]], a.partition_broadcast(P)).then_inc(rows_in, 16)
                pool.dma_start(rows[:, 1024:1024 + b.shape[0]], b.partition_broadcast(P)).then_inc(rows_in, 16)

            step = Chain(pool, pool_step)
            pool.memset(eps1, EPS1)
            step(pool.memset(mhalf, -0.5))
            for l in range(DEPTH):
                serve(pool, st[:, 2:4])
                if l == 0:
                    pool.wait_ge(const_in, 48)
                    load_rows(rows2[0, 0], rows2[0, 1])
                pool_mix1(pool, step, f"mix1{l}", l)
                serve(pool, st[:, 2:4])
            h_added(pool, f"mix1{DEPTH - 1}")
            pool.dma_start(final_row, rows1.partition_broadcast(P)).then_inc(side_in, 16)
            serve(pool, st[:, 2:4])
            serve(pool, moments[:, :, 1:2])
            for l in range(DEPTH):
                pool.wait_ge(side_free, l + 1)
                pool.dma_start(swt_sb, swt[l]).then_inc(side_in, 16)
                pool.dma_start(masks, levels.rearrange("n p t -> p n t")).then_inc(side_in, 16)
                pool.dma_start(wa_sb, wa[l]).then_inc(side_in, 16)
                pool.dma_start(wgu_sb, wgu[l]).then_inc(side_in, 16)
                pool.wait_ge(rows_free, 3 * l + 1)
                load_rows(rows3[l, 0], rows3[l, 1])
                pool.wait_ge(ev("bc_ready"), l + 1)
                for m in range(LEVELS + 1):
                    s = 1 << m
                    if m:
                        pool.wait_ge(ev("lv_exp"), (LEVELS + 1) * l + m)
                    b4, d4 = (a.rearrange("p m (k s) -> p (m k) s", s=2 * s) for a in (bc, dff))
                    mid = b4[:, :, s - 1:s].broadcast_to([P, T // s, s])
                    pool.tensor_tensor(d4[:, :, 0:s], mid, b4[:, :, 0:s], ALU.subtract)
                    pool.tensor_tensor(d4[:, :, s:2 * s], b4[:, :, s:2 * s], mid, ALU.subtract)\
                        .then_inc(ev("diff_ready"), 1)
                serve(pool, bag[:, :, 1:2])
                pool.wait_ge(rows_free, 3 * l + 2)
                load_rows(rows2[2 * l + 1, 0], rows2[2 * l + 1, 1])
                serve(pool, ssq2[:, 0, :])
                serve(pool, ssq2[:, 1, :])
                serve(pool, moments[:, :, 1:2])
                pool.wait_ge(ev("ln_ready"), 2 * l + 2)
                pool.dma_start(saved, h).then_inc(h_saved, 16)
                pool.wait_ge(h_saved, 16 * (l + 1))
                pool.wait_ge(ev("scores_read"), l + 1)
                pool.dma_start(h, saved).then_inc(h_back, 16)
                for b in range(NB):
                    Group(f"peer{l}", "selT").freed(pool, b)
                with pool.Fori(0, 16) as it:
                    for g in range(4):
                        pool.wait_ge(oh_equal, it * 4 + (64 * l + g + 1))
                        pool.tensor_tensor(oh[:, g, 1], oh[:, g, 1],
                                           selT[:, 2, bass.ds(it * 16 + 4 * g, 4)].unsqueeze(2)
                                           .broadcast_to([P, 4, NKEYS]), ALU.mult).then_inc(oh_second, 1)
                pool.wait_ge(g_freed, l + 1)
                load_rows(rows2[2 * l + 2, 0], rows2[2 * l + 2, 1])
                serve(pool, moments[:, :, 1:2])
            pool.wait_ge(ev("out_ready"), 1)
            pool.dma_start(out.rearrange("(b p) d -> p b d", p=P), h[:, :, :]).then_inc(stored, 16)
            pool.wait_ge(stored, 16)

        @block.tensor
        def _(pe):
            PARTS = ((0, 0), (0, 1), (1, 0))

            def product_unit(G, i, out_, it=0):
                w = G.unit(pe, i, it)
                for c in range(DC):
                    for n, (a, b) in enumerate(PARTS):
                        mm = pe.matmul(out_, lhsT=w[:, a, 128 * c:128 * c + 128], rhs=xsp[:, b, c, :],
                                       start=(c == 0 and n == 0), stop=(c == DC - 1 and n == 2))
                mm.then_inc(unit_done, 1)

            def make_xT(part, src, name, count):
                G = Group(part, name)
                for c in range(DC):
                    G.claim(pe, c)
                    if c == 0:
                        pe.wait_ge(ev(count[0]), count[1])
                    for b in range(NB):
                        mm = pe.transpose(G.bank(c)[:, 128 * b:128 * b + 128], src[:, b, 128 * c:128 * c + 128], ident)
                    mm.then_inc(job_done, 1)
                for c in range(DC - 4, DC):
                    G.freed(pe, c)

            def down_unit(G, i, act, first, last, it=0):
                w = G.unit(pe, i, it)
                for b in range(NB):
                    for m, (pa, pw) in enumerate(PARTS):
                        for n in range(2):
                            mm = pe.matmul(ACC[2 * b + n][:, :], lhsT=act[:, pa, 128 * b:128 * b + 128],
                                           rhs=w[:, pw, 512 * n:512 * n + 512],
                                           start=(first and m == 0), stop=(last and m == 2))
                mm.then_inc(unit_done, 1)

            def ffn(part, n, tiles):
                make_xT(part, xs, "xT", ("xs_ready", n))
                G = Group(part, "ffn")

                def gate_up(t, it=0):
                    i = 3 * t - 1 if t else 0
                    for m in range(2):
                        G.claim(pe, 2 * t + m, it)
                        product_unit(G, i + m, G.bank(2 * t + m)[:, 0:T], 6 * it)

                def down(t, first, last, it=0):
                    pe.wait_ge(act_low, tiles + t + 1 + 2 * it)
                    down_unit(G, min(3 * t + 4, 3 * FT - 1), hsp[:, t % 2, :, :], first, last, 6 * it)

                gate_up(0)
                gate_up(1)
                acc_claim(pe, part)
                down(0, True, False)
                gate_up(2)
                down(1, False, False)
                with pe.Fori(0, (FT - 4) // 2) as it:
                    for t in (3, 4):
                        gate_up(t, it)
                        down(t - 1, False, False, it)
                gate_up(FT - 1)
                down(FT - 2, False, False)
                down(FT - 1, False, True)

            def out_projection(part, n):
                make_xT(part, y, "yT", ("y_ready", n))
                G = Group(part, "wout")
                acc_claim(pe, part)
                for c in range(DC):
                    down_unit(G, c, xsp[:, :, c, :], c == 0, c == DC - 1)

            def token_group(part, g):
                G = Group(part, f"tok{g}")
                for b in range(NB):
                    G.claim(pe, b)
                for i in range(4):
                    w = G.unit(pe, i)
                    for cc in range(2):
                        c = 2 * i + cc
                        for b in range(NB):
                            for n, (px, pw) in enumerate(PARTS):
                                mm = pe.matmul(G.bank(b)[:, :], lhsT=xsp[:, px, c, 128 * b:128 * b + 128],
                                               rhs=w[:, pw, 512 * cc:512 * cc + 512],
                                               start=(c == 0 and n == 0), stop=(c == DC - 1 and n == 2))
                    mm.then_inc(unit_done, 1)

            def mix1(part, l):
                make_xT(part, xs, "xT", ("xs_ready", 3 * l + 2))
                pe.wait_ge(const_in, 48)

                def channel_group(g):
                    G = Group(part, f"tt{g}")
                    for q in range(4):
                        G.claim(pe, q)
                        product_unit(G, q, G.bank(q)[:, 0:T])

                G = Group(part, "small")
                G.claim(pe, 0)
                pe.wait_ge(ev("w16_low"), l + 1)
                for b in range(NB):
                    for c in range(DC):
                        for m, (px, pw) in enumerate(PARTS):
                            mm = pe.matmul(G.bank(0)[:, 16 * b:16 * b + 16], lhsT=xsp[:, px, c, 128 * b:128 * b + 128],
                                           rhs=w16[:, pw, 16 * c:16 * c + 16],
                                           start=(c == 0 and m == 0), stop=(c == DC - 1 and m == 2))
                mm.then_inc(job_done, 1)
                channel_group(0)
                G = Group(part, "cums")
                G.claim(pe, 0)
                pe.wait_ge(ev("cg_ready"), l + 1)
                o = G.bank(0)
                pe.matmul(o[:, 0:8], lhsT=tri, rhs=cg[:, 0, :], start=True, stop=True)
                pe.matmul(o[:, 8:16], lhsT=tri, rhs=cg[:, 1, :], start=True, stop=False)
                pe.matmul(o[:, 8:12], lhsT=ones, rhs=cg[:, 0, 0:4], start=False, stop=True)
                pe.matmul(o[:, 16:20], lhsT=ones, rhs=cg[:, 0, 4:8], start=True, stop=True)
                pe.matmul(o[:, 20:24], lhsT=ones, rhs=cg[:, 1, 4:8], start=True, stop=True).then_inc(job_done, 1)
                channel_group(1)
                G = Group(part, "rows")
                G.claim(pe, 0)
                pe.wait_ge(ev("pk_ready"), l + 1)
                for b in range(NB):
                    mm = pe.transpose(G.bank(0)[0:12, 128 * b:128 * b + 128], pk[:, b, :], ident)
                mm.then_inc(job_done, 1)
                channel_group(2)
                G = Group(part, "mcols")
                G.claim(pe, 0)
                pe.wait_ge(ev("mrow_ready"), l + 1)
                for b in range(NB):
                    mm = pe.transpose(G.bank(0)[:, 4 * b:4 * b + 4], mrow[0:4, 128 * b:128 * b + 128], ident[0:4, 0:4])
                mm.then_inc(job_done, 1)
                channel_group(3)
                token_group(part, 0)
                token_group(part, 1)
                G = Group(part, "gss")
                pe.wait_ge(ev("gsq_ready"), l + 1)
                for q in range(4):
                    G.claim(pe, q)
                    pe.matmul(G.bank(q)[:, :], lhsT=ones, rhs=gsq[:, 2 * q:2 * q + 2, :], start=True, stop=True)\
                      .then_inc(job_done, 1)
                token_group(part, 2)
                token_group(part, 3)

                def spread(name, src, first, n):
                    G = Group(part, name)
                    for q in range(2):
                        G.claim(pe, q)
                        for i in range(2):
                            r = first + 2 * q + i
                            mm = pe.matmul(G.bank(q)[:, T * i:T * i + T],
                                           lhsT=ident[0:n, r:r + 1].to_broadcast([n, P]), rhs=src[0:n, :],
                                           start=True, stop=True)
                        mm.then_inc(job_done, 1)

                spread("bM", mrow, 0, 4)

                def head_scores(name, qk, q0, k0):
                    G = Group(part, name)
                    for i in range(4):
                        s = slice(64 * (i % 2), 64 * (i % 2) + 64)
                        G.claim(pe, i)
                        kh, qh = qk[s, k0 + i // 2, :], qk[s, q0 + i // 2, :]
                        pe.matmul(G.bank(i)[:, 0:256], lhsT=kh[:, 0:128], rhs=qh, start=True, stop=True)
                        pe.matmul(G.bank(i)[:, 256:384], lhsT=kh[:, 128:256], rhs=qh[:, 128:256],
                                  start=True, stop=True).then_inc(job_done, 1)

                def head_out(name, p, v, n, of):
                    G, scores = Group(part, name), Group(part, of)
                    for b in range(NB):
                        G.claim(pe, b)
                        for i in range(4):
                            if b == 0:
                                scores.freed(pe, i)
                            o = G.bank(b)[:, n * i:n * i + n]
                            mm = pe.matmul(o, lhsT=p[:, i, 128 * b:128 * b + 128], rhs=v(0, i), start=True, stop=(b == 0))
                            if b:
                                mm = pe.matmul(o, lhsT=p[:, i, 256:384], rhs=v(1, i), start=False, stop=True)
                        mm.then_inc(job_done, 1)

                head_scores("msc", mqk, 0, 2)
                head_out("mout", pm, lambda b, i: vaug[:, b, i, :], 65, "msc")
                G = Group(part, "rtr")
                pe.wait_ge(ev("rope_ready"), l + 1)
                for q in range(4):
                    G.claim(pe, q)
                    for b in range(NB):
                        mm = pe.transpose(G.bank(q)[:, 128 * b:128 * b + 128], rope[:, b, 128 * q:128 * q + 128], ident)
                    mm.then_inc(job_done, 1)
                for q in range(4):
                    G.freed(pe, q)
                head_scores("rsc", rT, 0, 2)
                head_out("rout", rp, lambda b, i: tok[:, b, 768 + 64 * i:832 + 64 * i], 64, "rsc")
                G = Group(part, "gtr")
                pe.wait_ge(ev("qkn_ready"), 4 * l + 4)
                for i in range(4):
                    G.claim(pe, i)
                    for b in range(NB):
                        pe.transpose(G.bank(i)[:, 128 * b:128 * b + 128], cT[:, 4 + i, 128 * b:128 * b + 128], ident)
                        mm = pe.transpose(G.bank(i)[:, 256 + 128 * b:384 + 128 * b],
                                          cT[:, 8 + i, 128 * b:128 * b + 128], ident)
                    mm.then_inc(job_done, 1)
                spread("bg", rows12, 4, 12)
                spread("bb", rows12, 8, 12)
                G = Group(part, "gkk")
                for i in range(4):
                    G.claim(pe, i)
                    for b in range(NB):
                        t = slice(128 * b, 128 * b + 128)
                        pe.matmul(G.bank(i)[:, t], lhsT=cT[:, 4 + i, t], rhs=cT[:, 4 + i, t], start=True, stop=True)
                        mm = pe.matmul(G.bank(i)[:, 256 + 128 * b:384 + 128 * b], lhsT=cT[:, 4 + i, t],
                                       rhs=cT[:, i, t], start=True, stop=True)
                    mm.then_inc(job_done, 1)
                G = Group(part, "inv")
                for n in range(LEVELS):
                    pe.wait_ge(ev("EL_ready"), LEVELS * l + n + 1)
                    if n == 0:
                        for half in range(2):
                            G.claim(pe, half)
                            for m in range(4):
                                mm = pe.transpose(G.bank(half)[:, 128 * m:128 * m + 128], EL[:, 4 * half + m, :], ident)
                            mm.then_inc(job_done, 1)
                        pe.wait_ge(ev("W_ready"), l + 1)
                        continue
                    for q, (lhs, rhs) in enumerate(((EL, TI), (WI, XI), (XI, WI))):
                        if n == LEVELS - 1 and q == 1:
                            continue
                        for half in range(2):
                            job = inverse_job(n, q, half)
                            G.claim(pe, job)
                            if q == 0:
                                G.freed(pe, inverse_job(n - 1, 1, half))
                            elif q == 1 or n == LEVELS - 1:
                                G.freed(pe, inverse_job(n, 0, half))
                                if n > 1:
                                    G.freed(pe, inverse_job(n - 1, 2, half))
                            for m in range(4):
                                a = 4 * half + m
                                mm = pe.matmul(G.bank(job)[:, 128 * m:128 * m + 128], lhsT=lhs[:, a, :],
                                               rhs=rhs[:, a, :], start=True, stop=True)
                            mm.then_inc(job_done, 1)
                for back in (2, 1):
                    G.freed(pe, 6 * LEVELS - 6 - back)
                G = Group(part, "gout")

                def heads(job, pairs):
                    G.claim(pe, job)
                    for i in range(4):
                        for n, (lhs, rhs) in enumerate(pairs(i)):
                            mm = pe.matmul(G.bank(job)[:, 128 * i:128 * i + 128], lhsT=lhs, rhs=rhs,
                                           start=(n == 0), stop=(n == len(pairs(i)) - 1))
                    mm.then_inc(job_done, 1)

                pe.wait_ge(ev("vb_ready"), l + 1)
                pe.wait_ge(ev("kd_ready"), l + 1)
                heads(0, lambda i: [(WI[:, 2 * i, :], vb[:, i, 0, :])])
                heads(1, lambda i: [(WI[:, 2 * i + 1, :], vb[:, i, 1, :])])
                heads(2, lambda i: [(kbe[:, i, 1, :], WI[:, 2 * i + 1, :])])
                G.freed(pe, 0)
                heads(3, lambda i: [(kd[:, i, :], u0[:, i, :])])
                G.freed(pe, 2)
                G.freed(pe, 3)
                heads(4, lambda i: [(wT[:, i, :], S1[:, i, :])])
                heads(5, lambda i: [(QK[:, i, 0, :], u0[:, i, :])])
                G.freed(pe, 4)
                heads(6, lambda i: [(qe[:, i, :], S1[:, i, :]), (QK[:, i, 1, :], u1[:, i, :])])
                out_projection(part, l + 1)

            def mix2(part, l):
                make_xT(part, h, "xT", ("ln_ready", 2 * l + 1))
                G = Group(part, "small")
                G.claim(pe, 0)
                pe.wait_ge(side_in, 16 + 64 * (l + 1))
                pe.wait_ge(ev("wa_low"), l + 1)
                for c in range(DC):
                    for m, (px, pw) in enumerate(PARTS):
                        mm = pe.matmul(G.bank(0)[0:16, 0:T], lhsT=w16[:, pw, 16 * c:16 * c + 16], rhs=xsp[:, px, c, :],
                                       start=(c == 0 and m == 0), stop=(c == DC - 1 and m == 2))
                mm.then_inc(job_done, 1)
                S, G = G, Group(part, "tt")
                for q in range(4):
                    G.claim(pe, q)
                    product_unit(G, q, G.bank(q)[:, 0:T])
                QK4, G = G, Group(part, "logg")
                S.freed(pe, 0)
                G.claim(pe, 0)
                for m in range(2):
                    mm = pe.matmul(G.bank(0)[:, T * m:T * m + T], lhsT=wgu_sb[:, 128 * m:128 * m + 128],
                                   rhs=aT[0:16, :], start=True, stop=True)
                mm.then_inc(job_done, 1)

                def level_products(n):
                    G = Group(part, f"lvl{n}")
                    if n == LEVELS:
                        for q in range(4):
                            QK4.freed(pe, q)
                    else:
                        pe.wait_ge(ev("lv_ready"), (LEVELS + 1) * l + min(n, LEVELS) + 1)
                    qs, ks = (qkT[:, 0:2, :], qkT[:, 2:4, :]) if n == LEVELS else (lv_q[:, lv_buf(n)], lv_k[:, lv_buf(n)])
                    for odd in range(2):
                        G.claim(pe, odd)
                        s = slice(64 * odd, 64 * odd + 64)
                        pairs = [(0, 0), (1, 1)] if n <= LEVELS else [(0, 1)]
                        for m in range(2):
                            for b, (src, dst) in enumerate(pairs):
                                c = 128 * (len(pairs) * m + b)
                                mm = pe.matmul(G.bank(odd)[:, c:c + 128], lhsT=ks[s, m, 128 * src:128 * src + 128],
                                               rhs=qs[s, m, 128 * dst:128 * dst + 128], start=True, stop=True)
                        mm.then_inc(job_done, 1)

                for g in range(4):
                    token_group(part, g)
                    for n in LEVEL_ORDER[g]:
                        level_products(n)
                L = Group(part, "lvl8")
                G = Group(part, "gla")
                pe.wait_ge(ev("at_ready"), l + 1)
                L.freed(pe, 0)
                L.freed(pe, 1)
                for b in range(NB):
                    G.claim(pe, b)
                    for i in range(4):
                        o = G.bank(b)[:, 128 * i:128 * i + 128]
                        if b:
                            pe.matmul(o, lhsT=off[:, 2 * (i % 2) + i // 2, :], rhs=tok2[:, 0, 128 * i:128 * i + 128], start=True, stop=False)
                        mm = pe.matmul(o, lhsT=at_[:, i % 2, 2 * (i // 2) + b, :], rhs=tok2[:, b, 128 * i:128 * i + 128],
                                       start=(b == 0), stop=True)
                    mm.then_inc(job_done, 1)
                G = Group(part, "sgu")
                pe.wait_ge(ev("sgv_ready"), l + 1)
                for b in range(NB):
                    G.claim(pe, b)
                    for i in range(4):
                        mm = pe.matmul(G.bank(b)[:, 128 * i:128 * i + 128], lhsT=swt_sb[:, i, :],
                                       rhs=tok2[:, b, 1536 + 128 * i:1664 + 128 * i], start=True, stop=True)
                    mm.then_inc(job_done, 1)
                out_projection(part, DEPTH + l + 1)

            def peer(part, l):
                make_xT(part, h, "xT", ("ln_ready", 2 * l + 2))
                G = Group(part, "tt")
                for q in range(16):
                    G.claim(pe, q)
                    product_unit(G, q, G.bank(q)[:, 0:T])
                for q in range(12, 16):
                    G.freed(pe, q)
                acc_claim(pe, part + "s")
                G = Group(part, "score")
                for b in range(NB):
                    for i in range(PH):
                        if b and i % 2 == 0:
                            G.claim(pe, i // 2)
                        o = (ACC[i // 2] if b == 0 else G.bank(i // 2))[:, 256 * (i % 2):256 * (i % 2) + 256]
                        for m in range(2):
                            mm = pe.matmul(o[:, 128 * m:128 * m + 128], lhsT=qT[:, 2 * i + m, 128 * b:128 * b + 128],
                                           rhs=pr2[:, l, Q_K1 + 128 * m:Q_K1 + 128 * m + 128], start=True, stop=True)
                        if b and i % 2:
                            mm.then_inc(job_done, 1)
                G = Group(part, "U")
                with pe.Fori(0, NKEYS // UNITS_BODY) as it:
                    for q in range(UNITS_BODY):
                        G.claim(pe, q, it * (UNITS_BODY // 4))
                        product_unit(G, q, G.bank(q)[:, 0:T], it * UNITS_BODY)
                for q in range(NKEYS // UNITS_BODY * UNITS_BODY, NKEYS):
                    G.claim(pe, q)
                    product_unit(G, q, G.bank(q)[:, 0:T])
                G = Group(part, "selT")
                for b in range(NB):
                    G.claim(pe, b)
                    pe.wait_ge(ev("sel_ready"), NB * (l + 1))
                    for s in range(3):
                        mm = pe.transpose(G.bank(b)[:, 128 * s:128 * s + 128], selv[:, b, s, :], ident)
                    mm.then_inc(job_done, 1)
                G = Group(part, "G")
                with pe.Fori(0, 16) as it:
                    for q in range(4):
                        pe.wait_ge(oh_second, it * 4 + (64 * l + q + 1))
                        if q:
                            pe.wait_ge(oh_first, it * 3 + (48 * l + q))
                        G.claim(pe, q, it)
                        for t in range(4):
                            mm = pe.matmul(G.bank(q)[:, 128 * t:128 * t + 128], lhsT=oh[:, q, 0, t, :],
                                           rhs=oh[:, q, 1, t, :], start=True, stop=True)
                        mm.then_inc(job_done, 1)
                acc_claim(pe, part)
                G = Group(part, "V")

                def value_unit(i, first, last, it=None):
                    n = 0 if it is None else it
                    pe.wait_ge(act_low, n * 6 + (TILES + NKEYS * l + i + 1))
                    down_unit(G, i, hsp[:, i % 2, :, :], first, last, 6 * n)

                value_unit(0, True, False)
                value_unit(1, False, False)
                with pe.Fori(0, 20) as it:
                    for q in range(6):
                        value_unit(2 + q, False, False, it)
                for q in range(122, 128):
                    value_unit(q, False, q == 127)

            pe.wait_ge(first_in, 32)
            for l in range(DEPTH):
                ffn(f"ffn1{l}", 3 * l + 1, 2 * l * FT)
                mix1(f"mix1{l}", l)
                ffn(f"ffn2{l}", 3 * l + 3, (2 * l + 1) * FT)
            for l in range(DEPTH):
                mix2(f"mix2{l}", l)
                peer(f"peer{l}", l)

        @block.scalar
        def _(act):
            step = Chain(act, act_step)
            split = Splitter(act, True)

            def xsp_highs(part, name, gain):
                G = Group(part, name)
                for c in range(DC):
                    G.ready(act, c)
                    act.activation(xsp[:, 0, c, :], G.bank(c)[:, 0:T], ACT.Copy,
                                   scale=1.0 if gain is None else gain[:, c:c + 1]).then_inc(xsp_high, 1)

            def head_squares(G, q, d, waste, sums):
                for b in range(NB):
                    G.ready(act, q + b)
                    for i in range(4):
                        c = slice(d * i, d * i + d)
                        ins = act.activation(waste[b][:, c], G.bank(q + b)[:, c], ACT.Square,
                                             accum_out=sums[:, b, i:i + 1])
                    ins.then_inc(ev("head_sums"), 1)

            def squares(before=None):
                for b in range(NB):
                    if before is not None:
                        if b == 0:
                            act.wait_ge(ev("h_first"), acc_use[before] + 1)
                        else:
                            h_added(act, before)
                    act.activation(xs[:, b, :], h[:, b, :], ACT.Square, accum_out=st[:, b:b + 1])\
                       .then_inc(ev("sumsq"), 1)

            def ffn(part, l, gain, before):
                squares(before)
                xsp_highs(part, "xT", pr1[:, l, gain:gain + 8])
                G = Group(part, "ffn")

                def gate(t, it=0):
                    G.ready_unit(act, 3 * t - 1 if t else 0, 6 * it)
                    if t >= 2:
                        G.freed(act, 2 * t - 3, it)
                    G.free(act.activation(sil[:, t % 2, :], G.bank(2 * t)[:, 0:T], ACT.Silu), 2 * t)

                def high(t, it=0):
                    G.freed(act, 2 * t + 1, it)
                    if t >= 2:
                        G.ready_unit(act, 3 * (t - 2) + 4, 6 * it)
                    act.activation(hsp[:, t % 2, 0, :], prod[:, t % 2, :], ACT.Copy).then_inc(act_high, 1)

                for t in range(3):
                    split.upto(G.u + (3 * t + 1 if t else 2))
                    gate(t)
                    split.upto(G.u + (3 * t + 2 if t else 3))
                    high(t)
                with act.Fori(0, (FT - 4) // 2) as it:
                    for t in (3, 4):
                        split.one(G.u + 3 * t, it)
                        split.one(G.u + 3 * t + 1, it)
                        gate(t, it)
                        split.one(G.u + 3 * t + 2, it)
                        high(t, it)
                split.next = G.u + 3 * (FT - 1)
                split.upto(G.u + 3 * FT - 2)
                gate(FT - 1)
                split.upto(G.u + 3 * FT - 1)
                high(FT - 1)
                split.upto(G.u + 3 * FT + 1)

            def mix1(part, l):
                squares(f"ffn1{l}")
                act.wait_ge(const_in, 48)
                act.activation(w16[:, 0, :], pr1[:, l, P_W16:P_W16 + 128], ACT.Copy).then_inc(ev("w16_high"), 1)
                xsp_highs(part, "xT", pr1[:, l, P_MIX:P_MIX + 8])
                for q in range(16):
                    G = Group(part, f"tt{q // 4}")
                    split.upto(G.u + q % 4 + 2)
                    G.ready_unit(act, q % 4)
                    src = G.bank(q % 4)[:, 0:T]
                    if q < 4:
                        G.free(act.activation(mqk[:, q, :], src, ACT.Copy, scale=0.125 if q < 2 else 1.0), q % 4)
                    else:
                        G.free(act.activation(cin[:, q - 4, 3:3 + T], src, ACT.Copy), q % 4)
                    if q == 1:
                        act.wait_ge(ev("gate_abs"), l + 1)
                        step(act.activation(lsg[:, 1], lsg[:, 0], ACT.Exp))
                        act.activation(nea, pr1[:, l, P_ALOG:P_ALOG + 4], ACT.Exp)
                        act.activation(lsg[:, 2], lsg[:, 1], ACT.Ln, bias=1.0).then_inc(ev("gate_ln"), 1)
                        act.activation(pk[:, :, 8:12], g16[:, :, 12:16], ACT.Sigmoid).then_inc(ev("beta_ready"), 1)
                    if q == 7:
                        act.wait_ge(ev("gcols_ready"), l + 1)
                        act.activation(eg, cs[:, :, 4:8], ACT.Exp).then_inc(ev("egel_ready"), 1)
                        act.activation(el, el, ACT.Exp).then_inc(ev("egel_ready"), 1)
                    if q == 13:
                        act.wait_ge(ev("mm_ready"), l + 1)
                        act.activation(guard, guard, ACT.Exp, scale=-1.0).then_inc(ev("guard_ready"), 1)

                def root(q):
                    G = Group(part, "gss")
                    G.ready(act, q)
                    if q >= 2:
                        act.wait_ge(ev("qkn_ready"), 4 * l + q - 1)
                    G.free(act.activation(rn[:, q % 2, :], G.bank(q)[:, :], ACT.Sqrt, bias=eps1), q)

                for g in range(4):
                    G = Group(part, f"tok{g}")
                    for b in range(NB):
                        split.upto(G.u + 5)
                        G.ready_unit(act, 3)
                        o = G.bank(b)
                        if g == 0:
                            act.activation(vaug[:, b, :, 0:64], o[:, 0:256].rearrange("p (h d) -> p h d", h=4), ACT.Copy)
                            ins = act.activation(tok[:, b, 0:256], o[:, 256:512], ACT.Sigmoid)
                        elif g == 1:
                            ins = act.activation(tok[:, b, 256:768], o[:, :], ACT.Copy)
                        elif g == 2:
                            act.activation(tok[:, b, 768:1024], o[:, 0:256], ACT.Copy)
                            ins = act.activation(tok[:, b, 1024:1280], o[:, 256:512], ACT.Silu)
                        else:
                            ins = act.activation(tok[:, b, 1280:1792], o[:, :], ACT.Silu)
                        G.free(ins, b)
                    if g == 0:
                        for m in range(3):
                            act.wait_ge(ev("conv_done"), 12 * l + 4 * m + 4)
                            act.activation(cT[:, 4 * m:4 * m + 4, :], cT[:, 4 * m:4 * m + 4, :], ACT.Silu)\
                               .then_inc(ev("conv_silu"), 1)
                            split.upto(G.u + 5 + m)
                        act.wait_ge(ev("conv_silu"), 3 * l + 2)
                        act.activation(gsq, cT[:, 0:8, :], ACT.Square).then_inc(ev("gsq_ready"), 1)
                    if g == 1:
                        split.upto(G.u + 6)
                        root(0)
                        root(1)
                        split.upto(G.u + 7)
                        root(2)
                    if g == 2:
                        root(3)
                G = Group(part, "bM")
                for q in range(2):
                    G.freed(act, q)
                    act.activation(ew[:, 2 * q:2 * q + 2, :], ew[:, 2 * q:2 * q + 2, :], ACT.Exp, scale=-1.0)\
                       .then_inc(ev("ew_ready"), 1)
                G = Group(part, "rtr")
                for q in range(4):
                    G.ready(act, q)
                    G.free(act.activation(rT[:, q, :], G.bank(q)[:, 0:T], ACT.Copy), q)
                head_squares(Group(part, "rout"), 0, 64, (hh, sq), ssq)
                G = Group(part, "gtr")
                for i in range(4):
                    G.ready(act, i)
                    act.activation(kt[:, i].rearrange("p b d -> p (b d)"), G.bank(i)[:, 0:256], ACT.Copy)
                    G.free(act.activation(vt[:, i].rearrange("p b d -> p (b d)"), G.bank(i)[:, 256:512], ACT.Copy), i)
                G = Group(part, "bg")
                for q in range(2):
                    G.ready(act, q)
                    for i in range(2):
                        act.activation(egb[:, 2 * q + i, :], G.bank(q)[:, T * i + 128:T * i + 256], ACT.Exp)\
                           .then_inc(ev("egb_ready"), 1)
                for q in range(2):
                    G.freed(act, q)
                    act.activation(dec[:, 2 * q:2 * q + 2], dec[:, 2 * q:2 * q + 2], ACT.Exp)\
                       .then_inc(ev("dec_exp"), 1)
                G = Group(part, "inv")
                for n in range(1, LEVELS):
                    for half in range(2):
                        job = inverse_job(n, 0, half)
                        G.ready(act, job)
                        G.free(act.activation(XI[:, 4 * half:4 * half + 4, :].rearrange("p a t -> p (a t)"),
                                              G.bank(job)[:, :], ACT.Copy), job)
                G = Group(part, "gout")
                for job, dst, scale in ((0, u0, 1.0), (2, wT, -1.0), (3, S1, 1.0)):
                    G.ready(act, job)
                    G.free(act.activation(dst.rearrange("p h t -> p (h t)"), G.bank(job)[:, :], ACT.Copy, scale=scale), job)
                head_squares(G, 5, 128, (hh, sq), ssq)
                xsp_highs(part, "yT", pr1[:, l, P_Y:P_Y + 8])
                split.upto(Group(part, "wout").u + DC + 1)

            def mix2(part, l):
                xsp_highs(part, "xT", None)
                act.wait_ge(side_in, 16 + 64 * (l + 1))
                act.activation(w16[:, 0, :], wa_sb.rearrange("p c n -> p (c n)"), ACT.Copy).then_inc(ev("wa_high"), 1)
                G = Group(part, "small")
                G.ready(act, 0)
                G.free(act.activation(aT[0:16, :], G.bank(0)[0:16, 0:T], ACT.Copy), 0)
                G = Group(part, "tt")
                for q in range(4):
                    split.upto(G.u + q + 2)
                    G.ready_unit(act, q)
                    G.free(act.activation(qkT[:, q, :], G.bank(q)[:, 0:T], ACT.Copy, scale=0.125 if q < 2 else 1.0), q)
                K = [Group(part, f"tok{g}") for g in range(4)]
                split.upto(K[0].u + 2)
                act.wait_ge(ev("zabs_ready"), l + 1)
                step(act.activation(dff, dff, ACT.Exp))
                act.activation(lg, dff, ACT.Ln, bias=1.0).then_inc(ev("lg_ln"), 1)

                def decays(m):
                    act.wait_ge(ev("diff_ready"), (LEVELS + 1) * l + m + 1)
                    if m:
                        act.wait_ge(ev("lv_ready"), (LEVELS + 1) * l + m)
                    act.activation(lv_e, dff, ACT.Exp, scale=1.0 / 16.0).then_inc(ev("lv_exp"), 1)

                def copy_out(g):
                    func = (ACT.Copy, ACT.Silu, ACT.Gelu, ACT.Gelu)[g]
                    K[g].ready_unit(act, 3)
                    for b in range(NB):
                        K[g].free(act.activation(tok2[:, b, 512 * g:512 * g + 512], K[g].bank(b)[:, :], func), b)

                decays(0)
                split.upto(K[0].u + 3)
                decays(1)
                for g in range(4):
                    split.upto(K[g].u + 5)
                    copy_out(g)
                    if g < 3:
                        split.upto(K[g].u + 6)
                        decays(2 * g + 2 if g == 0 else 2 * g + 1)
                        split.upto(K[g].u + 7)
                        if g:
                            decays(2 * g + 2)
                decays(7)
                head_squares(Group(part, "gla"), 0, 128, (hh2, sq2), ssq2)
                xsp_highs(part, "yT", yg[:, l, :])
                split.upto(Group(part, "wout").u + DC + 1)

            def peer(part, l):
                xsp_highs(part, "xT", None)
                G = Group(part, "tt")
                for q in range(16):
                    split.upto(G.u + q + 2)
                    G.ready_unit(act, q)
                    G.free(act.activation(qT[:, q, :], G.bank(q)[:, 0:T], ACT.Copy), q)
                G = Group(part, "score")
                split.upto(G.u + 2)
                act.wait_ge(h_saved, 16 * (l + 1))
                for q in range(4):
                    G.ready(act, q)
                    G.free(act.activation(sc1[:, 512 * q:512 * q + 512], G.bank(q)[:, :], ACT.Copy), q)
                G = Group(part, "U")
                with act.Fori(0, NKEYS // UNITS_BODY) as it:
                    for q in range(UNITS_BODY):
                        split.one(G.u + q + 3, it, UNITS_BODY)
                        G.ready_unit(act, q, it * UNITS_BODY)
                        G.free(act.activation(arena[:, bass.ds(it * (UNITS_BODY * T) + q * T, T)],
                                              G.bank(q)[:, 0:T], ACT.Gelu), q)
                split.next = G.u + NKEYS // UNITS_BODY * UNITS_BODY + 3
                for q in range(NKEYS // UNITS_BODY * UNITS_BODY, NKEYS):
                    split.upto(G.u + q + 3)
                    G.ready_unit(act, q)
                    G.free(act.activation(A[:, q, :], G.bank(q)[:, 0:T], ACT.Gelu), q)
                for b in range(NB):
                    act.wait_ge(ev("smx_ready"), NB * l + b + 1)
                    act.activation(selv[:, b, 2, :], selv[:, b, 2, :], ACT.Exp).then_inc(ev("smx_exp"), 1)
                for b in range(NB):
                    Group(part, "selT").freed(act, b)
                G = Group(part, "G")
                with act.Fori(0, 16) as it:
                    for g in range(1, 4):
                        act.wait_ge(job_done, it * 4 + (G.j + g - 3))
                        for t in range(4):
                            ins = act.activation(oh[:, g, 0, t, :], iota, ACT.Square, scale=-1.0,
                                                 bias=selT[:, 0, bass.ds(it * 16 + (4 * g + t), 1)])
                        ins.then_inc(oh_square, 1)
                        act.wait_ge(oh_square, it * 3 + (48 * l + g))
                        act.activation(oh[:, g, 0], oh[:, g, 0], ACT.Relu, scale=-1.0, bias=1.0).then_inc(oh_first, 1)
                act.wait_ge(g_freed, l + 1)
                G = Group(part, "V")

                def stage(j, it=0):
                    if j >= 2:
                        G.ready_unit(act, j - 2, it * 6)
                    act.activation(hsp[:, j % 2, 0, :], arena[:, bass.ds(it * (6 * T) + j * T, T)], ACT.Copy)\
                       .then_inc(act_high, 1)

                split.one(G.u)
                stage(0)
                stage(1)
                split.one(G.u + 1)
                split.one(G.u + 2)
                with act.Fori(0, 20) as it:
                    for j in range(2, 8):
                        stage(j, it)
                        split.one(G.u + j + 1, it)
                split.next = G.u + 123
                for j in range(122, 128):
                    stage(j)
                    split.upto(G.u + j + 1)
                split.upto(G.u + 129)

            yg = pr2[:, :, Q_GAIN:Q_GAIN + 8]
            act.wait_ge(first_in, 32)
            act.wait_ge(x_in, 32)
            for l in range(DEPTH):
                ffn(f"ffn1{l}", l, P_FFN1, f"ffn2{l - 1}" if l else None)
                mix1(f"mix1{l}", l)
                ffn(f"ffn2{l}", l, P_FFN2, f"mix1{l}")
            squares(f"ffn2{DEPTH - 1}")
            for l in range(DEPTH):
                mix2(f"mix2{l}", l)
                peer(f"peer{l}", l)

        @block.vector
        def _(dve):
            step = Chain(dve, dve_step)
            ts, tt, stt = dve.tensor_scalar, dve.tensor_tensor, dve.scalar_tensor_tensor

            split = Splitter(dve, False)
            lows = [0]

            def xsp_lows(part, name, gain):
                G = Group(part, name)
                for c in range(DC):
                    lows[0] += 1
                    dve.wait_ge(xsp_high, lows[0])
                    G.free(stt(xsp[:, 1, c, :], G.bank(c)[:, 0:T], 1.0 if gain is None else gain[:, c:c + 1],
                               xsp[:, 0, c, :].bitcast(F32), ALU.mult, ALU.subtract), c)

            norms = [0]
            asked = [0]

            def rsqrt(ins):
                ins.then_inc(ev("square_ready"), 1)
                asked[0] += 1
                dve.wait_ge(ev("rsqrt_ready"), asked[0])

            def rms_scale():
                norms[0] += 1
                dve.wait_ge(ev("sumsq"), NB * norms[0])
                rsqrt(ts(st[:, 2:4], st[:, 0:2], 1.0 / D, EPS1, ALU.mult, ALU.add))

            def rms(part, gain):
                rms_scale()
                for b in range(NB):
                    ins = ts(xs[:, b, :], h[:, b, :], st[:, 2 + b:3 + b], None, ALU.mult)
                ins.then_inc(ev("xs_ready"), 1)
                xsp_lows(part, "xT", gain)

            def add_to_h(part, last, scale_acc, scale_h):
                G, i = last
                G.ready_unit(dve, i)
                for b in range(NB):
                    for n in range(2):
                        hs = h[:, b, 512 * n:512 * n + 512]
                        if scale_h == 1.0:
                            ins = stt(hs, ACC[2 * b + n][:, :], scale_acc, hs, ALU.mult, ALU.add)
                            if b == 0 and n == 1:
                                ins.then_inc(ev("h_first"), 1)
                        else:
                            ins = stt(hs, hs, scale_h, ACC[2 * b + n][:, :], ALU.mult, ALU.add)
                ins.then_inc(acc_free, 1)
                h_added(dve, part)

            def ffn(part, l, gain, tiles):
                rms(part, pr1[:, l, gain:gain + 8])
                G = Group(part, "ffn")

                def up(t, it=0):
                    G.ready_unit(dve, 3 * t if t else 1, 6 * it)
                    G.freed(dve, 2 * t, it)
                    if tiles + t >= 2:
                        dve.wait_ge(act_low, tiles + t - 1 + 2 * it)
                    G.free(tt(prod[:, t % 2, :], G.bank(2 * t + 1)[:, 0:T], sil[:, t % 2, :], ALU.mult), 2 * t + 1)

                def low(t, it=0):
                    G.freed(dve, 2 * t + 1, it)
                    dve.wait_ge(act_high, tiles + t + 1 + 2 * it)
                    tt(hsp[:, t % 2, 1, :], prod[:, t % 2, :], hsp[:, t % 2, 0, :].bitcast(F32), ALU.subtract)\
                        .then_inc(act_low, 1)

                for t in range(3):
                    split.upto(G.u + (3 * t + 2 if t else 3))
                    up(t)
                    low(t)
                with dve.Fori(0, (FT - 4) // 2) as it:
                    for t in (3, 4):
                        for n in range(3):
                            split.one(G.u + 3 * t + n, it)
                        up(t, it)
                        low(t, it)
                split.next = G.u + 3 * (FT - 1)
                split.upto(G.u + 3 * FT - 1)
                up(FT - 1)
                low(FT - 1)
                split.upto(G.u + 3 * FT + 1)
                add_to_h(part, (G, 3 * FT - 1), 0.5, 1.0)

            def head_norm(w, gate, dst, sqb, ss):
                w, s, gate, dst = (a.rearrange("p (h d) -> p h d", h=4) for a in (w, sqb[:, 0:256], gate, dst))
                step(tt(s, w, w, ALU.mult))
                step(dve.tensor_reduce(ss, s, AX_X, ALU.add))
                rsqrt(ts(ss, ss, 1.0 / 64, EPS1, ALU.mult, ALU.add))
                step(tt(w, w, ss.unsqueeze(2).broadcast_to([P, 4, 64]), ALU.mult))
                return tt(dst, w, gate, ALU.mult)

            summed = [0]

            def head_norms(G, q, d, eps, dst, gate, buf, ss):
                for b in range(NB):
                    summed[0] += 1
                    dve.wait_ge(ev("head_sums"), summed[0])
                    ts(ss[:, b, :], ss[:, b, :], 1.0 / d, eps, ALU.mult, ALU.add).then_inc(ev("square_ready"), 1)
                for b in range(NB):
                    w, o, g, y_ = (a.rearrange("p (h d) -> p h d", h=4)
                                   for a in (buf[b][:, 0:4 * d], G.bank(q + b)[:, 0:4 * d], gate(b), dst(b)))
                    asked[0] += 1
                    dve.wait_ge(ev("rsqrt_ready"), asked[0])
                    G.free(tt(w, o, ss[:, b, :].unsqueeze(2).broadcast_to([P, 4, d]), ALU.mult), q + b)
                    G.freed(dve, q + b)
                    ins = tt(y_, w, g, ALU.mult)
                return ins

            def mix1(part, l):
                rms(part, pr1[:, l, P_MIX:P_MIX + 8])
                dve.wait_ge(const_in, 48)
                dve.wait_ge(ev("w16_high"), l + 1)
                tt(w16[:, 1, :], pr1[:, l, P_W16:P_W16 + 128], w16[:, 0, :].bitcast(F32), ALU.subtract)\
                    .then_inc(ev("w16_low"), 1)
                dve.memset(cin[:, :, 0:3], 0.0)
                step(dve.memset(vaug[:, :, :, 64:65], 1.0))
                split.upto(Group(part, "tt0").u + 1)
                G = Group(part, "small")
                G.ready(dve, 0)
                o = G.bank(0)[:, 0:32].rearrange("p (b n) -> p b n", b=NB)
                tt(g16[:, :, 0:12], o[:, :, 0:12],
                   pr1[:, l, P_BIAS:P_BIAS + 12].unsqueeze(1).broadcast_to([P, NB, 12]), ALU.add)
                G.free(dve.tensor_copy(g16[:, :, 12:16], o[:, :, 12:16]), 0)
                G.freed(dve, 0)
                stt(lsg[:, 0], g16[:, :, 4:12], -1.0, g16[:, :, 4:12], ALU.mult, ALU.min).then_inc(ev("gate_abs"), 1)
                split.upto(Group(part, "tt0").u + 3)
                dve.wait_ge(ev("gate_ln"), l + 1)
                stt(cg[:, :, 0:4], g16[:, :, 4:8], 0.0, lsg[:, 2, :, 0:4], ALU.min, ALU.subtract)
                step(stt(cg[:, :, 4:8], g16[:, :, 8:12], 0.0, lsg[:, 2, :, 4:8], ALU.max, ALU.add))
                stt(cg[:, :, 4:8], cg[:, :, 4:8], -1.0, nea.unsqueeze(1).broadcast_to([P, NB, 4]), ALU.mult, ALU.mult)\
                    .then_inc(ev("cg_ready"), 1)
                for q in range(12):
                    split.upto(Group(part, "tt0").u + q + 6)
                    if q == 0:
                        G = Group(part, "cums")
                        G.ready(dve, 0)
                        dve.tensor_copy(cs, G.bank(0)[:, 0:16].rearrange("p (b n) -> p b n", b=NB))
                        G.free(dve.tensor_copy(gl, G.bank(0)[:, 16:24].rearrange("p (b n) -> p b n", b=NB)), 0)
                        G.freed(dve, 0)
                        tt(el, gl, cs[:, :, 4:8], ALU.subtract).then_inc(ev("gcols_ready"), 1)
                        tt(pk[:, :, 0:4], g16[:, :, 0:4], cs[:, :, 0:4], ALU.subtract)
                        dve.wait_ge(ev("beta_ready"), l + 1)
                        dve.tensor_copy(pk[:, :, 4:8], cs[:, :, 4:8]).then_inc(ev("pk_ready"), 1)
                    if q == 4:
                        G = Group(part, "rows")
                        G.ready(dve, 0)
                        G.free(dve.tensor_copy(rows12[0:12, :], G.bank(0)[0:12, 0:T]), 0)
                        G.freed(dve, 0)
                        dve.tensor_tensor_scan(mrow[0:4, :], rows12[0:4, :], rows12[0:4, :], 0.0, ALU.max, ALU.max)\
                           .then_inc(ev("mrow_ready"), 1)
                    if q == 8:
                        G = Group(part, "mcols")
                        G.ready(dve, 0)
                        G.free(tt(guard, cs[:, :, 0:4], G.bank(0)[:, 0:8].rearrange("p (b n) -> p b n", b=NB), ALU.add), 0)
                        G.freed(dve, 0)
                        dve.tensor_copy(guard, guard).then_inc(ev("mm_ready"), 1)
                    G = Group(part, f"tt{(q + 4) // 4}")
                    G.freed(dve, q % 4)
                    for tap in range(4):
                        w = pr1[:, l, P_CONV + 4 * q + tap:P_CONV + 4 * q + tap + 1]
                        src = cin[:, q, tap:tap + T]
                        if tap == 0:
                            step(ts(cT[:, q, :], src, w, None, ALU.mult))
                        elif tap < 3:
                            step(stt(cT[:, q, :], src, w, cT[:, q, :], ALU.mult, ALU.add))
                        else:
                            stt(cT[:, q, :], src, w, cT[:, q, :], ALU.mult, ALU.add).then_inc(ev("conv_done"), 1)
                split.upto(Group(part, "tok2").u + 1)
                dve.wait_ge(ev("conv_silu"), 3 * l + 3)
                G = Group(part, "gss")
                for q in range(4):
                    split.upto(Group(part, "tok2").u + 2 + 2 * q)
                    G.freed(dve, q)
                    step(dve.reciprocal(rn[:, q % 2, :], rn[:, q % 2, :]))
                    c2 = cT[:, 2 * q:2 * q + 2, :].rearrange("p a t -> p (a t)")
                    stt(c2, c2, 128.0 ** -0.5 if q < 2 else 1.0, rn[:, q % 2, :], ALU.mult, ALU.mult)\
                        .then_inc(ev("qkn_ready"), 1)
                    dve.wait_ge(ev("qkn_ready"), 4 * l + q + 1)
                split.upto(Group(part, "wout").u + 1)
                dve.wait_ge(ev("pk_ready"), l + 1)
                G = Group(part, "bM")
                for q in range(2):
                    G.ready(dve, q)
                    for i in range(2):
                        a = 2 * q + i
                        ts(ew[:, a, 0:256], G.bank(q)[:, T * i:T * i + T], pk[:, 0, a:a + 1], 0.0,
                           ALU.subtract, ALU.max)
                        ins = ts(ew[:, a, 256:384], G.bank(q)[:, T * i + 128:T * i + T], pk[:, 1, a:a + 1], 0.0,
                                 ALU.subtract, ALU.max)
                    G.free(ins, q)
                dve.wait_ge(ev("ew_ready"), 2 * l + 2)
                tri4 = tri.unsqueeze(1).broadcast_to([P, 4, P])
                tt(ew[:, :, 0:128], ew[:, :, 0:128], tri4, ALU.mult)
                step(tt(ew[:, :, 256:384], ew[:, :, 256:384], tri4, ALU.mult))
                G = Group(part, "msc")
                for i in range(4):
                    G.ready(dve, i)
                    G.free(tt(pm[:, i, :], G.bank(i)[:, 0:384], ew[:, i, :], ALU.mult), i)
                G = Group(part, "mout")
                dve.wait_ge(ev("guard_ready"), l + 1)
                for b in range(NB):
                    G.ready(dve, b)
                    o = G.bank(b)[:, 0:260].rearrange("p (h d) -> p h d", h=4)
                    den = o[:, :, 64:65].rearrange("p h d -> p (h d)")
                    step(tt(rden, den, guard[:, b, :], ALU.max))
                    step(stt(rden, den, -1.0, rden, ALU.mult, ALU.max))
                    step(dve.reciprocal(rden, rden))
                    G.free(tt(hh[:, 0:256].rearrange("p (h d) -> p h d", h=4), o[:, :, 0:64],
                              rden.unsqueeze(2).broadcast_to([P, 4, 64]), ALU.mult), b)
                    G.freed(dve, b)
                    step(head_norm(hh[:, 0:256], tok[:, b, 0:256], y[:, b, 0:256], sq, ssq[:, 0, :]))
                G = Group(part, "rsc")
                for i in range(4):
                    G.ready(dve, i)
                    dc = C_RET + 256 * i
                    tt(rp[:, i, 0:256], G.bank(i)[:, 0:256], cst1[:, dc:dc + 256], ALU.mult)
                    G.free(tt(rp[:, i, 256:384], G.bank(i)[:, 256:384], cst1[:, dc:dc + 128], ALU.mult), i)
                G = Group(part, "rout")
                step(head_norms(G, 0, 64, EPS1, lambda b: y[:, b, 256:512], lambda b: tok[:, b, 1024:1280],
                                (hh, sq), ssq))
                G = Group(part, "bg")
                for q in range(2):
                    G.ready(dve, q)
                    dve.wait_ge(ev("egb_ready"), 4 * l + 2 * q + 2)
                    for i in range(2):
                        for b in range(NB):
                            a = 2 * q + i
                            ins = ts(dec[:, a, b, :], G.bank(q)[:, T * i + 128 * b:T * i + 128 * b + 128],
                                     pk[:, b, 4 + a:5 + a], 0.0, ALU.subtract, ALU.min)
                    G.free(ins, q)
                dve.wait_ge(ev("dec_exp"), 2 * l + 2)
                d8 = dec.rearrange("p h b t -> p (h b) t")
                step(tt(d8, d8, tri.unsqueeze(1).broadcast_to([P, 8, P]), ALU.mult))
                G = Group(part, "bb")
                for q in range(2):
                    G.ready(dve, q)
                    G.free(tt(NT[:, 2 * q:2 * q + 2].rearrange("p h b t -> p (h b t)"),
                              dec[:, 2 * q:2 * q + 2].rearrange("p h b t -> p (h b t)"), G.bank(q)[:, :], ALU.mult), q)
                    G.freed(dve, q)
                G = Group(part, "gkk")
                for i in range(4):
                    G.ready(dve, i)
                    n2 = NT[:, i].rearrange("p b t -> p (b t)")
                    ins = tt(n2, n2, G.bank(i)[:, 0:256], ALU.mult)
                ins.then_inc(ev("NT_ready"), 1)
                for i in range(4):
                    G.free(tt(QK[:, i].rearrange("p b t -> p (b t)"), dec[:, i].rearrange("p b t -> p (b t)"),
                              G.bank(i)[:, 256:512], ALU.mult), i)
                G = Group(part, "inv")
                dve.wait_ge(ev("EL_ready"), LEVELS * l + 1)
                tt(WI, ident.unsqueeze(1).broadcast_to([P, 8, P]), EL, ALU.subtract).then_inc(ev("W_ready"), 1)
                for half in range(2):
                    G.ready(dve, half)
                    G.free(tt(TI[:, 4 * half:4 * half + 4, :], ident.unsqueeze(1).broadcast_to([P, 4, P]),
                              G.bank(half)[:, :].rearrange("p (a t) -> p a t", a=4), ALU.subtract), half)
                for n in range(1, LEVELS):
                    for q, buf in ((1, TI), (2, WI)):
                        if n == LEVELS - 1 and q == 1:
                            continue
                        for half in range(2):
                            job = inverse_job(n, q, half)
                            G.ready(dve, job)
                            if n > 1:
                                G.freed(dve, inverse_job(n - 1, q, half))
                            elif q == 1:
                                G.freed(dve, half)
                            b2 = buf[:, 4 * half:4 * half + 4, :].rearrange("p a t -> p (a t)")
                            G.free(tt(b2, b2, G.bank(job)[:, :], ALU.subtract), job)
                G = Group(part, "gout")
                G.ready(dve, 1)
                G.free(dve.tensor_copy(uv1.rearrange("p h t -> p (h t)"), G.bank(1)[:, :]), 1)
                G.freed(dve, 1)
                G.ready(dve, 4)
                G.free(tt(u1.rearrange("p h t -> p (h t)"), uv1.rearrange("p h t -> p (h t)"), G.bank(4)[:, :], ALU.add), 4)
                ins = head_norms(G, 5, 128, EPS1, lambda b: y[:, b, 512:1024], lambda b: tok[:, b, 1280:1792],
                                 (hh, sq), ssq)
                ins.then_inc(ev("y_ready"), 1)
                xsp_lows(part, "yT", pr1[:, l, P_Y:P_Y + 8])
                split.upto(Group(part, "wout").u + DC + 1)
                add_to_h(part, (Group(part, "wout"), DC - 1), 1.0, 1.0)

            def layer_norm(n):
                dve.wait_ge(rows_in, 32 * (n + 1))
                for b in range(NB):
                    for m in range(2):
                        ins = dve.bn_stats(st[:, 12 * b + 6 * m:12 * b + 6 * m + 6], h[:, b, 512 * m:512 * m + 512])
                step(ins)
                for b in range(NB):
                    ins = dve.bn_aggr(moments[:, b, :], st[:, 12 * b:12 * b + 12].rearrange("p (m s) -> p m s", m=2))
                step(ins)
                ts(moments[:, :, 1:2], moments[:, :, 1:2], EPS2, None, ALU.add).then_inc(ev("square_ready"), 1)
                for b in range(NB):
                    hb = h[:, b, :]
                    ins = stt(hb, hb, moments[:, b, 0:1], rows[:, 0:1024], ALU.subtract, ALU.mult)
                step(ins)
                asked[0] += 1
                dve.wait_ge(ev("rsqrt_ready"), asked[0])
                for b in range(NB):
                    hb = h[:, b, :]
                    ins = stt(hb, hb, moments[:, b, 1:2], rows[:, 1024:2048], ALU.mult, ALU.add)
                step(ins)
                dve.memset(st[:, 31:32], 0.0).then_inc(rows_free, 1)
                dve.memset(st[:, 30:31], 0.0).then_inc(ev("ln_ready" if n < 3 * DEPTH else "out_ready"), 1)

            def mix2(part, l):
                xsp_lows(part, "xT", None)
                dve.wait_ge(ev("wa_high"), l + 1)
                tt(w16[:, 1, :], wa_sb.rearrange("p c n -> p (c n)"), w16[:, 0, :].bitcast(F32), ALU.subtract)\
                    .then_inc(ev("wa_low"), 1)
                K = [Group(part, f"tok{g}") for g in range(4)]
                split.upto(K[0].u + 1)
                G = Group(part, "logg")
                G.ready(dve, 0)
                for m in range(2):
                    ins = ts(zg[:, m, :], G.bank(0)[:, T * m:T * m + T], pr2[:, l, Q_BG + m:Q_BG + m + 1], None, ALU.add)
                G.free(ins, 0)
                G.freed(dve, 0)
                stt(dff, zg, -1.0, zg, ALU.mult, ALU.min).then_inc(ev("zabs_ready"), 1)
                step(ts(zg, zg, 0.0, None, ALU.min))
                split.upto(K[0].u + 2)
                dve.wait_ge(ev("lg_ln"), l + 1)
                for m in range(2):
                    ins = dve.tensor_tensor_scan(bc[:, m, :], zg[:, m, :], lg[:, m, :], 0.0, ALU.add, ALU.subtract)
                ins.then_inc(ev("bc_ready"), 1)
                tt4 = Group(part, "tt")
                for q in range(4):
                    tt4.freed(dve, q)
                def level(m):
                    buf = lv_buf(m if m < LEVELS else LEVELS + 1)
                    dve.wait_ge(ev("lv_exp"), (LEVELS + 1) * l + m + 1)
                    tt(lv_q[:, buf], qkT[:, 0:2, :], lv_e, ALU.mult)
                    tt(lv_k[:, buf], qkT[:, 2:4, :], lv_e, ALU.mult).then_inc(ev("lv_ready"), 1)

                def gather(n):
                    G = Group(part, f"lvl{n}")
                    for odd in range(2):
                        G.ready(dve, odd)
                        o = G.bank(odd)[:, :].rearrange("p (h t) -> p h t", h=4)
                        if n == LEVELS:
                            G.free(tt(at_[:, odd], o, ident.unsqueeze(1).broadcast_to([P, 4, P]), ALU.mult), odd)
                            G.freed(dve, odd)
                        else:
                            mask = lvl(n).unsqueeze(1).broadcast_to([P, 4, P]).bitcast(U32)
                            G.free(dve.copy_predicated(at_[:, odd], mask, o), odd)
                            G.freed(dve, odd)

                level(0)
                split.upto(K[0].u + 3)
                level(1)
                split.upto(K[1].u + 2)
                gather(LEVELS)
                gather(0)
                level(2)
                split.upto(K[2].u + 2)
                for n in (1, 3):
                    gather(n)
                    gather(n + 1)
                    level(n + 2)
                    split.upto(K[2].u + 2 * n + 1)
                    level(n + 3)
                    split.upto(K[2].u + (6 if n == 1 else 9))
                gather(5)
                level(7)
                gather(6)
                dve.tensor_copy(st[:, 29:30], ident[:, 0:1]).then_inc(ev("at_ready"), 1)
                G = Group(part, "lvl8")
                for odd in range(2):
                    G.ready(dve, odd)
                    G.free(dve.tensor_copy(off[:, 2 * odd:2 * odd + 2, :].rearrange("p h t -> p (h t)"),
                                           G.bank(odd)[:, 0:256]), odd)
                for g in range(1, 4):
                    K[g].freed(dve, 0)
                    K[g].freed(dve, 1)
                dve.wait_ge(rows_in, 32 * (3 * l + 2))
                v2 = [tok2[:, b, 1536:2048] for b in range(NB)]
                for b in range(NB):
                    ins = dve.bn_stats(bst[:, b, :], v2[b])
                step(ins)
                for b in range(NB):
                    ins = dve.bn_aggr(bag[:, b, :], bst[:, b, :])
                step(ins)
                ts(bag[:, :, 1:2], bag[:, :, 1:2], EPS2, None, ALU.add).then_inc(ev("square_ready"), 1)
                for b in range(NB):
                    ins = stt(v2[b], v2[b], bag[:, b, 0:1], rows[:, 0:512], ALU.subtract, ALU.mult)
                step(ins)
                asked[0] += 1
                dve.wait_ge(ev("rsqrt_ready"), asked[0])
                for b in range(NB):
                    ins = stt(v2[b], v2[b], bag[:, b, 1:2], rows[:, 1024:1536], ALU.mult, ALU.add)
                step(ins)
                dve.memset(st[:, 31:32], 0.0).then_inc(rows_free, 1)
                dve.wait_ge(side_in, 16 + 64 * (l + 1))
                dve.memset(swt_sb[64:128, :, 0:64], 0.0).then_inc(ev("sgv_ready"), 1)
                G = Group(part, "gla")
                step(head_norms(G, 0, 128, EPS2, lambda b: y[:, b, 0:512], lambda b: tok2[:, b, 512:1024],
                                (hh2, sq2), ssq2))
                G = Group(part, "sgu")
                for b in range(NB):
                    G.ready(dve, b)
                    for i in range(4):
                        c = slice(128 * i, 128 * i + 128)
                        ins = stt(y[:, b, 512 + 128 * i:640 + 128 * i], G.bank(b)[:, c], pr2[:, l, Q_SB + i:Q_SB + i + 1],
                                  tok2[:, b, 1024 + 128 * i:1152 + 128 * i], ALU.add, ALU.mult)
                    G.free(ins, b)
                    G.freed(dve, b)
                dve.memset(st[:, 30:31], 0.0).then_inc(ev("y_ready"), 1)
                xsp_lows(part, "yT", yg[:, l, :])
                split.upto(Group(part, "wout").u + DC + 1)
                add_to_h(part, (Group(part, "wout"), DC - 1), 1.0, ALPHA)
                layer_norm(3 * l + 2)

            def top16(vals, idx, src, tmp):
                step(dve.max(vals[:, 0:8], src))
                step(dve.max_index(idx[:, 0:8], vals[:, 0:8], src))
                step(dve.match_replace(tmp, vals[:, 0:8], src, LOWEST))
                split.upto(split.next)
                step(dve.max(vals[:, 8:16], tmp))
                step(dve.max_index(idx[:, 8:16], vals[:, 8:16], tmp))
                split.upto(split.next)

            def peer(part, l):
                xsp_lows(part, "xT", None)
                U = Group(part, "U")
                split.upto(U.u + 2)
                for q in range(4):
                    Group(part, "score").freed(dve, q)
                for b in range(NB):
                    for i in range(PH):
                        for m in range(2):
                            c = 128 * m
                            src = ACC[i // 2][:, 256 * (i % 2) + c:256 * (i % 2) + c + 128] if b == 0 \
                                else sc1[:, 256 * i + c:256 * i + c + 128]
                            top16(topv[:, 2 * i + m, :], topi[:, 2 * i + m, :], src, cand[:, 0:128])
                        c3 = cand.rearrange("p (a c) -> p a c", a=TOPK)
                        step(tt(c3, topv[:, 2 * i, :].unsqueeze(2).broadcast_to([P, TOPK, TOPK]),
                                topv[:, 2 * i + 1, :].unsqueeze(1).broadcast_to([P, TOPK, TOPK]), ALU.add))
                        top16(selv[:, b, 2, 16 * i:16 * i + 16], posi[:, i, :], cand, cand2)
                    if b == 0:
                        dve.memset(st[:, 31:32], 0.0).then_inc(acc_free, 1)
                    else:
                        dve.memset(st[:, 31:32], 0.0).then_inc(ev("scores_read"), 1)
                    step(dve.tensor_copy(topf, topi))
                    step(ts(posa, posi, 4, None, ALU.logical_shift_right))
                    step(ts(posi, posi, 15, None, ALU.bitwise_and))
                    step(dve.tensor_copy(pfa, posa))
                    step(dve.tensor_copy(pfb, posi))
                    io16 = iota[:, 0:TOPK].unsqueeze(1).broadcast_to([P, TOPK, TOPK])
                    c3 = cand.rearrange("p (a c) -> p a c", a=TOPK)
                    for i in range(PH):
                        for m, place in ((0, pfa), (1, pfb)):
                            step(tt(c3, place[:, i, :].unsqueeze(2).broadcast_to([P, TOPK, TOPK]), io16, ALU.is_equal))
                            step(tt(c3, c3, topf[:, 2 * i + m, :].unsqueeze(1).broadcast_to([P, TOPK, TOPK]), ALU.mult))
                            step(dve.tensor_reduce(selv[:, b, m, 16 * i:16 * i + 16], c3, AX_X, ALU.add))
                            split.upto(split.next)
                    g3 = selv[:, b, 2, :].rearrange("p (h k) -> p h k", h=PH)
                    step(dve.tensor_copy(gmx[:, 0:PH], g3[:, :, 0:1].rearrange("p h k -> p (h k)")))
                    tt(g3, g3, gmx[:, 0:PH].unsqueeze(2).broadcast_to([P, PH, TOPK]), ALU.subtract)\
                        .then_inc(ev("smx_ready"), 1)
                    dve.wait_ge(ev("smx_ready"), NB * l + b + 1)
                split.upto(U.u + NKEYS - 1)
                for b in range(NB):
                    g3 = selv[:, b, 2, :].rearrange("p (h k) -> p h k", h=PH)
                    dve.wait_ge(ev("smx_exp"), NB * l + b + 1)
                    step(dve.tensor_reduce(gmx[:, 0:PH], g3, AX_X, ALU.add))
                    step(dve.reciprocal(gmx[:, 0:PH], gmx[:, 0:PH]))
                    tt(g3, g3, gmx[:, 0:PH].unsqueeze(2).broadcast_to([P, PH, TOPK]), ALU.mult)\
                        .then_inc(ev("sel_ready"), 1)
                    dve.wait_ge(ev("sel_ready"), NB * l + b + 1)
                S = Group(part, "selT")
                for b in range(NB):
                    S.ready(dve, b)
                    S.free(dve.tensor_copy(selT[:, :, 128 * b:128 * b + 128],
                                           S.bank(b)[:, 0:384].rearrange("p (s t) -> p s t", s=3)), b)
                    S.freed(dve, b)
                G = Group(part, "G")
                for q in range(NKEYS - 4, NKEYS):
                    U.freed(dve, q)

                def one_hot(g, it=0):
                    dve.wait_ge(job_done, it * 4 + (G.j + g - 3))
                    if g % 4 == 0:
                        tt(oh[:, 0, 0], iota.unsqueeze(1).broadcast_to([P, 4, NKEYS]),
                           selT[:, 0, bass.ds(it * 16 + 4 * g, 4)].unsqueeze(2).broadcast_to([P, 4, NKEYS]),
                           ALU.is_equal)
                    tt(oh[:, g % 4, 1], iota.unsqueeze(1).broadcast_to([P, 4, NKEYS]),
                       selT[:, 1, bass.ds(it * 16 + 4 * g, 4)].unsqueeze(2).broadcast_to([P, 4, NKEYS]),
                       ALU.is_equal).then_inc(oh_equal, 1)

                def gate(g, it=0):
                    dve.wait_ge(job_done, it * 4 + (G.j + g + 1))
                    a3 = A[:, :, bass.ds(it * 16 + 4 * g, 4)]
                    G.free(tt(a3, a3, G.bank(g)[:, :].rearrange("p (t j) -> p j t", t=4), ALU.mult), g)

                one_hot(0)
                one_hot(1)
                with dve.Fori(0, 15) as it:
                    for g in range(4):
                        one_hot(g + 2, it)
                        gate(g, it)
                for g in range(60, 64):
                    if g < 62:
                        one_hot(g + 2)
                    gate(g)
                for q in range(4):
                    G.freed(dve, 60 + q)
                dve.memset(st[:, 31:32], 0.0).then_inc(g_freed, 1)
                V = Group(part, "V")

                def low(j, it=0):
                    dve.wait_ge(act_high, it * 6 + (TILES + NKEYS * l + j + 1))
                    tt(hsp[:, j % 2, 1, :], arena[:, bass.ds(it * (6 * T) + j * T, T)],
                       hsp[:, j % 2, 0, :].bitcast(F32), ALU.subtract).then_inc(act_low, 1)

                split.one(V.u)
                low(0)
                low(1)
                split.one(V.u + 1)
                split.one(V.u + 2)
                with dve.Fori(0, 20) as it:
                    for j in range(2, 8):
                        low(j, it)
                        split.one(V.u + j + 1, it)
                split.next = V.u + 123
                for j in range(122, 128):
                    low(j)
                    split.upto(V.u + j + 1)
                split.upto(V.u + 129)
                dve.wait_ge(h_back, 16 * (l + 1))
                add_to_h(part, (V, NKEYS - 1), 1.0, ALPHA)
                dve.memset(st[:, 31:32], 0.0).then_inc(side_free, 1)
                layer_norm(3 * l + 3)

            yg = pr2[:, :, Q_GAIN:Q_GAIN + 8]
            dve.wait_ge(first_in, 32)
            dve.wait_ge(x_in, 32)
            for l in range(DEPTH):
                ffn(f"ffn1{l}", l, P_FFN1, 2 * l * FT)
                mix1(f"mix1{l}", l)
                ffn(f"ffn2{l}", l, P_FFN2, (2 * l + 1) * FT)
            rms_scale()
            dve.wait_ge(side_in, 16)
            for b in range(NB):
                ins = stt(h[:, b, :], h[:, b, :], st[:, 2 + b:3 + b], final_row, ALU.mult, ALU.mult)
            step(ins)
            dve.memset(st[:, 31:32], 0.0).then_inc(side_free, 1)
            layer_norm(0)
            for l in range(DEPTH):
                mix2(f"mix2{l}", l)
                peer(f"peer{l}", l)


def tables():
    c = np.zeros((P, C_N), np.float32)
    i = np.arange(P)
    c[:, C_ID:C_ID + 128] = np.eye(P)
    c[:, C_TRI:C_TRI + 128] = i[:, None] <= i[None, :]
    c[:, C_ONE:C_ONE + 128] = 1.0
    masks = np.zeros((LEVELS, P, P), np.float32)
    for n in range(LEVELS):
        s = 1 << n
        m = (i[:, None] // (2 * s) == i[None, :] // (2 * s)) & (i[:, None] % (2 * s) < s) & (i[None, :] % (2 * s) >= s)
        masks[n] = m
    c1 = np.zeros((P, C_N1), np.float32)
    for a in range(4):
        lg = np.log1p(-np.exp2(-5.0 - a))
        for b in range(2):
            rel = i[None, :] + 128.0 * b - i[:, None]
            c1[:, C_RET + 256 * a + 128 * b:C_RET + 256 * a + 128 * b + 128] = \
                np.where(rel >= 0, np.exp(np.maximum(rel, 0) * lg), 0.0) * 0.125
    inv = (np.float32(10000.0) ** (-np.arange(0, 64, 2, dtype=np.float32) / np.float32(64))).astype(np.float32)
    for b in range(NB):
        ang = ((i + 128 * b).astype(np.float32)[:, None] * inv[None, :]).astype(np.float32).astype(np.float64)
        c1[:, C_COS + 32 * b:C_COS + 32 * b + 32] = np.cos(ang)
        c1[:, C_SIN + 32 * b:C_SIN + 32 * b + 32] = np.sin(ang)
    c[:, C_IOTA:C_IOTA + 128] = i[None, :]
    return c, c1, masks


def columns(w):
    n = w.shape[1] // 128
    return w.reshape(DC, P, n, 128).transpose(2, 1, 0, 3).reshape(n, P, 1024)


def wide_columns(w):
    n = w.shape[1] // 512
    return w.reshape(4, 2, P, n, 512).transpose(3, 0, 2, 1, 4).reshape(4 * n, P, 1024)


def lay_out(v):
    units = np.empty((UNITS, P, 1024), np.float32)
    first = {n: u for n, (_, _, u) in BASE.items()}

    def put(part, name, a, i=0, step=1):
        u = first[part, name] + i
        units[u:u + step * (len(a) - 1) + 1:step] = a

    def ffn(part, gate, up, down):
        g, u, d = columns(gate), columns(up), down.reshape(FT, P, 1024)
        put(part, "ffn", g[:1], 0)
        put(part, "ffn", u[:1], 1)
        put(part, "ffn", g[1:], 2, 3)
        put(part, "ffn", u[1:], 3, 3)
        put(part, "ffn", d[:-1], 4, 3)
        put(part, "ffn", d[-1:], 3 * FT - 1)

    off = np.cumsum([0, 256, 256, 256, 256, 4, 4, 256, 256, 256, 256, 512, 512, 512, 512, 4, 4])
    off2 = np.cumsum([0, 256, 256, 512, 512, 16, 512, 512])
    p1 = np.zeros((DEPTH, P, P_N), np.float32)
    p2 = np.zeros((DEPTH, P, Q_N), np.float32)
    wa = np.zeros((DEPTH, P, DC, 16), np.float32)
    for l in range(DEPTH):
        ffn(f"ffn1{l}", v["ffn1_w_gate"][l], v["ffn1_w_up"][l], v["ffn1_w_down"][l])
        ffn(f"ffn2{l}", v["ffn2_w_gate"][l], v["ffn2_w_up"][l], v["ffn2_w_down"][l])
        w = v["w_in"][l]
        s = [w[:, off[n]:off[n + 1]] for n in range(16)]
        put(f"mix1{l}", "tt0", columns(np.concatenate([s[0], s[1], s[10], s[11], s[12]], 1)))
        put(f"mix1{l}", "tok0", wide_columns(np.concatenate([s[2], s[3], s[6], s[7], s[8], s[9], s[13]], 1)))
        put(f"mix1{l}", "wout", v["w_out"][l].reshape(DC, P, D))
        for at, name in ((P_FFN1, "ffn1_norm"), (P_MIX, "mix_norm"), (P_FFN2, "ffn2_norm")):
            p1[l, :, at:at + 8] = v[name][l].reshape(DC, P).T
        gains = np.concatenate([v["m_out_norm"][l], v["r_out_norm"][l], v["g_out_norm"][l]])
        p1[l, :, P_Y:P_Y + 8] = gains.reshape(DC, P).T
        p1[l, :, P_CONV:P_CONV + 48] = v["g_conv"][l].reshape(4, 12, P).transpose(2, 1, 0).reshape(P, 48)
        p1[l, :, P_BIAS:P_BIAS + 12] = np.concatenate([v["m_i_bias"][l], v["m_f_bias"][l], v["g_dt_bias"][l]])
        p1[l, :, P_ALOG:P_ALOG + 4] = v["g_a_log"][l]
        gates = np.concatenate([s[4], s[5], s[14], s[15]], 1)
        p1[l, :, P_W16:P_W16 + 128] = gates.reshape(DC, P, 16).transpose(1, 0, 2).reshape(P, 128)

        w = v["w_in_2"][l]
        s = [w[:, off2[n]:off2[n + 1]] for n in range(7)]
        put(f"mix2{l}", "tt", columns(np.concatenate([s[0], s[1]], 1)))
        for g, cols in enumerate((s[2], s[3], s[5], s[6])):
            put(f"mix2{l}", f"tok{g}", wide_columns(cols))
        put(f"mix2{l}", "wout", v["w_out_2"][l].reshape(DC, P, D))
        wa[l] = s[4].reshape(DC, P, 16).transpose(1, 0, 2)
        put(f"peer{l}", "tt", columns(v["peer_wq_2"][l]))
        u = v["peer_u_2"][l].reshape(NKEYS, NKEYS, DC, P)
        put(f"peer{l}", "U", u.transpose(1, 3, 2, 0).reshape(NKEYS, P, 1024))
        put(f"peer{l}", "V", v["peer_v_2"][l].reshape(NKEYS, NKEYS, D).transpose(1, 0, 2))
        p2[l, :, Q_GAIN:Q_GAIN + 4] = v["gla_norm_g_2"][l][:, None]
        p2[l, :, Q_GAIN + 4:Q_GAIN + 8] = 1.0
        p2[l, :, Q_BG:Q_BG + 2] = v["b_gate_2"][l].reshape(2, P).T
        p2[l, :, Q_SB:Q_SB + 4] = v["sgu_b_2"][l].T
        p2[l, :, Q_K1:Q_K1 + 128] = v["peer_k1_2"][l].T
        p2[l, :, Q_K1 + 128:Q_K1 + 256] = v["peer_k2_2"][l].T
    swt = np.ascontiguousarray(v["sgu_w_2"].transpose(0, 3, 1, 2))
    rows2 = np.stack([np.stack([v["ln_in_g_2"], v["ln_in_b_2"]])] +
                     [np.stack([v[f"ln{n}_g_2"][l], v[f"ln{n}_b_2"][l]]) for l in range(DEPTH) for n in (1, 2)])
    rows3 = np.stack([v["sgu_ln_g_2"], v["sgu_ln_b_2"]], 1)
    consts, consts1, levels = tables()
    return {
        "x": np.ascontiguousarray(v["x"][0]), "stream": units, "consts": consts, "consts1": consts1, "levels": levels, "p1": p1, "p2": p2,
        "swt": swt, "wa": wa, "wgu": np.ascontiguousarray(v["w_gate_up_2"]),
        "rows1": np.ascontiguousarray(v["final_norm"]), "rows2": rows2, "rows3": rows3,
    }


def kernel(**inputs):
    import concourse.bacc as bacc
    from concourse.bass_utils import run_bass_kernel_spmd

    arrays = lay_out({k: np.asarray(a) for k, a in inputs.items()})
    nc = bacc.Bacc("TRN2", target_bir_lowering=False, num_devices=1)
    args = [nc.dram_tensor(f"in_{n}", a.shape, F32, kind="ExternalInput").ap() for n, a in arrays.items()]
    out = nc.dram_tensor("out", (T, D), F32, kind="ExternalOutput").ap()
    build_program(nc, *args, out)
    r = run_bass_kernel_spmd(nc, [{f"in_{n}": a for n, a in arrays.items()}], core_ids=[0])
    return r.results[0]["out"].reshape(1, T, D)
```
